# Optimizing a Trainium2 kernel written in Bass

```python
import math
import jax, jax.numpy as jnp
from jax import lax
import numpy as np

D_MODEL = 1024
BATCH = 1
SEQ = 1024
DEPTH = 1

POOL_WIDTH = D_MODEL
POOL_GROUPS = 4
POOL_GROUP_WIDTH = POOL_WIDTH // POOL_GROUPS
POOL_WINDOWS = (2, 4, 8, 16)
SSD_INNER = 2 * D_MODEL
SSD_HEAD_DIM = 64
SSD_HEADS = SSD_INNER // SSD_HEAD_DIM
SSD_GROUPS = 4
SSD_STATE = 128
SSD_CONV = 4
SSD_CHUNK = 128
SSD_CONV_DIM = SSD_INNER + 2 * SSD_GROUPS * SSD_STATE
N_BRANCH = 2
IN_COLS = POOL_WIDTH + SSD_INNER + SSD_CONV_DIM + SSD_HEADS + N_BRANCH * D_MODEL
MOE_GROUPS = 4
EXPERTS_PER_GROUP = 8
N_EXPERTS = MOE_GROUPS * EXPERTS_PER_GROUP
MOE_TOPK = 2
EXPERT_FF = 512
MOE_BLOCK = 256
EPS = 1e-6

kernel_name = 'hybrid_pool_ssd_hiermoe_adaln'

def rmsnorm(x, g):
    x32 = x.astype(jnp.float32)
    y = x32 * lax.rsqrt(jnp.mean(x32 * x32, axis=-1, keepdims=True) + EPS)
    return (y * g.astype(jnp.float32)).astype(x.dtype)

def multiscale_pool(xp, pool_w, pool_scale):
    b, s, _ = xp.shape
    xg = xp.reshape(b, s, POOL_GROUPS, POOL_GROUP_WIDTH).astype(jnp.float32)
    cs = jnp.cumsum(xg, axis=1)
    pos = jnp.arange(s)
    outs = []
    for gi, w in enumerate(POOL_WINDOWS):
        csg = cs[:, :, gi]
        lagged = jnp.pad(csg, ((0, 0), (w, 0), (0, 0)))[:, :s]
        cnt = jnp.minimum(pos + 1, w).astype(jnp.float32)[None, :, None]
        outs.append((csg - lagged) / cnt - xg[:, :, gi])
    d = jnp.stack(outs, axis=2).astype(xp.dtype)
    y = jnp.einsum('bsgc,gcd->bsgd', d, pool_w)
    return y.reshape(b, s, POOL_WIDTH) * pool_scale

def causal_dwconv(x, w, bias):
    out = lax.conv_general_dilated(x, w[:, None, :].astype(x.dtype), window_strides=(1,),
                                   padding=[(SSD_CONV - 1, 0)],
                                   dimension_numbers=('NWC', 'WIO', 'NWC'),
                                   feature_group_count=x.shape[-1])
    return out + bias

def ssd_chunked(X, Adt, Bm, Cm):
    b, s, h, p = X.shape
    g, n = Bm.shape[2], Bm.shape[3]
    r = h // g
    nc = s // SSD_CHUNK
    Q = SSD_CHUNK
    X = X.reshape(b, nc, Q, g, r, p)
    A = Adt.reshape(b, nc, Q, g, r).transpose(0, 3, 4, 1, 2)
    Bc = Bm.reshape(b, nc, Q, g, n)
    Cc = Cm.reshape(b, nc, Q, g, n)
    A_cs = jnp.cumsum(A, axis=-1)
    seg = A_cs[..., :, None] - A_cs[..., None, :]
    mask = jnp.tril(jnp.ones((Q, Q), dtype=bool))
    L = jnp.exp(jnp.where(mask, seg, -jnp.inf))
    CB = jnp.einsum('bclgn,bcsgn->bgcls', Cc, Bc)
    Y_diag = jnp.einsum('bgrcls,bcsgrp->bclgrp', L * CB[:, :, None], X)
    decay_states = jnp.exp(A_cs[..., -1:] - A_cs)
    states = jnp.einsum('bclgn,bgrcl,bclgrp->bcgrpn', Bc, decay_states, X)
    chunk_decay = jnp.exp(A_cs[..., -1])

    def step(carry, inp):
        st, dec = inp
        return carry * dec[..., None, None] + st, carry

    states_c = states.transpose(1, 0, 2, 3, 4, 5)
    dec_c = chunk_decay.transpose(3, 0, 1, 2)
    _, prev = lax.scan(step, jnp.zeros(states_c.shape[1:], states_c.dtype), (states_c, dec_c))
    prev = prev.transpose(1, 0, 2, 3, 4, 5)
    Y_off = jnp.einsum('bclgn,bcgrpn,bgrcl->bclgrp', Cc, prev, jnp.exp(A_cs))
    return (Y_diag + Y_off).reshape(b, s, h, p)

def ssd_branch(z, xbc, dt_raw, conv_w, conv_b, dt_bias, a_log, d_skip, ssd_norm_g):
    b, s, _ = xbc.shape
    xbc = jax.nn.silu(causal_dwconv(xbc, conv_w, conv_b))
    xs, Bm, Cm = jnp.split(xbc, [SSD_INNER, SSD_INNER + SSD_GROUPS * SSD_STATE], axis=-1)
    xs = xs.reshape(b, s, SSD_HEADS, SSD_HEAD_DIM).astype(jnp.float32)
    Bm = Bm.reshape(b, s, SSD_GROUPS, SSD_STATE).astype(jnp.float32)
    Cm = Cm.reshape(b, s, SSD_GROUPS, SSD_STATE).astype(jnp.float32)
    dt = jax.nn.softplus(dt_raw.astype(jnp.float32) + dt_bias.astype(jnp.float32))
    A = -jnp.exp(a_log.astype(jnp.float32))
    y = ssd_chunked(xs * dt[..., None], dt * A, Bm, Cm) + d_skip.astype(jnp.float32)[:, None] * xs
    y = y.reshape(b, s, SSD_INNER) * jax.nn.silu(z.astype(jnp.float32))
    return rmsnorm(y, ssd_norm_g).astype(z.dtype)

def mixer(h, w_in, pool_w, pool_scale, conv_w, conv_b, dt_bias, a_log, d_skip, ssd_norm_g,
          w_branch_pool, w_branch_ssd, w_out):
    proj = h @ w_in
    i0 = POOL_WIDTH
    i1 = i0 + SSD_INNER
    i2 = i1 + SSD_CONV_DIM
    i3 = i2 + SSD_HEADS
    xp, z, xbc, dt_raw, gates = jnp.split(proj, [i0, i1, i2, i3], axis=-1)
    y_pool = multiscale_pool(xp, pool_w, pool_scale)
    y_ssd = ssd_branch(z, xbc, dt_raw, conv_w, conv_b, dt_bias, a_log, d_skip, ssd_norm_g)
    g_pool, g_ssd = jnp.split(jax.nn.sigmoid(gates), 2, axis=-1)
    u = g_pool * (y_pool @ w_branch_pool) + g_ssd * (y_ssd @ w_branch_ssd)
    return u @ w_out

def hier_moe(h, wg, bg, we, be, w13, w2):
    b, s, d = h.shape
    T = b * s
    ht = h.reshape(T, d)
    p_group = jax.nn.softmax((ht @ wg + bg).astype(jnp.float32), axis=-1)
    gw, gsel = lax.top_k(p_group, 1)
    e_logits = (ht @ we + be).astype(jnp.float32).reshape(T, MOE_GROUPS, EXPERTS_PER_GROUP)
    e_in = jnp.take_along_axis(e_logits, gsel[:, :, None], axis=1)[:, 0]
    ew, ei = lax.top_k(jax.nn.softmax(e_in, axis=-1), MOE_TOPK)
    ew = ew / jnp.sum(ew, axis=-1, keepdims=True)
    weights = (gw * ew).reshape(-1)
    experts = (gsel * EXPERTS_PER_GROUP + ei).reshape(-1).astype(jnp.int32)
    A = T * MOE_TOPK
    P = A + N_EXPERTS * MOE_BLOCK
    n_blocks = P // MOE_BLOCK
    order = jnp.argsort(experts)
    e_sorted = experts[order]
    tok_sorted = (order // MOE_TOPK).astype(jnp.int32)
    w_sorted = weights[order]
    counts = jnp.bincount(experts, length=N_EXPERTS).astype(jnp.int32)
    starts = jnp.cumsum(counts) - counts
    padded = ((counts + MOE_BLOCK - 1) // MOE_BLOCK) * MOE_BLOCK
    pad_ends = jnp.cumsum(padded)
    pad_starts = pad_ends - padded
    dest = pad_starts[e_sorted] + jnp.arange(A, dtype=jnp.int32) - starts[e_sorted]
    x_buf = jnp.zeros((P, d), h.dtype).at[dest].set(ht[tok_sorted])
    w_buf = jnp.zeros((P,), jnp.float32).at[dest].set(w_sorted)
    t_buf = jnp.zeros((P,), jnp.int32).at[dest].set(tok_sorted)
    block_expert = jnp.minimum(
        jnp.searchsorted(pad_ends, jnp.arange(n_blocks, dtype=jnp.int32) * MOE_BLOCK, side='right'),
        N_EXPERTS - 1)

    def expert_block(args):
        xb, e = args
        a, g = jnp.split(xb @ w13[e], 2, axis=-1)
        return (jax.nn.silu(a) * g) @ w2[e]

    y = lax.map(expert_block, (x_buf.reshape(n_blocks, MOE_BLOCK, d), block_expert)).reshape(P, d)
    out = jnp.zeros((T, d), y.dtype).at[t_buf].add(y * w_buf[:, None].astype(y.dtype))
    return out.reshape(b, s, d)

def setup_inputs(seed: int = 0) -> dict:
    key = jax.random.key(seed)
    ks = jax.random.split(key, 32)
    D = D_MODEL
    L = DEPTH
    f32 = jnp.float32
    nrm = lambda k, shape, fan: jax.random.normal(k, shape, f32) * (fan ** -0.5)
    dt0 = jnp.exp(jax.random.uniform(ks[10], (L, SSD_HEADS), f32, math.log(1e-3), math.log(1e-1)))
    return {
        'x': jax.random.normal(ks[0], (BATCH, SEQ, D), f32),
        'c': jax.random.normal(ks[1], (BATCH, D), f32),
        'ada_w': nrm(ks[2], (L, D, 6 * D), D),
        'ada_b': 0.02 * jax.random.normal(ks[3], (L, 6 * D), f32),
        'norm1_g': 1.0 + 0.05 * jax.random.normal(ks[4], (L, D), f32),
        'w_in': nrm(ks[5], (L, D, IN_COLS), D),
        'pool_w': nrm(ks[6], (L, POOL_GROUPS, POOL_GROUP_WIDTH, POOL_GROUP_WIDTH), POOL_GROUP_WIDTH),
        'pool_scale': 1.0 + 0.1 * jax.random.normal(ks[7], (L, POOL_WIDTH), f32),
        'conv_w': nrm(ks[8], (L, SSD_CONV, SSD_CONV_DIM), SSD_CONV),
        'conv_b': 0.02 * jax.random.normal(ks[9], (L, SSD_CONV_DIM), f32),
        'dt_bias': dt0 + jnp.log(-jnp.expm1(-dt0)),
        'a_log': jnp.log(jax.random.uniform(ks[11], (L, SSD_HEADS), f32, 1.0, 16.0)),
        'd_skip': 1.0 + 0.1 * jax.random.normal(ks[12], (L, SSD_HEADS), f32),
        'ssd_norm_g': 1.0 + 0.05 * jax.random.normal(ks[13], (L, SSD_INNER), f32),
        'w_branch_pool': nrm(ks[14], (L, POOL_WIDTH, D), POOL_WIDTH),
        'w_branch_ssd': nrm(ks[15], (L, SSD_INNER, D), SSD_INNER),
        'w_out': nrm(ks[16], (L, D, D), D),
        'norm2_g': 1.0 + 0.05 * jax.random.normal(ks[17], (L, D), f32),
        'router_group_w': nrm(ks[18], (L, D, MOE_GROUPS), D),
        'router_group_b': 0.01 * jax.random.normal(ks[19], (L, MOE_GROUPS), f32),
        'router_expert_w': nrm(ks[20], (L, D, N_EXPERTS), D),
        'router_expert_b': 0.01 * jax.random.normal(ks[21], (L, N_EXPERTS), f32),
        'w13': nrm(ks[22], (L, N_EXPERTS, D, 2 * EXPERT_FF), D),
        'w2': nrm(ks[23], (L, N_EXPERTS, EXPERT_FF, D), EXPERT_FF),
        'final_norm_g': 1.0 + 0.05 * jax.random.normal(ks[24], (D,), f32),
    }

def reference(x, c, ada_w, ada_b, norm1_g, w_in, pool_w, pool_scale, conv_w, conv_b, dt_bias, a_log,
              d_skip, ssd_norm_g, w_branch_pool, w_branch_ssd, w_out, norm2_g, router_group_w,
              router_group_b, router_expert_w, router_expert_b, w13, w2, final_norm_g):
    for l in range(DEPTH):
        mod = jax.nn.silu(c) @ ada_w[l] + ada_b[l]
        sh1, sc1, g1, sh2, sc2, g2 = jnp.split(mod[:, None, :], 6, axis=-1)
        h = rmsnorm(x, norm1_g[l]) * (1.0 + sc1) + sh1
        x = x + g1 * mixer(h, w_in[l], pool_w[l], pool_scale[l], conv_w[l], conv_b[l], dt_bias[l],
                           a_log[l], d_skip[l], ssd_norm_g[l], w_branch_pool[l], w_branch_ssd[l], w_out[l])
        h = rmsnorm(x, norm2_g[l]) * (1.0 + sc2) + sh2
        x = x + g2 * hier_moe(h, router_group_w[l], router_group_b[l], router_expert_w[l],
                              router_expert_b[l], w13[l], w2[l])
    return rmsnorm(x, final_norm_g)


_drawn_inputs = setup_inputs


def setup_inputs(seed=0):
    import zlib

    import numpy as np

    out = dict(_drawn_inputs(seed))
    spreads = {}
    factors = {'conv_b': 3.233, 'd_skip': 3.028, 'router_group_b': 4.34, 'router_expert_b': 5.175}
    for name, (base, spread) in spreads.items():
        noise = np.random.default_rng([zlib.crc32(name.encode()), seed]).standard_normal(out[name].shape)
        drawn = base * np.exp(spread * noise) if base else spread * noise
        out[name] = __import__('jax').numpy.asarray(drawn.astype(out[name].dtype))
    for name, factor in factors.items():
        out[name] = (out[name] * factor).astype(out[name].dtype)
    return out
```

```python
from contextlib import ExitStack

import numpy as np

import concourse.bass as bass
from concourse import mybir

F32 = mybir.dt.float32
F32R = mybir.dt.float32r
BF16 = mybir.dt.bfloat16
U32 = mybir.dt.uint32
I32 = mybir.dt.int32
ALU = mybir.AluOpType
ACT = mybir.ActivationFunctionType
AX = mybir.AxisListType

P = 128
D = 1024
T = 1024
KT = D // P
TT = T // P
HALF = 512
HEADS = 32
HEAD_DIM = 64
GROUPS = 4
GH = HEADS // GROUPS
INNER = HEADS * HEAD_DIM
STATE = 128
CONV = 4
CONV_TILES = (INNER + 2 * GROUPS * STATE) // P
COL_Z = D
COL_X = COL_Z + INNER
COL_B = COL_X + INNER
COL_C = COL_B + GROUPS * STATE
COL_DT = COL_C + GROUPS * STATE
COL_GATE = COL_DT + HEADS
POOL_GROUPS = 4
WINDOWS = (2, 4, 8, 16)
PAD = max(WINDOWS)
MG = 4
EPG = 8
NE = MG * EPG
FF = 512
BLOCK = P
MAX_BLOCKS = 2 * T // BLOCK + NE - 1
EPS = 1e-6
NEG = -3.0e38

BASE = 16512


class Arena:

    def __init__(self, nc, prefix, start):
        self.nc, self.prefix, self.at = nc, prefix, start

    def __call__(self, name, shape, dtype=F32, at=None):
        offset = self.at if at is None else at
        t = self.nc.alloc_sbuf_tensor_at(f"{self.prefix}_{name}", shape, dtype, offset=offset)
        size = int(np.prod(shape[1:])) * (2 if dtype == BF16 else 4)
        if at is None:
            self.at = offset + (size + 31) // 32 * 32
        return t


class Chain:

    def __init__(self, eng, sem, base=0, per_pass=None):
        self.eng, self.sem, self.base, self.n, self.per_pass = eng, sem, base, 0, per_pass

    def __call__(self, ins):
        ins.then_inc(self.sem, 1)
        self.n += 1
        self.eng.wait_ge(self.sem, self.base + self.n)

    def done(self):
        assert self.per_pass is None or self.n == self.per_pass, (self.n, self.per_pass)


def bc(ap, shape):
    return ap.to_broadcast(shape)


def product(pe, out, hi, lo, rhs_hi, rhs_lo, start, stop):
    pe.matmul(out, hi, rhs_hi, start=start, stop=False)
    pe.matmul(out, hi, rhs_lo, start=False, stop=False)
    return pe.matmul(out, lo, rhs_hi, start=False, stop=stop)


class Kept:

    def __init__(self, nc):
        sb = self.sb = Arena(nc, "kept", BASE)
        self.ident = sb("ident", [P, P])
        self.ones = sb("ones", [P, P])
        self.tri = sb("tri", [P, P])
        self.tri_strict = sb("tri_strict", [P, P], BF16)
        self.ones_bf = sb("ones_bf", [P, P], BF16)
        self.cols_a = sb("cols_a", [P, P])
        self.cols_b = sb("cols_b", [P, 32])
        self.skip_col = sb("skip_col", [P, INNER // P])
        self.sq_acc = sb("sq_acc", [P, T])
        self.weight = [sb(f"weight{k}", [P, TT]) for k in range(2)]
        self.slot = [sb(f"slot{k}", [P, TT], U32) for k in range(2)]
        self.table = sb("table", [1, MAX_BLOCKS + 3], I32)
        self.logits = sb("logits", [P, TT, MG + NE])
        self.end = sb.at


def phase_modulate(nc, kept, a, dram):
    sb = Arena(nc, "p0", kept.end)
    hT_hi = sb("hT_hi", [P, KT, T], F32R)
    hT_lo = sb("hT_lo", [P, KT, T], F32R)
    x = sb("x", [P, TT, D])
    ADA = 4
    ada = sb("ada", [P, ADA, KT, 512 // 2])
    NCH = 6 * D // 256
    modr = sb("modr", [1, 6 * D])
    h_tmp = sb("h_tmp", [P, 2, T])
    rows_a = sb("rows_a", [P, P])
    rows_b = sb("rows_b", [32, P])
    skip_row = sb("skip_row", [P, HEADS])
    th_c = sb("th_c", [P, KT])
    silu_c = sb("silu_c", [P, KT])
    ss = sb("ss", [P, TT])
    var = sb("var", [P, TT])
    std = sb("std", [P, TT])
    rstd = sb("rstd", [P, TT])
    sh1 = sb("sh1", [P, KT])
    gs1 = sb("gs1", [P, KT])
    FIRST = 2 * D // 256

    with ExitStack() as ctx:
        sem = lambda n: nc.alloc_semaphore("p0_" + n)
        ps = lambda n: ctx.enter_context(nc.psum_tensor("p0_" + n, [P, HALF], F32))
        ps_cols = ps("cols")
        ps_ada = [ps("ada0"), ps("ada1")]
        ps_t = [[ps("t00"), ps("t01")], [ps("t10"), ps("t11")]]
        par_in, ident_made, consts_made, memsets = sem("par_in"), sem("ident_made"), sem("consts_made"), sem("memsets")
        ada_b_in, skip_in = sem("ada_b_in"), sem("skip_in")
        x_in = [sem(f"x_in{i}") for i in range(TT)]
        ada_in = [sem(f"ada_in{i}") for i in range(ADA)]
        ada_done, mod_row = sem("ada_done"), sem("mod_row")
        cols_turned, cols_copied, th_made, c_made = sem("cols_turned"), sem("cols_copied"), sem("th_made"), sem("c_made")
        squared, var_made, std_made, x_normed = sem("squared"), sem("var_made"), sem("std_made"), sem("x_normed")
        sh_turned, sh_made = sem("sh_turned"), sem("sh_made")
        x_turned, h_made, h_split = sem("x_turned"), sem("h_made"), sem("h_split")
        dve_seq, mod_out = sem("dve_seq"), sem("mod_out")
        blk = ctx.enter_context(nc.Block())

        @blk.sync
        def _(sp):
            sp.dma_start(rows_a[0:8, :], a["norm1_g"][0].rearrange("(j p) -> j p", p=P)).then_inc(par_in, 16)
            sp.dma_start(rows_a[8:32, :], a["conv_b"][0].rearrange("(j p) -> j p", p=P)).then_inc(par_in, 16)
            sp.dma_start(rows_a[32:128, :], a["conv_w"][0].rearrange("w (j p) -> (w j) p", p=P)).then_inc(par_in, 16)
            sp.dma_start(rows_b[0:8, :], a["pool_scale"][0].rearrange("(j p) -> j p", p=P)).then_inc(par_in, 16)
            sp.dma_start(rows_b[8:24, :], a["ssd_norm_g"][0].rearrange("(j p) -> j p", p=P)).then_inc(par_in, 16)
            sp.dma_start(rows_b[24:32, :], a["c"][0].rearrange("(j p) -> j p", p=P)).then_inc(par_in, 16)
            for n in range(NCH):
                if n >= ADA:
                    sp.wait_ge(ada_done, n - ADA + 1)
                sp.dma_start(ada[:, n % ADA], a["ada_w"][0, :, n * 256:(n + 1) * 256]
                             .rearrange("(k p) n -> p k n", p=P)).then_inc(ada_in[n % ADA], 16)
            sp.wait_ge(mod_row, NCH)
            sp.dma_start(dram["mod"], modr[0:1, 2 * D:]).then_inc(mod_out, 16)
            sp.wait_ge(mod_out, 16)

        @blk.gpsimd
        def _(pool):
            pool.memset(kept.ident[:], 0.0).then_inc(memsets, 1)
            pool.memset(kept.tri[:], 1.0).then_inc(memsets, 1)
            pool.memset(kept.tri_strict[:], 1.0).then_inc(memsets, 1)
            pool.memset(kept.ones[:], 1.0).then_inc(consts_made, 1)
            pool.memset(kept.ones_bf[:], 1.0).then_inc(consts_made, 1)
            pool.wait_ge(memsets, 3)
            pool.affine_select(out=kept.ident[:], in_=kept.ident[:], compare_op=ALU.not_equal, fill=1.0,
                               base=0, pattern=[[-1, P]], channel_multiplier=1).then_inc(ident_made, 1)
            pool.affine_select(out=kept.tri[:], in_=kept.tri[:], compare_op=ALU.is_ge, fill=0.0,
                               base=0, pattern=[[1, P]], channel_multiplier=-1).then_inc(consts_made, 1)
            pool.affine_select(out=kept.tri_strict[:], in_=kept.tri_strict[:], compare_op=ALU.is_gt, fill=0.0,
                               base=0, pattern=[[1, P]], channel_multiplier=-1).then_inc(consts_made, 1)

        @blk.scalar
        def _(act):
            act.dma_start(modr[:], a["ada_b"]).then_inc(ada_b_in, 16)
            act.dma_start(skip_row[:], a["d_skip"][0].partition_broadcast(P)).then_inc(skip_in, 16)
            for i in range(TT):
                act.dma_start(x[:, i, :], a["x"][0, i * P:(i + 1) * P, :]).then_inc(x_in[i], 16)
            act.wait_ge(cols_copied, 2)
            act.activation(th_c[:], kept.cols_b[:, 24:32], ACT.Tanh, scale=0.5).then_inc(th_made, 1)
            for i in range(TT):
                act.wait_ge(x_in[i], 16)
                if i >= 2:
                    act.wait_ge(squared, i - 1)
                act.activation(h_tmp[:, i % 2, :], x[:, i, :], ACT.Square,
                               accum_out=ss[:, i:i + 1]).then_inc(squared, 1)
            act.wait_ge(var_made, 1)
            act.activation(std[:], var[:], ACT.Sqrt).then_inc(std_made, 1)
            act.wait_ge(sh_made, 2)
            act.wait_ge(squared, TT)
            for k in range(KT):
                act.wait_ge(x_turned, k + 1)
                if k >= 2:
                    act.wait_ge(h_split, k - 1)
                for b in range(2):
                    act.activation(h_tmp[:, k % 2, b * HALF:(b + 1) * HALF], ps_t[k % 2][b][:], ACT.Identity,
                                   bias=sh1[:, k:k + 1], scale=gs1[:, k:k + 1]).then_inc(h_made, 1)

        @blk.vector
        def _(dve):
            link = Chain(dve, dve_seq)
            dve.wait_ge(cols_turned, 1)
            dve.tensor_copy(kept.cols_a[:], ps_cols[:, 0:P]).then_inc(cols_copied, 1)
            dve.tensor_copy(kept.cols_b[:], ps_cols[:, P:P + 32]).then_inc(cols_copied, 1)
            dve.wait_ge(th_made, 1)
            dve.wait_ge(cols_copied, 2)
            link(dve.scalar_tensor_tensor(silu_c[:], th_c[:], 1.0, kept.cols_b[:, 24:32], ALU.add, ALU.mult))
            dve.tensor_scalar(silu_c[:], silu_c[:], 0.5, None, ALU.mult).then_inc(c_made, 1)
            dve.wait_ge(skip_in, 16)
            dve.tensor_copy(kept.skip_col[0:64, :], skip_row[0:64, 0::2])
            dve.tensor_copy(kept.skip_col[64:128, :], skip_row[64:128, 1::2])
            dve.wait_ge(squared, TT)
            dve.tensor_scalar(var[:], ss[:], 1.0 / D, EPS, ALU.mult, ALU.add).then_inc(var_made, 1)
            dve.wait_ge(std_made, 1)
            link(dve.reciprocal(rstd[:], std[:]))
            for i in range(TT):
                dve.tensor_scalar(x[:, i, :], x[:, i, :], rstd[:, i:i + 1], None, ALU.mult).then_inc(x_normed, 1)

            def mod_chunk(n):
                dve.wait_ge(ada_done, n + 1)
                if n == 0:
                    dve.wait_ge(ada_b_in, 16)
                row = modr[0:1, n * 256:(n + 1) * 256]
                dve.tensor_tensor(row, ps_ada[n % 2][0:1, 0:256], row, ALU.add).then_inc(mod_row, 1)

            for n in range(FIRST):
                mod_chunk(n)
            dve.wait_ge(sh_turned, 1)
            dve.tensor_copy(sh1[:], ps_cols[:, 256:264]).then_inc(sh_made, 1)
            dve.scalar_tensor_tensor(gs1[:], ps_cols[:, 264:272], 1.0, kept.cols_a[:, 0:8],
                                     ALU.add, ALU.mult).then_inc(sh_made, 1)
            for k in range(KT):
                dve.wait_ge(h_made, 2 * k + 2)
                link(dve.tensor_copy(hT_hi[:, k, :], h_tmp[:, k % 2, :]))
                dve.tensor_tensor(hT_lo[:, k, :], h_tmp[:, k % 2, :], hT_hi[:, k, :].bitcast(F32),
                                  ALU.subtract).then_inc(h_split, 1)
                mod_chunk(FIRST + 2 * k)
                mod_chunk(FIRST + 2 * k + 1)

        @blk.tensor
        def _(pe):
            pe.wait_ge(par_in, 96)
            pe.wait_ge(ident_made, 1)
            pe.transpose(ps_cols[:, 0:P], rows_a[:], kept.ident[:])
            pe.transpose(ps_cols[:, P:P + 32], rows_b[:], kept.ident[0:32, 0:32]).then_inc(cols_turned, 1)
            pe.wait_ge(c_made, 1)

            def ada_chunk(n):
                pe.wait_ge(ada_in[n % ADA], 16 * (n // ADA + 1))
                if n >= 2:
                    pe.wait_ge(mod_row, n - 1)
                for k in range(KT):
                    mm = pe.matmul(ps_ada[n % 2][0:1, 0:256], silu_c[:, k:k + 1], ada[:, n % ADA, k, :],
                                   start=(k == 0), stop=(k == KT - 1))
                mm.then_inc(ada_done, 1)

            for n in range(FIRST):
                ada_chunk(n)
            pe.wait_ge(mod_row, FIRST)
            pe.wait_ge(consts_made, 4)
            for j in range(2 * KT):
                mm = pe.matmul(ps_cols[:, 256 + j:257 + j], modr[0:1, j * P:(j + 1) * P], kept.ones[0:1, 0:1],
                               start=True, stop=True)
            mm.then_inc(sh_turned, 1)
            pe.wait_ge(x_normed, TT)
            for k in range(KT):
                if k >= 2:
                    pe.wait_ge(h_made, 2 * k - 2)
                for i in range(TT):
                    mm = pe.transpose(ps_t[k % 2][i // 4][:, (i % 4) * P:(i % 4 + 1) * P],
                                      x[:, i, k * P:(k + 1) * P], kept.ident[:])
                mm.then_inc(x_turned, 1)
                ada_chunk(FIRST + 2 * k)
                ada_chunk(FIRST + 2 * k + 1)
    return hT_hi, hT_lo


def phase_steps(nc, kept, a, dram, hT_hi, hT_lo):
    sb = Arena(nc, "p1", kept.end + 2 * KT * T * 4)
    small = sb("small", [P, 5, TT, HEADS])
    small_g = sb("small_g", [P, GROUPS, 5 * TT, GH])
    acs, dt, dtdec, exp_acs, exp_end = (small[:, n] for n in range(5))
    w = sb("w", [P, KT, HEADS])
    w_hi = sb("w_hi", [P, KT, HEADS], F32R)
    w_lo = sb("w_lo", [P, KT, HEADS], F32R)
    bias = sb("bias", [P, HEADS])
    a_log = sb("a_log", [P, HEADS])
    a_neg = sb("a_neg", [P, HEADS])
    S = [P, TT, HEADS]
    raw, mag, ex, u, ln_u, um1, is0, a_dt, dif = (sb(n, S) for n in
                                                  ("raw", "mag", "ex", "u", "ln_u", "um1", "is0", "a_dt", "dif"))
    acs_rows = sb("acs_rows", [HEADS, T])
    with ExitStack() as ctx:
        sem = lambda n: nc.alloc_semaphore("p1_" + n)
        ps = lambda n: ctx.enter_context(nc.psum_tensor("p1_" + n, [P, HALF], F32))
        ps_dt, ps_cum, ps_end = ps("dt"), ps("cum"), ps("end")
        ps_rows = [ps("rows0"), ps("rows1")]
        par_in, w_split, dt_done, seq, act_seq = sem("par_in"), sem("w_split"), sem("dt_done"), sem("seq"), sem("act_seq")
        mag_made, ex_made, u_made, ln_made, a_made = sem("mag_made"), sem("ex_made"), sem("u_made"), sem("ln_made"), sem("a_made")
        alog_done, summed, acs_made, rows_turned = sem("alog_done"), sem("summed"), sem("acs_made"), sem("rows_turned")
        dif_made, dec_made, rows_made, rows_out = sem("dif_made"), sem("dec_made"), sem("rows_made"), sem("rows_out")
        by_group = sem("by_group")
        blk = ctx.enter_context(nc.Block())

        @blk.sync
        def _(sp):
            sp.dma_start(w[:], a["w_in"][0, :, COL_DT:COL_DT + HEADS].rearrange("(k p) n -> p k n", p=P)).then_inc(par_in, 16)
            sp.dma_start(bias[:], a["dt_bias"][0].partition_broadcast(P)).then_inc(par_in, 16)
            sp.dma_start(a_log[:], a["a_log"][0].partition_broadcast(P)).then_inc(par_in, 16)
            sp.wait_ge(rows_made, 2)
            sp.dma_start(dram["acs"], acs_rows[:]).then_inc(rows_out, 16)
            sp.wait_ge(by_group, 1)
            sp.dma_start(dram["small"], small_g[:]).then_inc(rows_out, 16)
            sp.wait_ge(rows_out, 32)

        @blk.scalar
        def _(act):
            act.wait_ge(par_in, 48)
            act.activation(a_neg[:], a_log[:], ACT.Exp).then_inc(alog_done, 1)
            act.wait_ge(mag_made, 1)
            act.activation(ex[:], mag[:], ACT.Exp, scale=-1.0).then_inc(ex_made, 1)
            act.wait_ge(u_made, 1)
            act.activation(ln_u[:], u[:], ACT.Ln).then_inc(ln_made, 1)
            act.wait_ge(dif_made, 1)
            act.activation(dif[:], dif[:], ACT.Exp).then_inc(dec_made, 1)
            act.activation(exp_acs, acs, ACT.Exp).then_inc(dec_made, 1)
            act.activation(exp_end, exp_end, ACT.Exp).then_inc(dec_made, 1)

        @blk.vector
        def _(dve):
            link = Chain(dve, seq)
            dve.wait_ge(par_in, 48)
            link(dve.tensor_copy(w_hi[:], w[:]))
            dve.tensor_tensor(w_lo[:], w[:], w_hi[:].bitcast(F32), ALU.subtract).then_inc(w_split, 1)
            dve.wait_ge(dt_done, 1)
            link(dve.tensor_tensor(raw[:], ps_dt[:, 0:TT * HEADS].rearrange("p (t h) -> p t h", h=HEADS),
                                   bc(bias[:].unsqueeze(1), S), ALU.add))
            link(dve.tensor_scalar(mag[:], raw[:], -1.0, None, ALU.mult))
            dve.tensor_tensor(mag[:], raw[:], mag[:], ALU.max).then_inc(mag_made, 1)
            dve.wait_ge(ex_made, 1)
            dve.tensor_scalar(u[:], ex[:], 1.0, None, ALU.add).then_inc(u_made, 1)
            dve.wait_ge(u_made, 1)
            link(dve.tensor_scalar(um1[:], u[:], -1.0, None, ALU.add))
            link(dve.tensor_scalar(is0[:], um1[:], 0.0, None, ALU.is_equal))
            link(dve.tensor_tensor(um1[:], um1[:], is0[:], ALU.add))
            link(dve.reciprocal(um1[:], um1[:]))
            dve.wait_ge(ln_made, 1)
            link(dve.tensor_tensor(ln_u[:], ln_u[:], um1[:], ALU.mult))
            link(dve.tensor_tensor(ln_u[:], ln_u[:], is0[:], ALU.add))
            link(dve.tensor_tensor(ln_u[:], ln_u[:], ex[:], ALU.mult))
            link(dve.scalar_tensor_tensor(dt, raw[:], 0.0, ln_u[:], ALU.max, ALU.add))
            dve.wait_ge(alog_done, 1)
            link(dve.tensor_scalar(a_neg[:], a_neg[:], -1.0, None, ALU.mult))
            dve.tensor_tensor(a_dt[:], dt, bc(a_neg[:].unsqueeze(1), S), ALU.mult).then_inc(a_made, 1)
            dve.wait_ge(summed, 1)
            dve.tensor_copy(acs, ps_cum[:, 0:TT * HEADS].rearrange("p (t h) -> p t h", h=HEADS)).then_inc(acs_made, 1)
            link(dve.tensor_copy(exp_end, ps_end[:, 0:TT * HEADS].rearrange("p (t h) -> p t h", h=HEADS)))
            dve.wait_ge(acs_made, 1)
            dve.tensor_tensor(dif[:], exp_end, acs, ALU.subtract).then_inc(dif_made, 1)
            for b in range(2):
                dve.wait_ge(rows_turned, b + 1)
                dve.tensor_copy(acs_rows[:, b * HALF:(b + 1) * HALF], ps_rows[b][0:HEADS, :]).then_inc(rows_made, 1)
            dve.wait_ge(dec_made, 3)
            link(dve.tensor_tensor(dtdec, dt, dif[:], ALU.mult))
            dve.tensor_copy(small_g[:], small[:].rearrange("p a t (g h) -> p g (a t) h", h=GH)).then_inc(by_group, 1)

        @blk.tensor
        def _(pe):
            pe.wait_ge(w_split, 1)
            for i in range(TT):
                rows = slice(i * P, (i + 1) * P)
                for k in range(KT):
                    mm = product(pe, ps_dt[:, i * HEADS:(i + 1) * HEADS], hT_hi[:, k, rows], hT_lo[:, k, rows],
                                 w_hi[:, k, :], w_lo[:, k, :], k == 0, k == KT - 1)
            mm.then_inc(dt_done, 1)
            pe.wait_ge(a_made, 1)
            pe.matmul(ps_cum[:, 0:TT * HEADS], kept.tri[:], a_dt[:].rearrange("p t h -> p (t h)"), start=True, stop=True)
            pe.matmul(ps_end[:, 0:TT * HEADS], kept.ones[:], a_dt[:].rearrange("p t h -> p (t h)"),
                      start=True, stop=True).then_inc(summed, 1)
            pe.wait_ge(acs_made, 1)
            for i in range(TT):
                mm = pe.transpose(ps_rows[i // 4][0:HEADS, (i % 4) * P:(i % 4 + 1) * P], acs[:, i, :], kept.ident[:])
                if i % 4 == 3:
                    mm.then_inc(rows_turned, 1)



def phase_ssd(nc, kept, a, dram, hT_hi, hT_lo):
    sb = Arena(nc, "p2", kept.end + 2 * KT * T * 4)
    acc = sb("acc", [P, KT, T])
    RAW = 2
    raw = sb("raw", [P, RAW, KT, P])
    w_hi = sb("w_hi", [P, RAW, KT, P], F32R)
    w_lo = sb("w_lo", [P, RAW, KT, P], F32R)
    NX = INNER // GROUPS // P
    NXBC = NX + 2
    cvb = sb("cvb", [P, CONV - 1 + T])
    xcT = sb("xcT", [P, NXBC, T])
    at = sb.at
    zT = sb("zT", [P, NX, T])
    yh = sb("yh", [P, NX, T], F32R, at=at)
    at = sb.at
    yT = sb("yT", [P, NX, T])
    yl = sb("yl", [P, NX, T], F32R, at=at)
    seg = sb("seg", [P, 2, GH, P])
    XG = [P, GH, HEAD_DIM]
    x_dt, x_dec, y_tok, state = (sb(n, XG) for n in ("x_dt", "x_dec", "y_tok", "state"))
    b_tok = sb("b_tok", [P, P])
    cbm = sb("cbm", [P, P])
    gp = sb("gp", [P, 1 + CONV, NXBC])
    gs = sb("gs", [P, 5, TT, GH])
    gcol = sb("gcol", [P, 2, NX])
    NPROJ, NBR = NXBC + NX, KT
    NW = NPROJ + NBR // 2

    with ExitStack() as ctx:
        sem = lambda n: nc.alloc_semaphore("p2_" + n)
        ps = lambda n: ctx.enter_context(nc.psum_tensor("p2_" + n, [P, HALF], F32))
        pair = [[ps("pair00"), ps("pair01")], [ps("pair10"), ps("pair11")]]
        ps_x, ps_cb, ps_yd, ps_yo = ps("x"), ps("cb"), ps("yd"), ps("yo")
        w_in = [sem(f"w_in{i}") for i in range(RAW)]
        seg_in = [sem(f"seg_in{i}") for i in range(2)]
        hi_made, lo_made, w_used = sem("hi_made"), sem("lo_made"), sem("w_used")
        proj_done, br_done, proj_read, br_read = sem("proj_done"), sem("br_done"), sem("proj_read"), sem("br_read")
        pads, acc_zeroed, params = sem("pads"), sem("acc_zeroed"), sem("params")
        pre_made, th_made, xc_made, zth_made, z_made = (sem(n) for n in ("pre_made", "th_made", "xc_made", "zth_made", "z_made"))
        xt_done, xdt_made, cb_done, cbm_made, bt_made = (sem(n) for n in ("xt_done", "xdt_made", "cb_done", "cbm_made", "bt_made"))
        seg_made, exp_made, g_made, yo_done, yd_done = (sem(n) for n in ("seg_made", "exp_made", "g_made", "yo_done", "yd_done"))
        st_done, y_made, st_made, ytr_done, yT_made = (sem(n) for n in ("st_done", "y_made", "st_made", "ytr_done", "yT_made"))
        y_gated, sq_made, sq_added, yh_made, yl_made = (sem(n) for n in ("y_gated", "sq_made", "sq_added", "yh_made", "yl_made"))
        seq, zeroed, acc_out, gs_in = sem("seq"), sem("zeroed"), sem("acc_out"), sem("gs_in")
        blk = ctx.enter_context(nc.Block())
        W_CREDIT = RAW
        BR_CREDIT = 2
        SEG_CREDIT = 2
        SQ_CREDIT = 1
        SEQ_N = 2 + NXBC * (CONV - 1) + (TT - 1) + (TT - 2) + NX

        @blk.sync
        def _(sp):
            with sp.Fori(0, GROUPS) as g:
                def load(i, src):
                    sp.wait_ge(lo_made, g * NW + i + 1)
                    sp.dma_start(raw[:, i % RAW] if i < NPROJ else
                                 raw[:, i % RAW].rearrange("p k n -> p (k n)").rearrange("p (k n) -> p k n", k=NX),
                                 src).then_inc(w_in[i % RAW], 16)
                wide, narrow = sp.snap(g * (NX * P)), sp.snap(g * P)
                cols = [(COL_X + j * P, wide) for j in range(NX)] + [(COL_B, narrow), (COL_C, narrow)] + \
                       [(COL_Z + j * P, wide) for j in range(NX)]
                for i, (first, col) in enumerate(cols):
                    load(i, a["w_in"][0, :, first:][:, bass.ds(col, P)].rearrange("(k p) n -> p k n", p=P))
                for m in range(NBR // 2):
                    load(NPROJ + m, a["w_branch_ssd"][0, bass.ds(g * (NX * P), NX * P), 2 * m * P:(2 * m + 2) * P]
                         .rearrange("(k p) n -> p k n", p=P))
            sp.wait_ge(br_read, BR_CREDIT + GROUPS * NBR)
            sp.dma_start(dram["acc"], acc[:]).then_inc(acc_out, 16)
            sp.wait_ge(acc_out, 16)

        @blk.gpsimd
        def _(pool):
            pool.sem_inc(yd_done, SEG_CREDIT)
            pool.sem_inc(sq_added, SQ_CREDIT)
            pool.memset(cvb[:, 0:CONV - 1], 0.0).then_inc(pads, 1)
            pool.memset(kept.sq_acc[:], 0.0).then_inc(acc_zeroed, 1)
            pool.memset(acc[:], 0.0).then_inc(acc_zeroed, 1)
            x_buf = dram["x_buf"].rearrange("(b p) c -> b p c", p=P)
            pool.wait_ge(acc_zeroed, 2)
            for b in range(MAX_BLOCKS + 1):
                pool.dma_start(x_buf[b], acc[:, 0, :]).then_inc(zeroed, 16)
            with pool.Fori(0, GROUPS) as g:
                pool.dma_start(gs[:], dram["small"][:, bass.ds(g, 1)].rearrange("p g (a t) h -> p (g a) t h", t=TT)).then_inc(gs_in, 16)
                for c in range(TT):
                    pool.wait_ge(yd_done, g * TT + c + 1)
                    pool.dma_start(seg[:, c % 2], dram["acs"][bass.ds(g * GH, GH), c * P:(c + 1) * P]
                                   .partition_broadcast(P)).then_inc(seg_in[c % 2], 16)
                for j in range(NX):
                    pool.wait_ge(sq_made, g * NX + j + 1)
                    if j:
                        pool.wait_ge(sq_added, g * NX + j + SQ_CREDIT)
                    pool.tensor_tensor(kept.sq_acc[:], kept.sq_acc[:], cvb[:, CONV - 1:], ALU.add).then_inc(sq_added, 1)
            pool.wait_ge(zeroed, 16 * (MAX_BLOCKS + 1))

        @blk.scalar
        def _(act):
            with act.Fori(0, GROUPS) as g:
                def hi(i):
                    slot = i % RAW
                    act.wait_ge(w_in[slot], 16 * (g * (NW // RAW) + i // RAW + 1))
                    act.wait_ge(w_used, g * NW + i + 1)
                    act.activation(w_hi[:, slot], raw[:, slot], ACT.Copy).then_inc(hi_made, 1)

                hi(0)
                hi(1)
                for i in range(NXBC):
                    if i == 0:
                        act.wait_ge(sq_added, g * NX + SQ_CREDIT)
                    else:
                        act.wait_ge(xc_made, g * NXBC + i)
                    for b in range(2):
                        act.wait_ge(proj_done, g * (2 * NPROJ) + 2 * i + b + 1)
                        act.activation(cvb[:, CONV - 1 + b * HALF:CONV - 1 + (b + 1) * HALF], pair[i % 2][b][:],
                                       ACT.Copy).then_inc(proj_read, 1)
                    hi(i + 2)
                    act.wait_ge(pre_made, g * NXBC + i + 1)
                    act.activation(cvb[:, CONV - 1:], xcT[:, i, :], ACT.Tanh).then_inc(th_made, 1)

                def y_out(c):
                    act.wait_ge(ytr_done, g * TT + c + 1)
                    act.activation(yT[:, :, c * P:(c + 1) * P], ps_yo[:].rearrange("p (j l) -> p j l", l=P),
                                   ACT.Copy).then_inc(yT_made, 1)

                for c in range(TT):
                    j, b = divmod(c, 2)
                    i = NXBC + j
                    act.wait_ge(seg_made, g * TT + c + 1)
                    act.activation(seg[:, c % 2], seg[:, c % 2], ACT.Exp).then_inc(exp_made, 1)
                    act.wait_ge(cbm_made, g * TT + c + 1)
                    act.activation(b_tok[:], ps_cb[:, P:2 * P], ACT.Copy).then_inc(bt_made, 1)
                    if c:
                        y_out(c - 1)
                    if b == 0:
                        if j == 0:
                            act.wait_ge(xc_made, g * NXBC + NXBC)
                        else:
                            act.wait_ge(z_made, g * NX + j)
                    act.wait_ge(proj_done, g * (2 * NPROJ) + 2 * i + b + 1)
                    half = slice(b * HALF, (b + 1) * HALF)
                    act.activation(zT[:, j, half], pair[i % 2][b][:], ACT.Copy, scale=0.5)
                    act.activation(cvb[:, CONV - 1 + b * HALF:CONV - 1 + (b + 1) * HALF], pair[i % 2][b][:],
                                   ACT.Tanh, scale=0.5).then_inc(proj_read, 1)
                    if b == 1:
                        hi(i + 2)
                y_out(TT - 1)
                for j in range(NX):
                    act.wait_ge(y_gated, g * NX + j + 1)
                    act.activation(yh[:, j, :], yT[:, j, :], ACT.Copy, scale=gcol[:, 0, j:j + 1]).then_inc(yh_made, 1)
                    act.wait_ge(sq_added, g * NX + j + SQ_CREDIT)
                    act.activation(cvb[:, CONV - 1:], yT[:, j, :], ACT.Square).then_inc(sq_made, 1)
                hi(NW - 2)
                hi(NW - 1)

        @blk.vector
        def _(dve):
            dve.sem_inc(lo_made, W_CREDIT)
            dve.sem_inc(br_read, BR_CREDIT)
            dve.wait_ge(pads, 1)
            dve.wait_ge(acc_zeroed, 2)
            with dve.Fori(0, GROUPS) as g:
                link = Chain(dve, seq, g * SEQ_N, SEQ_N)

                def lo(i):
                    slot = i % RAW
                    dve.wait_ge(hi_made, g * NW + i + 1)
                    dve.tensor_tensor(w_lo[:, slot], raw[:, slot], w_hi[:, slot].bitcast(F32),
                                      ALU.subtract).then_inc(lo_made, 1)

                conv_cols = kept.cols_a[:, 8:8 + (1 + CONV) * CONV_TILES].rearrange("p (w m) -> p w m", m=CONV_TILES)
                dve.tensor_copy(gp[:, :, 0:NX], conv_cols[:, :, bass.ds(g * NX, NX)])
                dve.tensor_copy(gp[:, :, NX:NX + 1], conv_cols[:, :, bass.ds(g + INNER // P, 1)])
                dve.tensor_copy(gp[:, :, NX + 1:NX + 2], conv_cols[:, :, bass.ds(g + INNER // P + GROUPS, 1)])
                dve.tensor_copy(gcol[:, 0, :], kept.cols_b[:, bass.ds(g * NX + 8, NX)])
                link(dve.tensor_copy(gcol[:, 1, :], kept.skip_col[:, bass.ds(g * NX, NX)]))
                link(dve.tensor_scalar(gp[:], gp[:], 0.5, None, ALU.mult))
                g_acs, g_dt, g_dtdec, g_exp, g_end = (gs[:, n] for n in range(5))
                lo(0)
                lo(1)
                for i in range(NXBC):
                    dve.wait_ge(proj_read, g * (2 * NPROJ) + 2 * i + 2)
                    link(dve.tensor_scalar(xcT[:, i, :], cvb[:, 0:T], gp[:, 1, i:i + 1], gp[:, 0, i:i + 1],
                                           ALU.mult, ALU.add))
                    for w in range(1, CONV):
                        ins = dve.scalar_tensor_tensor(xcT[:, i, :], cvb[:, w:w + T], gp[:, 1 + w, i:i + 1],
                                                       xcT[:, i, :], ALU.mult, ALU.add)
                        if w < CONV - 1:
                            link(ins)
                    ins.then_inc(pre_made, 1)
                    lo(i + 2)
                    dve.wait_ge(th_made, g * NXBC + i + 1)
                    dve.wait_ge(pre_made, g * NXBC + i + 1)
                    dve.scalar_tensor_tensor(xcT[:, i, :], cvb[:, CONV - 1:], 1.0, xcT[:, i, :],
                                             ALU.add, ALU.mult).then_inc(xc_made, 1)

                def segments(c):
                    dve.wait_ge(seg_in[c % 2], 16 * (g * (TT // 2) + c // 2 + 1))
                    for h in range(GH):
                        ins = dve.tensor_scalar(seg[:, c % 2, h, :], seg[:, c % 2, h, :], g_acs[:, c, h:h + 1], 0.0,
                                                ALU.subtract, ALU.min)
                    ins.then_inc(seg_made, 1)

                dve.wait_ge(gs_in, 16 * (g + 1))
                segments(0)
                for c in range(TT):
                    dve.wait_ge(xt_done, g * TT + c + 1)
                    xt = ps_x[:].rearrange("p (h d) -> p h d", d=HEAD_DIM)
                    dve.tensor_tensor(x_dt[:], xt, bc(g_dt[:, c, :].unsqueeze(2), XG), ALU.mult)
                    dve.tensor_tensor(x_dec[:], xt, bc(g_dtdec[:, c, :].unsqueeze(2), XG), ALU.mult).then_inc(xdt_made, 1)
                    dve.wait_ge(cb_done, g * TT + c + 1)
                    dve.tensor_tensor(cbm[:], ps_cb[:, 0:P], kept.tri[:], ALU.mult).then_inc(cbm_made, 1)
                    dve.wait_ge(cbm_made, g * TT + c + 1)
                    dve.wait_ge(exp_made, g * TT + c + 1)
                    dve.tensor_tensor(seg[:, c % 2], seg[:, c % 2], bc(cbm[:].unsqueeze(1), [P, GH, P]),
                                      ALU.mult).then_inc(g_made, 1)
                    if c + 1 < TT:
                        segments(c + 1)
                    if c:
                        dve.wait_ge(yo_done, g * (TT - 1) + c)
                        dve.wait_ge(ytr_done, g * TT + c)
                        link(dve.tensor_tensor(y_tok[:], ps_yo[:].rearrange("p (h d) -> p h d", d=HEAD_DIM),
                                               bc(g_exp[:, c, :].unsqueeze(2), XG), ALU.mult))
                        dve.wait_ge(yd_done, g * TT + c + 1 + SEG_CREDIT)
                        dve.tensor_tensor(y_tok[:], ps_yd[:].rearrange("p (h d) -> p h d", d=HEAD_DIM), y_tok[:],
                                          ALU.add).then_inc(y_made, 1)
                    else:
                        dve.wait_ge(yd_done, g * TT + c + 1 + SEG_CREDIT)
                        dve.tensor_copy(y_tok[:], ps_yd[:].rearrange("p (h d) -> p h d", d=HEAD_DIM)).then_inc(y_made, 1)
                    if c < TT - 1:
                        dve.wait_ge(st_done, g * (TT - 1) + c + 1)
                        if c:
                            link(dve.tensor_tensor(state[:], state[:], bc(g_end[:, c, :].unsqueeze(2), XG), ALU.mult))
                            dve.tensor_tensor(state[:], ps_x[:].rearrange("p (h d) -> p h d", d=HEAD_DIM), state[:],
                                              ALU.add).then_inc(st_made, 1)
                        else:
                            dve.tensor_copy(state[:], ps_x[:].rearrange("p (h d) -> p h d", d=HEAD_DIM)).then_inc(st_made, 1)
                    if c % 2:
                        j = c // 2
                        dve.wait_ge(proj_read, g * (2 * NPROJ) + 2 * (NXBC + j) + 2)
                        dve.scalar_tensor_tensor(zT[:, j, :], cvb[:, CONV - 1:], 1.0, zT[:, j, :],
                                                 ALU.add, ALU.mult).then_inc(z_made, 1)
                        lo(NXBC + j + 2)
                dve.wait_ge(yT_made, g * TT + TT)
                dve.wait_ge(z_made, g * NX + NX)
                for j in range(NX):
                    link(dve.scalar_tensor_tensor(yT[:, j, :], xcT[:, j, :], gcol[:, 1, j:j + 1], yT[:, j, :],
                                                  ALU.mult, ALU.add))
                    dve.tensor_tensor(yT[:, j, :], yT[:, j, :], zT[:, j, :], ALU.mult).then_inc(y_gated, 1)
                for j in range(NX):
                    dve.wait_ge(yh_made, g * NX + j + 1)
                    dve.wait_ge(sq_made, g * NX + j + 1)
                    dve.scalar_tensor_tensor(yl[:, j, :], yT[:, j, :], gcol[:, 0, j:j + 1], yh[:, j, :].bitcast(F32),
                                             ALU.mult, ALU.subtract).then_inc(yl_made, 1)
                dve.wait_ge(zeroed, 16 * (MAX_BLOCKS + 1))
                for n in range(NBR):
                    if n % 2 == 0 and NPROJ + n // 2 + 2 < NW:
                        lo(NPROJ + n // 2 + 2)
                    for b in range(2):
                        half = slice(b * HALF, (b + 1) * HALF)
                        dve.wait_ge(br_done, g * (2 * NBR) + 2 * n + b + 1)
                        ins = dve.tensor_tensor(acc[:, n, half], pair[n % 2][b][:], acc[:, n, half], ALU.add)
                    ins.then_inc(br_read, 1)
                link.done()

        @blk.tensor
        def _(pe):
            pe.sem_inc(w_used, W_CREDIT)
            with pe.Fori(0, GROUPS) as g:
                def begin(i):
                    pe.wait_ge(lo_made, g * NW + i + 1 + W_CREDIT)
                    pe.wait_ge(hi_made, g * NW + i + 1)

                def part(i, b, k0, k1):
                    for k in range(k0, k1):
                        mm = product(pe, pair[i % 2][b][:], w_hi[:, i % RAW, k, :], w_lo[:, i % RAW, k, :],
                                     hT_hi[:, k, b * HALF:(b + 1) * HALF], hT_lo[:, k, b * HALF:(b + 1) * HALF],
                                     k == 0, k == KT - 1)
                    if k1 == KT:
                        mm.then_inc(proj_done, 1)
                        if b == 1:
                            pe.wait_ge(proj_done, g * (2 * NPROJ) + 2 * i + 2)
                            pe.sem_inc(w_used, 1)

                for i in range(NXBC):
                    begin(i)
                    if i < 2:
                        pe.wait_ge(br_read, g * NBR + i + 1)
                    else:
                        pe.wait_ge(proj_read, g * (2 * NPROJ) + 2 * (i - 2) + 2)
                    part(i, 0, 0, KT)
                    part(i, 1, 0, KT)

                def y_turn(c):
                    pe.wait_ge(y_made, g * TT + c + 1)
                    for j in range(NX):
                        mm = pe.transpose(ps_yo[:, j * P:(j + 1) * P],
                                          y_tok[:].rearrange("p h d -> p (h d)")[:, j * P:(j + 1) * P], kept.ident[:])
                    mm.then_inc(ytr_done, 1)

                bT, cT = xcT[:, NX, :], xcT[:, NX + 1, :]
                pe.wait_ge(xc_made, g * NXBC + NXBC)
                for c in range(TT):
                    ch = slice(c * P, (c + 1) * P)
                    j, b = divmod(c, 2)
                    i = NXBC + j
                    if c:
                        pe.wait_ge(st_made, g * (TT - 1) + c)
                    for m in range(NX):
                        mm = pe.transpose(ps_x[:, m * P:(m + 1) * P], xcT[:, m, ch], kept.ident[:])
                    mm.then_inc(xt_done, 1)
                    pe.matmul(ps_cb[:, 0:P], bT[:, ch], cT[:, ch], start=True, stop=True)
                    pe.transpose(ps_cb[:, P:2 * P], bT[:, ch], kept.ident[:]).then_inc(cb_done, 1)
                    if c:
                        y_turn(c - 1)
                    if b == 0:
                        begin(i)
                        pe.wait_ge(proj_read, g * (2 * NPROJ) + 2 * (i - 2) + 2)
                    part(i, b, 0, KT // 2)
                    if c:
                        pe.wait_ge(yT_made, g * TT + c)
                        pe.matmul(ps_yo[:], cT[:, ch], state[:].rearrange("p h d -> p (h d)"),
                                  start=True, stop=True).then_inc(yo_done, 1)
                    pe.wait_ge(g_made, g * TT + c + 1)
                    for h in range(GH):
                        mm = pe.matmul(ps_yd[:, h * HEAD_DIM:(h + 1) * HEAD_DIM], seg[:, c % 2, h, :], x_dt[:, h, :],
                                       start=True, stop=True)
                    mm.then_inc(yd_done, 1)
                    pe.wait_ge(bt_made, g * TT + c + 1)
                    if c < TT - 1:
                        pe.matmul(ps_x[:], b_tok[:], x_dec[:].rearrange("p h d -> p (h d)"),
                                  start=True, stop=True).then_inc(st_done, 1)
                    part(i, b, KT // 2, KT)
                y_turn(TT - 1)
                for n in range(NBR):
                    i = NPROJ + n // 2
                    if n % 2 == 0:
                        begin(i)
                    if n < 2:
                        pe.wait_ge(proj_read, g * (2 * NPROJ) + 2 * (NPROJ - 2 + n) + 2)
                    else:
                        pe.wait_ge(br_read, g * NBR + n - 1 + BR_CREDIT)
                    wh = w_hi[:, i % RAW].rearrange("p k n -> p (k n)").rearrange("p (k n) -> p k n", k=NX)
                    wl = w_lo[:, i % RAW].rearrange("p k n -> p (k n)").rearrange("p (k n) -> p k n", k=NX)
                    m = slice((n % 2) * P, (n % 2 + 1) * P)
                    for b in range(2):
                        half = slice(b * HALF, (b + 1) * HALF)
                        for k in range(NX):
                            pe.wait_ge(yl_made, g * NX + k + 1)
                            mm = product(pe, pair[n % 2][b][:], wh[:, k, m], wl[:, k, m], yh[:, k, half], yl[:, k, half],
                                         k == 0, k == NX - 1)
                        mm.then_inc(br_done, 1)
                    if n % 2:
                        pe.wait_ge(br_done, g * (2 * NBR) + 2 * n + 2)
                        pe.sem_inc(w_used, 1)



def phase_pool(nc, kept, a, dram, hT_hi, hT_lo):
    start = kept.end + 2 * KT * T * 4
    sb = Arena(nc, "p3", start)
    ypT_hi = sb("ypT_hi", [P, KT, T], F32R)
    ypT_lo = sb("ypT_lo", [P, KT, T], F32R)
    RAW = 2
    raw = sb("raw", [P, RAW, KT, P])
    w_hi = sb("w_hi", [P, RAW, KT, P], F32R)
    w_lo = sb("w_lo", [P, RAW, KT, P], F32R)
    sq_n = INNER
    at = sb.at
    xpad, win0, win1 = (sb(n, [P, PAD + T]) for n in ("xpad", "win0", "win1"))
    sb.at = at
    t_a, t_b, acc_n = (sb(n, [P, T]) for n in ("t_a", "t_b", "acc_n"))
    sb.at = at + 3 * (PAD + T) * 4
    inv_count = sb("inv_count", [P, PAD])
    edge = sb("edge", [P, PAD])
    at = u_at = sb.at
    u = sb("u", [P, KT, T])
    NDT = 4
    d_hi = sb("d_hi", [P, NDT, T], F32R, at=at)
    d_lo = sb("d_lo", [P, NDT, T], F32R, at=at + NDT * T * 4)
    rstd = kept.sq_acc

    PW = 2
    order = []
    for m in range(KT):
        order.append(("x", m))
        if m % PW == PW - 1 and m >= 2 * PW - 1:
            order.append(("w", m // PW - 1))
    order.append(("w", POOL_GROUPS - 1))
    NS = len(order)
    assert NS % RAW == 0
    pair_of, n_pairs = {}, 0
    for kind, m in order:
        for o in range(1 if kind == "x" else PW):
            pair_of[(kind, m, o)] = n_pairs
            n_pairs += 1
    assert n_pairs % 2 == 0

    with ExitStack() as ctx:
        sem = lambda n: nc.alloc_semaphore("p3_" + n)
        ps = lambda n: ctx.enter_context(nc.psum_tensor("p3_" + n, [P, HALF], F32))
        pair = [[ps("pair00"), ps("pair01")], [ps("pair10"), ps("pair11")]]
        ps_sq = [ps("sq0"), ps("sq1")]
        w_in = [sem(f"w_in{i}") for i in range(RAW)]
        acc_in = sem("acc_in")
        hi_made, lo_made, w_used = sem("hi_made"), sem("lo_made"), sem("w_used")
        pads, counts, iota_made, sq_summed, var_made, std_made = (sem(n) for n in ("pads", "counts", "iota_made", "sq_summed", "var_made", "std_made"))
        done, x_read, d_made, dh_made, dl_made, yh_made, yl_made = (sem(n) for n in
            ("done", "x_read", "d_made", "dh_made", "dl_made", "yh_made", "yl_made"))
        gb_done, gate_read, br_read, tb_used, u_made, seq, seq2 = (sem(n) for n in
            ("gb_done", "gate_read", "br_read", "tb_used", "u_made", "seq", "seq2"))
        blk = ctx.enter_context(nc.Block())
        W_CREDIT = RAW
        PASSES, NQ = KT // 2, 2
        NI = 3 * NQ
        GATE_CREDIT, BR_CREDIT, TB_CREDIT, U_CREDIT = 1, 1, 1, 1
        SEQ2 = 2 * NQ

        @blk.sync
        def _(sp):
            for n, (kind, m) in enumerate(order):
                sp.wait_ge(lo_made, n + 1)
                if kind == "x":
                    src, dst = a["w_in"][0, :, m * P:(m + 1) * P].rearrange("(k p) n -> p k n", p=P), raw[:, n % RAW]
                else:
                    src = a["pool_w"][0, m].rearrange("(k p) n -> p k n", p=P)
                    dst = raw[:, n % RAW, 0:2 * PW].rearrange("p k n -> p (k n)").rearrange("p (k n) -> p k n", k=PW)
                sp.dma_start(dst, src).then_inc(w_in[n % RAW], 16)
            for p in range(PASSES):
                for i in range(NI):
                    q, r = divmod(i, 3)
                    sp.wait_ge(lo_made, p * NI + NS + i + 1)
                    first = q * P + (COL_GATE + r * D if r < 2 else 0)
                    src = a["w_in" if r < 2 else "w_branch_pool"][0, :, p * (NQ * P) + first:p * (NQ * P) + first + P]
                    sp.dma_start(raw[:, i % RAW], src.rearrange("(k p) n -> p k n", p=P)).then_inc(w_in[i % RAW], 16)

        @blk.gpsimd
        def _(pool):
            pool.sem_inc(lo_made, W_CREDIT)
            pool.sem_inc(w_used, W_CREDIT)
            pool.sem_inc(gate_read, GATE_CREDIT)
            pool.sem_inc(br_read, BR_CREDIT)
            pool.sem_inc(tb_used, TB_CREDIT)
            pool.sem_inc(u_made, U_CREDIT)
            pool.memset(xpad[:, 0:PAD], 0.0).then_inc(pads, 1)
            pool.iota(inv_count[:], pattern=[[1, PAD]], base=1, channel_multiplier=0,
                      allow_small_or_imprecise_dtypes=True).then_inc(iota_made, 1)
            pool.wait_ge(yl_made, KT)
            with pool.Fori(0, PASSES) as p:
                for q in range(NQ):
                    pool.wait_ge(tb_used, p * NQ + q + TB_CREDIT)
                    pool.dma_start(acc_n[:], dram["acc"][:, bass.ds(p * NQ + q, 1), :]
                                   .rearrange("p k t -> p (k t)")).then_inc(acc_in, 16)

        @blk.scalar
        def _(act):
            def hi(n, base=0):
                slot = n % RAW
                act.wait_ge(w_in[slot], 16 * (base + n // RAW + 1))
                act.wait_ge(w_used, base * RAW + n + 1)
                act.activation(w_hi[:, slot], raw[:, slot], ACT.Copy).then_inc(hi_made, 1)

            hi(0)
            hi(1)
            act.wait_ge(var_made, 1)
            act.activation(rstd[:], rstd[:], ACT.Sqrt).then_inc(std_made, 1)
            for n, (kind, m) in enumerate(order):
                if kind == "x":
                    if m:
                        act.wait_ge(d_made, m)
                    k = pair_of[(kind, m, 0)]
                    for b in range(2):
                        act.wait_ge(done, 2 * k + b + 1)
                        act.activation(xpad[:, PAD + b * HALF:PAD + (b + 1) * HALF], pair[k % 2][b][:],
                                       ACT.Copy).then_inc(x_read, 1)
                else:
                    for o in range(PW):
                        k, t = pair_of[(kind, m, o)], m * PW + o
                        for b in range(2):
                            act.wait_ge(done, 2 * k + b + 1)
                            act.activation(ypT_hi[:, t, b * HALF:(b + 1) * HALF], pair[k % 2][b][:], ACT.Copy,
                                           scale=kept.cols_b[:, t:t + 1]).then_inc(yh_made, 1)
                if n + 2 < NS:
                    hi(n + 2)
                if kind == "x":
                    act.wait_ge(d_made, m + 1)
                    act.activation(d_hi[:, m % NDT, :], win1[:, 0:T], ACT.Copy).then_inc(dh_made, 1)
            with act.Fori(0, PASSES) as p:
                pass_base = p * (NI // RAW) + NS // RAW
                hi(0, pass_base)
                hi(1, pass_base)
                for i in range(NI):
                    q, r = divmod(i, 3)
                    if r < 2:
                        if r == 0:
                            act.wait_ge(u_made, p * NQ + q + U_CREDIT)
                        t = t_a if r == 0 else t_b
                        for b in range(2):
                            act.wait_ge(gb_done, p * (2 * NI) + 2 * i + b + 1)
                            ins = act.activation(t[:, b * HALF:(b + 1) * HALF], pair[i % 2][b][:], ACT.Tanh, scale=0.5)
                        ins.then_inc(gate_read, 1)
                    if i + 2 < NI:
                        hi(i + 2, pass_base)

        @blk.vector
        def _(dve):
            link = Chain(dve, seq)

            def lo(n, base=0):
                slot = n % RAW
                dve.wait_ge(hi_made, base * RAW + n + 1)
                dve.tensor_tensor(w_lo[:, slot], raw[:, slot], w_hi[:, slot].bitcast(F32),
                                  ALU.subtract).then_inc(lo_made, 1)

            lo(0)
            lo(1)
            dve.wait_ge(sq_summed, 1)
            for b in range(2):
                ins = dve.tensor_scalar(rstd[:, b * HALF:(b + 1) * HALF], ps_sq[b][:], 1.0 / INNER, EPS, ALU.mult, ALU.add)
            ins.then_inc(var_made, 1)
            dve.wait_ge(std_made, 1)
            link(dve.reciprocal(rstd[:], rstd[:]))
            dve.wait_ge(iota_made, 1)
            link(dve.reciprocal(inv_count[:], inv_count[:]))
            dve.wait_ge(pads, 1)
            for n, (kind, m) in enumerate(order):
                if kind == "x":
                    w = WINDOWS[m // PW]
                    dve.wait_ge(x_read, 2 * m + 2)
                    if m:
                        dve.wait_ge(dh_made, m)
                    src, dst, span, free = xpad, win0, 1, win1
                    while span < w:
                        link(dve.tensor_tensor(dst[:, 2 * span - 1:], src[:, 2 * span - 1:],
                                               src[:, span - 1:PAD + T - span], ALU.add))
                        src, dst, free = dst, free, dst
                        span *= 2
                    x_, s_ = xpad[:, PAD:], src[:, PAD:]
                    link(dve.tensor_tensor(edge[:, 0:w], s_[:, 0:w], inv_count[:, 0:w], ALU.mult))
                    out = win0 if src is win1 else win1
                    link(dve.scalar_tensor_tensor(out[:, 0:T], s_, 1.0 / w, x_, ALU.mult, ALU.subtract))
                    ins = dve.tensor_tensor(out[:, 0:w], edge[:, 0:w], x_[:, 0:w], ALU.subtract)
                    if out is win0:
                        link(ins)
                        ins = dve.tensor_copy(win1[:, 0:T], win0[:, 0:T])
                    ins.then_inc(d_made, 1)
                if n + 2 < NS:
                    lo(n + 2)
                if kind == "x":
                    dve.wait_ge(dh_made, m + 1)
                    dve.tensor_tensor(d_lo[:, m % NDT, :], win1[:, 0:T], d_hi[:, m % NDT, :].bitcast(F32),
                                      ALU.subtract).then_inc(dl_made, 1)
                else:
                    for o in range(PW):
                        k, t = pair_of[(kind, m, o)], m * PW + o
                        dve.wait_ge(yh_made, 2 * t + 2)
                        for b in range(2):
                            half = slice(b * HALF, (b + 1) * HALF)
                            ins = dve.scalar_tensor_tensor(ypT_lo[:, t, half], pair[k % 2][b][:], kept.cols_b[:, t:t + 1],
                                                           ypT_hi[:, t, half].bitcast(F32), ALU.mult, ALU.subtract)
                        ins.then_inc(yl_made, 1)
            with dve.Fori(0, PASSES) as p:
                link = Chain(dve, seq2, p * SEQ2, SEQ2)
                pass_base = p * (NI // RAW) + NS // RAW
                lo(0, pass_base)
                lo(1, pass_base)
                for i in range(NI):
                    q, r = divmod(i, 3)
                    if i + 2 < NI:
                        lo(i + 2, pass_base)
                    if r == 1:
                        dve.wait_ge(acc_in, 16 * (p * NQ + q + 1))
                        dve.wait_ge(gate_read, p * (2 * NQ) + 2 * q + 2 + GATE_CREDIT)
                        link(dve.scalar_tensor_tensor(t_b[:], t_b[:], 1.0, acc_n[:], ALU.add, ALU.mult))
                        dve.sem_inc(tb_used, 1)
                        link(dve.tensor_tensor(t_b[:], t_b[:], rstd[:], ALU.mult))
                    if r == 2:
                        for b in range(2):
                            half = slice(b * HALF, (b + 1) * HALF)
                            dve.wait_ge(gb_done, p * (2 * NI) + 2 * i + b + 1)
                            ins = dve.scalar_tensor_tensor(t_a[:, half], t_a[:, half], 1.0, pair[i % 2][b][:], ALU.add, ALU.mult)
                        ins.then_inc(br_read, 1)
                        dve.wait_ge(br_read, p * NQ + q + 1 + BR_CREDIT)
                        dve.tensor_tensor(u[:, bass.ds(p * NQ + q, 1), :], t_a[:].unsqueeze(1), t_b[:].unsqueeze(1),
                                          ALU.add).then_inc(u_made, 1)
                link.done()

        @blk.tensor
        def _(pe):
            for b in range(2):
                mm = pe.matmul(ps_sq[b][:], kept.ones[:], kept.sq_acc[:, b * HALF:(b + 1) * HALF], start=True, stop=True)
            mm.then_inc(sq_summed, 1)
            taken = []
            for n, (kind, m) in enumerate(order):
                pe.wait_ge(hi_made, n + 1)
                pe.wait_ge(lo_made, n + 1 + W_CREDIT)
                for o in range(1 if kind == "x" else PW):
                    k = pair_of[(kind, m, o)]
                    if k >= 2:
                        was, wm, wo = taken[k - 2]
                        if was == "x":
                            pe.wait_ge(x_read, 2 * wm + 2)
                        else:
                            pe.wait_ge(yl_made, wm * PW + wo + 1)
                    taken.append((kind, m, o))
                    for b in range(2):
                        half = slice(b * HALF, (b + 1) * HALF)
                        if kind == "x":
                            for kk in range(KT):
                                mm = product(pe, pair[k % 2][b][:], w_hi[:, n % RAW, kk, :], w_lo[:, n % RAW, kk, :],
                                             hT_hi[:, kk, half], hT_lo[:, kk, half], kk == 0, kk == KT - 1)
                        else:
                            pe.wait_ge(dl_made, m * PW + PW)
                            wh = w_hi[:, n % RAW, 0:2 * PW].rearrange("p k n -> p (k n)").rearrange("p (k n) -> p k n", k=PW)
                            wl = w_lo[:, n % RAW, 0:2 * PW].rearrange("p k n -> p (k n)").rearrange("p (k n) -> p k n", k=PW)
                            for kk in range(PW):
                                t = (m * PW + kk) % NDT
                                mm = product(pe, pair[k % 2][b][:], wh[:, kk, o * P:(o + 1) * P], wl[:, kk, o * P:(o + 1) * P],
                                             d_hi[:, t, half], d_lo[:, t, half], kk == 0, kk == PW - 1)
                        mm.then_inc(done, 1)
                pe.wait_ge(done, 2 * k + 2)
                pe.sem_inc(w_used, 1)
            pe.wait_ge(yl_made, KT)
            with pe.Fori(0, PASSES) as p:
                for i in range(NI):
                    q, r = divmod(i, 3)
                    pe.wait_ge(hi_made, p * NI + NS + i + 1)
                    pe.wait_ge(lo_made, p * NI + NS + i + 1 + W_CREDIT)
                    if i == 0:
                        pe.wait_ge(gate_read, p * (2 * NQ) + GATE_CREDIT)
                    elif i == 1:
                        pe.wait_ge(br_read, p * NQ + BR_CREDIT)
                    elif (i - 2) % 3 == 2:
                        pe.wait_ge(br_read, p * NQ + (i - 2) // 3 + 1 + BR_CREDIT)
                    else:
                        pe.wait_ge(gate_read, p * (2 * NQ) + (i - 2) // 3 * 2 + (i - 2) % 3 + 1 + GATE_CREDIT)
                    for b in range(2):
                        half = slice(b * HALF, (b + 1) * HALF)
                        rhs_hi, rhs_lo = (hT_hi, hT_lo) if r < 2 else (ypT_hi, ypT_lo)
                        for kk in range(KT):
                            mm = product(pe, pair[i % 2][b][:], w_hi[:, i % RAW, kk, :], w_lo[:, i % RAW, kk, :],
                                         rhs_hi[:, kk, half], rhs_lo[:, kk, half], kk == 0, kk == KT - 1)
                        mm.then_inc(gb_done, 1)
                    pe.wait_ge(gb_done, p * (2 * NI) + 2 * i + 2)
                    pe.sem_inc(w_used, 1)
    return u, u_at



def phase_mix(nc, kept, a, dram, u, u_at):
    fixed = kept.end
    sb = Arena(nc, "p4", fixed)
    u_hi = sb("u_hi", [P, KT, T], F32R)
    u_lo = sb("u_lo", [P, KT, T], F32R)
    w_hi = sb("w_hi", [P, KT, D], F32R)
    w_lo = sb("w_lo", [P, KT, D], F32R)
    RAW = 2
    raw = sb("raw", [P, RAW, D])
    g1, gs2, sh2 = (sb(n, [P, D]) for n in ("g1", "gs2", "sh2"))
    x = sb("x", [P, D])
    h2 = sb("h2", [P, 2, D])
    h2T = sb("h2T", [P, KT, P])
    assert sb.at <= u_at
    x1 = sb("x1", [P, TT, D], at=u_at)
    sb.at = u_at + TT * D * 4
    NR = MG + NE
    rw = sb("rw", [P, KT, NR])
    rb = sb("rb", [P, NR])
    ss, var, std, rstd = (sb(n, [P, TT]) for n in ("ss", "var", "std", "rstd"))
    with ExitStack() as ctx:
        sem = lambda n: nc.alloc_semaphore("p4_" + n)
        ps = lambda n: ctx.enter_context(nc.psum_tensor("p4_" + n, [P, HALF], F32))
        pair = [[ps("pair00"), ps("pair01")], [ps("pair10"), ps("pair11")]]
        ps_t = [ps("t0"), ps("t1")]
        ps_r = ps("r")
        w_in = [sem(f"w_in{i}") for i in range(RAW)]
        par_in, x_in, hi_made, lo_made, uh_made, ul_made, sc_made = (sem(n) for n in
            ("par_in", "x_in", "hi_made", "lo_made", "uh_made", "ul_made", "sc_made"))
        done, x1_made, squared, var_made, std_made, h2_made, turned, h2T_made, routed = (sem(n) for n in
            ("done", "x1_made", "squared", "var_made", "std_made", "h2_made", "turned", "h2T_made", "routed"))
        h2_out = [sem(f"h2_out{i}") for i in range(2)]
        seq = sem("seq")
        blk = ctx.enter_context(nc.Block())

        @blk.sync
        def _(sp):
            for k in range(KT):
                if k >= RAW:
                    sp.wait_ge(lo_made, k - RAW + 1)
                sp.dma_start(raw[:, k % RAW], a["w_out"][0, k * P:(k + 1) * P, :]).then_inc(w_in[k % RAW], 16)
            for i in range(TT):
                if i:
                    sp.wait_ge(x1_made, i)
                sp.dma_start(x[:], a["x"][0, i * P:(i + 1) * P, :]).then_inc(x_in, 16)

        @blk.gpsimd
        def _(pool):
            mod = dram["mod"]
            pool.dma_start(g1[:], mod[0, 0:D].partition_broadcast(P)).then_inc(par_in, 16)
            pool.dma_start(sh2[:], mod[0, D:2 * D].partition_broadcast(P)).then_inc(par_in, 16)
            pool.dma_start(gs2[:], mod[0, 2 * D:3 * D].partition_broadcast(P)).then_inc(par_in, 16)
            pool.dma_start(h2[:, 0], a["norm2_g"][0].partition_broadcast(P)).then_inc(par_in, 16)
            pool.dma_start(rw[:, :, 0:MG], a["router_group_w"][0].rearrange("(k p) n -> p k n", p=P)).then_inc(par_in, 16)
            pool.dma_start(rw[:, :, MG:], a["router_expert_w"][0].rearrange("(k p) n -> p k n", p=P)).then_inc(par_in, 16)
            pool.dma_start(rb[:, 0:MG], a["router_group_b"][0].partition_broadcast(P)).then_inc(par_in, 16)
            pool.dma_start(rb[:, MG:], a["router_expert_b"][0].partition_broadcast(P)).then_inc(par_in, 16)
            for k in range(KT):
                pool.wait_ge(hi_made, k + 1)
                pool.tensor_tensor(w_lo[:, k], raw[:, k % RAW], w_hi[:, k].bitcast(F32), ALU.subtract).then_inc(lo_made, 1)
            for i in range(TT):
                pool.wait_ge(h2_made, i + 1)
                pool.dma_start(dram["h2"][i * P:(i + 1) * P, :], h2[:, i % 2]).then_inc(h2_out[i % 2], 16)
            for i in range(2):
                pool.wait_ge(h2_out[i], 16 * TT // 2)

        @blk.scalar
        def _(act):
            for k in range(KT):
                act.activation(u_hi[:, k], u[:, k], ACT.Copy, scale=0.5).then_inc(uh_made, 1)
                act.wait_ge(w_in[k % RAW], 16 * (k // RAW + 1))
                act.activation(w_hi[:, k], raw[:, k % RAW], ACT.Copy).then_inc(hi_made, 1)
            for i in range(TT):
                act.wait_ge(x1_made, i + 1)
                act.activation(h2[:, i % 2], x1[:, i], ACT.Square, accum_out=ss[:, i:i + 1]).then_inc(squared, 1)
                act.wait_ge(var_made, i + 1)
                act.activation(std[:, i:i + 1], var[:, i:i + 1], ACT.Sqrt).then_inc(std_made, 1)
                if i >= 1:
                    for b in range(2):
                        act.wait_ge(turned, 2 * (i - 1) + b + 1)
                        if b == 0 and i >= 2:
                            act.wait_ge(routed, i - 1)
                        act.activation(h2T[:, 4 * b:4 * b + 4], ps_t[b][:].rearrange("p (k t) -> p k t", t=P),
                                       ACT.Copy).then_inc(h2T_made, 1)
            for b in range(2):
                act.wait_ge(turned, 2 * (TT - 1) + b + 1)
                if b == 0:
                    act.wait_ge(routed, TT - 1)
                act.activation(h2T[:, 4 * b:4 * b + 4], ps_t[b][:].rearrange("p (k t) -> p k t", t=P),
                               ACT.Copy).then_inc(h2T_made, 1)

        @blk.vector
        def _(dve):
            link = Chain(dve, seq)
            for k in range(KT):
                dve.wait_ge(uh_made, k + 1)
                dve.scalar_tensor_tensor(u_lo[:, k], u[:, k], 0.5, u_hi[:, k].bitcast(F32),
                                         ALU.mult, ALU.subtract).then_inc(ul_made, 1)
            dve.wait_ge(par_in, 16 * 8)
            link(dve.scalar_tensor_tensor(gs2[:], gs2[:], 1.0, h2[:, 0], ALU.add, ALU.mult))
            for i in range(TT):
                if i >= 2:
                    dve.wait_ge(h2_out[i % 2], 16 * (i // 2))
                    dve.wait_ge(turned, 2 * (i - 2) + 2)
                for b in range(2):
                    half = slice(b * HALF, (b + 1) * HALF)
                    dve.wait_ge(done, 2 * i + b + 1)
                    link(dve.tensor_tensor(h2[:, i % 2, half], pair[i % 2][b][:], g1[:, half], ALU.mult))
                dve.wait_ge(x_in, 16 * (i + 1))
                dve.tensor_tensor(x1[:, i], h2[:, i % 2], x[:], ALU.add).then_inc(x1_made, 1)
                dve.wait_ge(squared, i + 1)
                dve.tensor_scalar(var[:, i:i + 1], ss[:, i:i + 1], 1.0 / D, EPS, ALU.mult, ALU.add).then_inc(var_made, 1)
                dve.wait_ge(std_made, i + 1)
                link(dve.reciprocal(rstd[:, i:i + 1], std[:, i:i + 1]))
                link(dve.scalar_tensor_tensor(h2[:, i % 2], x1[:, i], rstd[:, i:i + 1], gs2[:], ALU.mult, ALU.mult))
                dve.tensor_tensor(h2[:, i % 2], h2[:, i % 2], sh2[:], ALU.add).then_inc(h2_made, 1)
            dve.wait_ge(routed, TT)
            dve.tensor_tensor(kept.logits[:], ps_r[:, 0:TT * NR].rearrange("p (t n) -> p t n", n=NR),
                              bc(rb[:].unsqueeze(1), [P, TT, NR]), ALU.add)

        @blk.tensor
        def _(pe):
            def turn(i):
                pe.wait_ge(h2_made, i + 1)
                if i:
                    pe.wait_ge(h2T_made, 2 * i)
                for k in range(KT):
                    mm = pe.transpose(ps_t[k // 4][:, (k % 4) * P:(k % 4 + 1) * P], h2[:, i % 2, k * P:(k + 1) * P],
                                      kept.ident[:])
                    if k % 4 == 3:
                        mm.then_inc(turned, 1)

            def route(i):
                pe.wait_ge(h2T_made, 2 * i + 2)
                for k in range(KT):
                    mm = pe.matmul(ps_r[:, i * NR:(i + 1) * NR], h2T[:, k, :], rw[:, k, :],
                                   start=(k == 0), stop=(k == KT - 1))
                mm.then_inc(routed, 1)

            pe.wait_ge(ul_made, KT)
            pe.wait_ge(lo_made, KT)
            pe.wait_ge(par_in, 16 * 8)
            for i in range(TT):
                if i >= 2:
                    pe.wait_ge(x1_made, i - 1)
                rows = slice(i * P, (i + 1) * P)
                for b in range(2):
                    half = slice(b * HALF, (b + 1) * HALF)
                    for k in range(KT):
                        mm = product(pe, pair[i % 2][b][:], u_hi[:, k, rows], u_lo[:, k, rows],
                                     w_hi[:, k, half], w_lo[:, k, half], k == 0, k == KT - 1)
                    mm.then_inc(done, 1)
                if i >= 1:
                    turn(i - 1)
                if i >= 2:
                    route(i - 2)
            route(TT - 2)
            turn(TT - 1)
            route(TT - 1)
    return x1


def phase_route(nc, kept, a, dram):
    sb = Arena(nc, "p5", kept.end)
    E3 = [P, TT, NE]
    G3 = [P, TT, MG]
    X3 = [P, TT, EPG]
    rev = sb("rev", [P, 1, EPG])
    gmax, gsum, gw = (sb(n, [P, TT, 1]) for n in ("gmax", "gsum", "gw"))
    glog, gexp, gone = (sb(n, G3) for n in ("glog", "gexp", "gone"))
    e_in, e_two, prod, one0, one1 = (sb(n, X3) for n in ("e_in", "e_two", "prod", "one0", "one1"))
    m0, m1, first, ratio = (sb(n, [P, TT, 1]) for n in ("m0", "m1", "first", "ratio"))
    hot = [sb(f"hot{k}", E3) for k in range(2)]
    both = sb("both", E3, BF16)
    where, slot_f = sb("where", E3), sb("slot_f", [P, TT])
    base = sb("base", [P, NE])
    count_f, count_i, blocks_f = sb("count_f", [NE, 1]), sb("count_i", [NE, 1], I32), sb("blocks_f", [NE, 1])
    blocks_bf = sb("blocks_bf", [NE, P], BF16)
    ends, block_no, past = sb("ends", [NE, 1]), sb("block_no", [NE, MAX_BLOCKS + 1]), sb("past", [NE, MAX_BLOCKS + 1])
    h2 = sb("h2", [P, TT, D])
    logits = kept.logits
    with ExitStack() as ctx:
        sem = lambda n: nc.alloc_semaphore("p5_" + n)
        ps = lambda n: ctx.enter_context(nc.psum_tensor("p5_" + n, [P, HALF], F32))
        ps_pos, ps_cnt, ps_base = ps("pos"), ps("cnt"), ps("base")
        h2_in = [sem(f"h2_in{i}") for i in range(TT)]
        iotas, seq, top_made, gexp_made, ratio_in, ratio_made = (sem(n) for n in
            ("iotas", "seq", "top_made", "gexp_made", "ratio_in", "ratio_made"))
        both_made, counted, placed, blocks_made, based, past_made, tabled, slots_made, scattered = (sem(n) for n in
            ("both_made", "counted", "placed", "blocks_made", "based", "past_made", "tabled", "slots_made", "scattered"))
        blk = ctx.enter_context(nc.Block())

        @blk.sync
        def _(sp):
            for i in range(TT):
                sp.dma_start(h2[:, i], dram["h2"][i * P:(i + 1) * P, :]).then_inc(h2_in[i], 16)

        @blk.gpsimd
        def _(pool):
            pool.iota(rev[:], pattern=[[-1, EPG]], base=EPG, channel_multiplier=0,
                      allow_small_or_imprecise_dtypes=True).then_inc(iotas, 1)
            pool.iota(block_no[:], pattern=[[1, MAX_BLOCKS + 1]], base=0, channel_multiplier=0,
                      allow_small_or_imprecise_dtypes=True).then_inc(iotas, 1)
            pool.wait_ge(slots_made, 2)
            for i in range(TT):
                pool.wait_ge(h2_in[i], 16)
                for k in range(2):
                    pool.indirect_dma_start(out=dram["x_buf"], out_offset=bass.IndirectOffsetOnAxis(ap=kept.slot[k][:, i:i + 1], axis=0),
                                            in_=h2[:, i], in_offset=None).then_inc(scattered, 16)
            pool.wait_ge(scattered, 16 * 2 * TT)

        @blk.scalar
        def _(act):
            act.wait_ge(top_made, 1)
            act.activation(gexp[:], glog[:], ACT.Exp).then_inc(gexp_made, 1)
            act.wait_ge(ratio_in, 1)
            act.activation(ratio[:], m1[:], ACT.Exp).then_inc(ratio_made, 1)

        @blk.vector
        def _(dve):
            link = Chain(dve, seq)
            TE = [P, TT, EPG]

            def first_hot(out, values, top, n):
                link(dve.tensor_reduce(top[:], values, AX.X, ALU.max))
                link(dve.tensor_tensor(out, values, bc(top[:], [P, TT, n]), ALU.is_equal))
                link(dve.tensor_tensor(out, out, bc(rev[:, :, 0:n], [P, TT, n]), ALU.mult))
                link(dve.tensor_reduce(first[:], out, AX.X, ALU.max))
                link(dve.tensor_tensor(out, out, bc(first[:], [P, TT, n]), ALU.is_equal))

            dve.wait_ge(iotas, 2)
            lg = logits[:, :, 0:MG]
            first_hot(gone[:], lg, gmax, MG)
            dve.tensor_tensor(glog[:], lg, bc(gmax[:], G3), ALU.subtract).then_inc(top_made, 1)
            for g in range(MG):
                le = logits[:, :, MG + g * EPG:MG + (g + 1) * EPG]
                out = e_in if g == 0 else prod
                link(dve.tensor_tensor(out[:], le, bc(gone[:, :, g:g + 1], TE), ALU.mult))
                if g:
                    link(dve.tensor_tensor(e_in[:], e_in[:], prod[:], ALU.add))
            first_hot(one0[:], e_in[:], m0, EPG)
            link(dve.scalar_tensor_tensor(e_two[:], one0[:], NEG, e_in[:], ALU.mult, ALU.add))
            first_hot(one1[:], e_two[:], m1, EPG)
            dve.tensor_tensor(m1[:], m1[:], m0[:], ALU.subtract).then_inc(ratio_in, 1)
            for k, one in enumerate((one0, one1)):
                for g in range(MG):
                    ins = dve.tensor_tensor(hot[k][:, :, g * EPG:(g + 1) * EPG], one[:], bc(gone[:, :, g:g + 1], TE), ALU.mult)
            link(ins)
            dve.tensor_tensor(both[:], hot[0][:], hot[1][:], ALU.add).then_inc(both_made, 1)
            dve.wait_ge(gexp_made, 1)
            link(dve.tensor_reduce(gsum[:], gexp[:], AX.X, ALU.add))
            dve.wait_ge(ratio_made, 1)
            link(dve.scalar_tensor_tensor(gw[:], ratio[:], 1.0, gsum[:], ALU.add, ALU.mult))
            link(dve.reciprocal(kept.weight[0][:], gw[:].rearrange("p t o -> p (t o)")))
            link(dve.tensor_tensor(kept.weight[1][:], ratio[:].rearrange("p t o -> p (t o)"), kept.weight[0][:], ALU.mult))
            dve.wait_ge(counted, 1)
            link(dve.tensor_scalar(count_f[:], ps_cnt[0:NE, 0:1], float(BLOCK - 1), None, ALU.add))
            link(dve.tensor_copy(count_i[:], count_f[:]))
            link(dve.tensor_scalar(count_i[:], count_i[:], BLOCK.bit_length() - 1, None, ALU.arith_shift_right))
            link(dve.tensor_copy(blocks_f[:], count_i[:]))
            dve.tensor_copy(blocks_bf[:], bc(blocks_f[:], [NE, P])).then_inc(blocks_made, 1)
            dve.wait_ge(based, 1)
            link(dve.tensor_copy(base[:], ps_base[:, 0:NE]))
            link(dve.tensor_copy(ends[:], ps_base[0:NE, NE:NE + 1]))
            dve.tensor_scalar(past[:], block_no[:], ends[:], None, ALU.is_ge).then_inc(past_made, 1)
            dve.wait_ge(placed, 1)
            link(dve.scalar_tensor_tensor(where[:], bc(base[:].unsqueeze(1), E3), float(BLOCK),
                                          ps_pos[:, 0:TT * NE].rearrange("p (t n) -> p t n", n=NE), ALU.mult, ALU.add))
            for k in range(2):
                link(dve.tensor_tensor(hot[k][:], hot[k][:], where[:], ALU.mult))
                link(dve.tensor_reduce(slot_f[:], hot[k][:], AX.X, ALU.add))
                dve.tensor_copy(kept.slot[k][:], slot_f[:]).then_inc(slots_made, 1)
                dve.wait_ge(slots_made, k + 1)
            dve.wait_ge(tabled, 1)
            dve.tensor_scalar(kept.table[0:1, 0:MAX_BLOCKS + 1], ps_cnt[0:1, 64:64 + MAX_BLOCKS + 1], float(NE - 1), None, ALU.min)
            dve.tensor_copy(kept.table[0:1, MAX_BLOCKS + 1:MAX_BLOCKS + 2], ps_cnt[0:1, 192:193])

        @blk.tensor
        def _(pe):
            pe.wait_ge(both_made, 1)
            for i in range(TT):
                mm = pe.matmul(ps_cnt[0:NE, 0:1], both[:, i, :], kept.ones_bf[:, 0:1], start=(i == 0), stop=(i == TT - 1))
            mm.then_inc(counted, 1)
            for i in range(TT):
                out = ps_pos[:, i * NE:(i + 1) * NE]
                for j in range(i):
                    pe.matmul(out, kept.ones_bf[:], both[:, j, :], start=(j == 0), stop=False)
                mm = pe.matmul(out, kept.tri_strict[:], both[:, i, :], start=(i == 0), stop=True)
            mm.then_inc(placed, 1)
            pe.wait_ge(blocks_made, 1)
            pe.matmul(ps_base[:, 0:NE], blocks_bf[:], kept.tri_strict[0:NE, 0:NE], start=True, stop=True)
            pe.matmul(ps_base[0:NE, NE:NE + 1], kept.tri[0:NE, 0:NE], blocks_f[:], start=True, stop=True).then_inc(based, 1)
            pe.wait_ge(past_made, 1)
            pe.matmul(ps_cnt[0:1, 64:64 + MAX_BLOCKS + 1], kept.ones[0:NE, 0:1], past[:], start=True, stop=True)
            pe.matmul(ps_cnt[0:1, 192:193], blocks_f[:], kept.ones[0:NE, 0:1], start=True, stop=True).then_inc(tabled, 1)


def phase_experts(nc, kept, a, dram):
    sb = Arena(nc, "p6", kept.end)
    FT = FF // P
    NP = KT + FT
    NS = 4
    AHEAD = NS
    raw = sb("raw", [P, NP, D])
    w_hi = sb("w_hi", [P, NS, D], F32R)
    w_lo = sb("w_lo", [P, NS, D], F32R)
    xb = sb("xb", [P, D])
    xT_hi = sb("xT_hi", [P, KT, P], F32R)
    xT_lo = sb("xT_lo", [P, KT, P], F32R)
    th = sb("th", [P, FF])
    s = sb("s", [P, FF])
    sT_hi = sb("sT_hi", [P, FT, P], F32R)
    sT_lo = sb("sT_lo", [P, FT, P], F32R)
    yb = sb("yb", [P, D])
    g2 = sb("g2", [P, D])
    with ExitStack() as ctx:
        sem = lambda n: nc.alloc_semaphore("p6_" + n)
        ps = lambda n: ctx.enter_context(nc.psum_tensor("p6_" + n, [P, HALF], F32))
        ps_a, ps_g, ps_s = ps("a"), ps("g"), ps("s")
        ps_x = [ps("x0"), ps("x1")]
        ps_y = [ps("y0"), ps("y1")]
        w_in = [sem(f"w_in{i}") for i in range(NP)]
        x_in, y_out, g2_in = sem("x_in"), sem("y_out"), sem("g2_in")
        hi_made, lo_made, used, x_turned, xh_made, xl_made, up_done, th_made, t_made, s_made = (sem(n) for n in
            ("hi_made", "lo_made", "used", "x_turned", "xh_made", "xl_made", "up_done", "th_made", "t_made", "s_made"))
        s_turned, sh_made, sl_made, y_done, y_read, y_scaled, y_free = (sem(n) for n in
            ("s_turned", "sh_made", "sl_made", "y_done", "y_read", "y_scaled", "y_free"))
        blk = ctx.enter_context(nc.Block())
        LO_CREDIT, USED_CREDIT, Y_CREDIT = NP, NS, 1

        def blocks(eng):
            return eng.value_load(kept.table[0:1, MAX_BLOCKS + 1:MAX_BLOCKS + 2], min_val=1, max_val=MAX_BLOCKS)

        @blk.sync
        def _(sp):
            nb = blocks(sp)

            def expert(j):
                return sp.value_load(kept.table[0:1, bass.ds(j, 1)], min_val=0, max_val=NE - 1)

            def load(e, j, q):
                src = a["w13"][0, bass.ds(e, 1), q * P:(q + 1) * P, :] if q < KT else \
                    a["w2"][0, bass.ds(e, 1), (q - KT) * P:(q - KT + 1) * P, :]
                sp.wait_ge(lo_made, j * NP + q + 1)
                sp.dma_start(raw[:, q], src.rearrange("e p n -> p (e n)")).then_inc(w_in[q], 16)

            e = expert(0)
            for q in range(AHEAD):
                load(e, 0, q)
            with sp.Fori(0, nb) as j:
                e = expert(j)
                for q in range(AHEAD, NP):
                    load(e, j, q)
                e = expert(j + 1)
                for q in range(AHEAD):
                    load(e, j + 1, q)

        @blk.gpsimd
        def _(pool):
            pool.dma_start(g2[:], dram["mod"][0, 3 * D:4 * D].partition_broadcast(P)).then_inc(g2_in, 16)
            pool.sem_inc(lo_made, LO_CREDIT)
            pool.sem_inc(used, USED_CREDIT)
            pool.sem_inc(y_free, Y_CREDIT)
            nb = blocks(pool)
            x_rows = dram["x_buf"].rearrange("(b p) d -> p b d", p=P)
            y_rows = x_rows
            pool.dma_start(xb[:], x_rows[:, 0, :]).then_inc(x_in, 16)
            pool.wait_ge(g2_in, 16)
            with pool.Fori(0, nb) as j:
                pool.wait_ge(x_turned, 2 * j + 2)
                pool.dma_start(xb[:].unsqueeze(1), x_rows[:, bass.ds(j + 1, 1), :]).then_inc(x_in, 16)
                pool.wait_ge(y_read, 2 * j + 2)
                pool.tensor_tensor(yb[:], yb[:], g2[:], ALU.mult).then_inc(y_scaled, 1)
                pool.wait_ge(y_scaled, j + 1)
                pool.dma_start(y_rows[:, bass.ds(j, 1), :], yb[:].unsqueeze(1)).then_inc(y_out, 16)
                pool.wait_ge(y_out, j * 16 + 16)
                pool.sem_inc(y_free, 1)
            pool.wait_ge(x_in, nb * 16 + 16)

        @blk.scalar
        def _(act):
            nb = blocks(act)

            def hi(j, q):
                act.wait_ge(w_in[q], j * 16 + 16)
                act.wait_ge(used, j * NP + q + 1)
                act.activation(w_hi[:, q % NS], raw[:, q], ACT.Copy).then_inc(hi_made, 1)

            def x_hi(j):
                for b in range(2):
                    act.wait_ge(x_turned, 2 * j + b + 1)
                    act.activation(xT_hi[:, 4 * b:4 * b + 4], ps_x[b][:].rearrange("p (k t) -> p k t", t=P),
                                   ACT.Copy).then_inc(xh_made, 1)

            x_hi(0)
            for q in range(AHEAD):
                hi(0, q)
            with act.Fori(0, nb) as j:
                for q in range(AHEAD, NP - 1):
                    hi(j, q)
                act.wait_ge(up_done, j + 1)
                act.activation(th[:], ps_a[:], ACT.Tanh, scale=0.5).then_inc(th_made, 1)
                x_hi(j + 1)
                act.wait_ge(s_turned, j + 1)
                act.activation(sT_hi[:], ps_s[:].rearrange("p (k t) -> p k t", t=P), ACT.Copy).then_inc(sh_made, 1)
                hi(j, NP - 1)
                for q in range(AHEAD):
                    hi(j + 1, q)
                act.wait_ge(y_done, 2 * j + 1)
                act.wait_ge(y_free, j + 1)
                act.activation(yb[:, 0:HALF], ps_y[0][:], ACT.Copy).then_inc(y_read, 1)
                act.wait_ge(y_done, 2 * j + 2)
                act.activation(yb[:, HALF:], ps_y[1][:], ACT.Copy).then_inc(y_read, 1)

        @blk.vector
        def _(dve):
            nb = blocks(dve)

            def lo(j, q):
                dve.wait_ge(hi_made, j * NP + q + 1)
                dve.tensor_tensor(w_lo[:, q % NS], raw[:, q], w_hi[:, q % NS].bitcast(F32),
                                  ALU.subtract).then_inc(lo_made, 1)

            def x_lo(j):
                for b in range(2):
                    dve.wait_ge(xh_made, 2 * j + b + 1)
                    ks = slice(4 * b, 4 * b + 4)
                    dve.tensor_tensor(xT_lo[:, ks], ps_x[b][:].rearrange("p (k t) -> p k t", t=P),
                                      xT_hi[:, ks].bitcast(F32), ALU.subtract).then_inc(xl_made, 1)

            x_lo(0)
            for q in range(AHEAD):
                lo(0, q)
            with dve.Fori(0, nb) as j:
                for q in range(AHEAD, NP - 1):
                    lo(j, q)
                dve.wait_ge(th_made, j + 1)
                dve.scalar_tensor_tensor(th[:], th[:], 1.0, ps_a[:], ALU.add, ALU.mult).then_inc(t_made, 1)
                dve.wait_ge(t_made, j + 1)
                dve.scalar_tensor_tensor(s[:], th[:], 0.5, ps_g[:], ALU.mult, ALU.mult).then_inc(s_made, 1)
                x_lo(j + 1)
                dve.wait_ge(sh_made, j + 1)
                dve.tensor_tensor(sT_lo[:], ps_s[:].rearrange("p (k t) -> p k t", t=P), sT_hi[:].bitcast(F32),
                                  ALU.subtract).then_inc(sl_made, 1)
                lo(j, NP - 1)
                for q in range(AHEAD):
                    lo(j + 1, q)

        @blk.tensor
        def _(pe):
            nb = blocks(pe)

            def turn_x(j):
                pe.wait_ge(x_in, j * 16 + 16)
                for k in range(KT):
                    mm = pe.transpose(ps_x[k // 4][:, (k % 4) * P:(k % 4 + 1) * P], xb[:, k * P:(k + 1) * P], kept.ident[:])
                    if k % 4 == 3:
                        mm.then_inc(x_turned, 1)

            turn_x(0)
            with pe.Fori(0, nb) as j:
                for q in range(KT):
                    if q % 4 == 0:
                        pe.wait_ge(xl_made, j * 2 + q // 4 + 1)
                    pe.wait_ge(lo_made, j * NP + q + 1 + LO_CREDIT)
                    for b, out in enumerate((ps_a, ps_g)):
                        half = slice(b * HALF, (b + 1) * HALF)
                        mm = product(pe, out[:], xT_hi[:, q], xT_lo[:, q], w_hi[:, q % NS, half], w_lo[:, q % NS, half],
                                     q == 0, q == KT - 1)
                    mm.then_inc(used, 1)
                pe.wait_ge(used, j * NP + KT + USED_CREDIT)
                pe.sem_inc(up_done, 1)
                turn_x(j + 1)
                pe.wait_ge(s_made, j + 1)
                for k in range(FT):
                    mm = pe.transpose(ps_s[:, k * P:(k + 1) * P], s[:, k * P:(k + 1) * P], kept.ident[:])
                mm.then_inc(s_turned, 1)
                pe.wait_ge(sl_made, j + 1)
                for q in range(KT, NP):
                    pe.wait_ge(lo_made, j * NP + q + 1 + LO_CREDIT)
                    for b in range(2):
                        half = slice(b * HALF, (b + 1) * HALF)
                        mm = product(pe, ps_y[b][:], sT_hi[:, q - KT], sT_lo[:, q - KT],
                                     w_hi[:, q % NS, half], w_lo[:, q % NS, half], q == KT, q == NP - 1)
                        if q == NP - 1:
                            mm.then_inc(y_done, 1)
                    if q < NP - 1:
                        mm.then_inc(used, 1)
                pe.wait_ge(y_done, 2 * j + 2)
                pe.sem_inc(used, 1)


def phase_combine(nc, kept, a, dram, x1, out):
    sb = Arena(nc, "p7", kept.end)
    R = 3
    y0, y1 = sb("y0", [P, R, D]), sb("y1", [P, R, D])
    sq = sb("sq", [P, 2, D])
    gf = sb("gf", [P, D])
    res = sb("res", [P, 2, D])
    ss, var, std, rstd = (sb(n, [P, TT]) for n in ("ss", "var", "std", "rstd"))
    with ExitStack() as ctx:
        sem = lambda n: nc.alloc_semaphore("p7_" + n)
        y_in = [[sem(f"y_in{k}{i}") for i in range(R)] for k in range(2)]
        res_out = [sem(f"res_out{i}") for i in range(2)]
        gf_in, seq, used0, used1, x2_made, squared, var_made, std_made, res_made = (sem(n) for n in
            ("gf_in", "seq", "used0", "used1", "x2_made", "squared", "var_made", "std_made", "res_made"))
        blk = ctx.enter_context(nc.Block())

        @blk.sync
        def _(sp):
            sp.dma_start(gf[:], a["final_norm_g"].partition_broadcast(P)).then_inc(gf_in, 16)
            for i in range(TT):
                sp.wait_ge(res_made, i + 1)
                sp.dma_start(out[0, i * P:(i + 1) * P, :], res[:, i % 2]).then_inc(res_out[i % 2], 16)
            for i in range(2):
                sp.wait_ge(res_out[i], 16 * TT // 2)

        @blk.gpsimd
        def _(pool):
            for i in range(TT):
                if i >= R:
                    pool.wait_ge(x2_made, i - R + 1)
                for k, y in enumerate((y0, y1)):
                    pool.indirect_dma_start(out=y[:, i % R], out_offset=None, in_=dram["x_buf"],
                                            in_offset=bass.IndirectOffsetOnAxis(ap=kept.slot[k][:, i:i + 1], axis=0)
                                            ).then_inc(y_in[k][i % R], 16)

        @blk.scalar
        def _(act):
            for i in range(TT):
                act.wait_ge(x2_made, i + 1)
                if i >= 2:
                    act.wait_ge(squared, i - 1)
                act.activation(sq[:, i % 2], x1[:, i], ACT.Square, accum_out=ss[:, i:i + 1]).then_inc(squared, 1)
                act.wait_ge(var_made, i + 1)
                act.activation(std[:, i:i + 1], var[:, i:i + 1], ACT.Sqrt).then_inc(std_made, 1)

        @blk.vector
        def _(dve):
            link = Chain(dve, seq)

            def norm(i):
                dve.wait_ge(squared, i + 1)
                dve.tensor_scalar(var[:, i:i + 1], ss[:, i:i + 1], 1.0 / D, EPS, ALU.mult, ALU.add).then_inc(var_made, 1)
                dve.wait_ge(std_made, i + 1)
                link(dve.reciprocal(rstd[:, i:i + 1], std[:, i:i + 1]))
                if i >= 2:
                    dve.wait_ge(res_out[i % 2], 16 * (i // 2))
                dve.scalar_tensor_tensor(res[:, i % 2], x1[:, i], rstd[:, i:i + 1], gf[:], ALU.mult, ALU.mult).then_inc(res_made, 1)

            dve.wait_ge(gf_in, 16)
            for i in range(TT):
                dve.wait_ge(y_in[0][i % R], 16 * (i // R + 1))
                link(dve.scalar_tensor_tensor(x1[:, i], y0[:, i % R], kept.weight[0][:, i:i + 1], x1[:, i], ALU.mult, ALU.add))
                dve.wait_ge(y_in[1][i % R], 16 * (i // R + 1))
                dve.scalar_tensor_tensor(x1[:, i], y1[:, i % R], kept.weight[1][:, i:i + 1], x1[:, i],
                                         ALU.mult, ALU.add).then_inc(x2_made, 1)
                if i:
                    norm(i - 1)
            norm(TT - 1)


def build(nc, a, out, stop=9):
    dram = {
        "mod": nc.dram_tensor("mod_rows", (1, 4 * D), F32).ap(),
        "acs": nc.dram_tensor("acs_rows", (HEADS, T), F32).ap(),
        "small": nc.dram_tensor("small_by_group", (P, GROUPS, 5 * TT, GH), F32).ap(),
        "acc": nc.dram_tensor("acc_ssd", (P, KT, T), F32).ap(),
        "h2": nc.dram_tensor("h2_rows", (T, D), F32).ap(),
        "x_buf": nc.dram_tensor("x_buf", ((MAX_BLOCKS + 1) * BLOCK, D), F32).ap(),
    }
    kept = Kept(nc)
    with nc.cleanup_on_exit():
        hT_hi, hT_lo = phase_modulate(nc, kept, a, dram)
        phase_steps(nc, kept, a, dram, hT_hi, hT_lo)
        phase_ssd(nc, kept, a, dram, hT_hi, hT_lo)
    u, u_at = phase_pool(nc, kept, a, dram, hT_hi, hT_lo)
    x1 = phase_mix(nc, kept, a, dram, u, u_at)
    phase_route(nc, kept, a, dram)
    phase_experts(nc, kept, a, dram)
    phase_combine(nc, kept, a, dram, x1, out)


NAMES = ["x", "c", "ada_w", "ada_b", "norm1_g", "w_in", "pool_w", "pool_scale", "conv_w", "conv_b", "dt_bias", "a_log",
         "d_skip", "ssd_norm_g", "w_branch_pool", "w_branch_ssd", "w_out", "norm2_g", "router_group_w",
         "router_group_b", "router_expert_w", "router_expert_b", "w13", "w2", "final_norm_g"]


def kernel(**inputs):
    import concourse.bacc as bacc
    from concourse.bass_utils import run_bass_kernel_spmd

    nc = bacc.Bacc("TRN2", target_bir_lowering=False, num_devices=1)
    arrays, aps = {}, {}
    for name in NAMES:
        value = np.ascontiguousarray(inputs[name])
        arrays[f"in_{name}"] = value
        aps[name] = nc.dram_tensor(f"in_{name}", value.shape, mybir.dt.from_np(value.dtype), kind="ExternalInput").ap()
    out = nc.dram_tensor("out_0", (1, T, D), F32, kind="ExternalOutput").ap()
    build(nc, aps, out)
    return run_bass_kernel_spmd(nc, [arrays], core_ids=[0]).results[0]["out_0"]
```

```python
from contextlib import ExitStack

import numpy as np

import concourse.bass as bass
from concourse import mybir

F32 = mybir.dt.float32
F32R = mybir.dt.float32r
BF16 = mybir.dt.bfloat16
U32 = mybir.dt.uint32
I32 = mybir.dt.int32
ALU = mybir.AluOpType
ACT = mybir.ActivationFunctionType
AX = mybir.AxisListType

P = 128
D = 1024
T = 1024
KT = D // P
TT = T // P
HALF = 512
HEADS = 32
HEAD_DIM = 64
GROUPS = 4
GH = HEADS // GROUPS
INNER = HEADS * HEAD_DIM
STATE = 128
CONV = 4
CONV_TILES = (INNER + 2 * GROUPS * STATE) // P
COL_Z = D
COL_X = COL_Z + INNER
COL_B = COL_X + INNER
COL_C = COL_B + GROUPS * STATE
COL_DT = COL_C + GROUPS * STATE
COL_GATE = COL_DT + HEADS
POOL_GROUPS = 4
WINDOWS = (2, 4, 8, 16)
PAD = max(WINDOWS)
MG = 4
EPG = 8
NE = MG * EPG
FF = 512
BLOCK = P
MAX_BLOCKS = 2 * T // BLOCK + NE - 1
EPS = 1e-6
NEG = -3.0e38

BASE = 16512


class Arena:

    def __init__(self, nc, prefix, start):
        self.nc, self.prefix, self.at = nc, prefix, start

    def __call__(self, name, shape, dtype=F32, at=None):
        offset = self.at if at is None else at
        t = self.nc.alloc_sbuf_tensor_at(f"{self.prefix}_{name}", shape, dtype, offset=offset)
        size = int(np.prod(shape[1:])) * (2 if dtype == BF16 else 4)
        if at is None:
            self.at = offset + (size + 31) // 32 * 32
        return t


class Chain:

    def __init__(self, eng, sem, base=0, per_pass=None):
        self.eng, self.sem, self.base, self.n, self.per_pass = eng, sem, base, 0, per_pass

    def __call__(self, ins):
        ins.then_inc(self.sem, 1)
        self.n += 1
        self.eng.wait_ge(self.sem, self.base + self.n)

    def done(self):
        assert self.per_pass is None or self.n == self.per_pass, (self.n, self.per_pass)


def bc(ap, shape):
    return ap.to_broadcast(shape)


def product(pe, out, hi, lo, rhs_hi, rhs_lo, start, stop):
    pe.matmul(out, hi, rhs_hi, start=start, stop=False)
    pe.matmul(out, hi, rhs_lo, start=False, stop=False)
    return pe.matmul(out, lo, rhs_hi, start=False, stop=stop)


class Kept:

    def __init__(self, nc):
        sb = self.sb = Arena(nc, "kept", BASE)
        self.ident = sb("ident", [P, P])
        self.ones = sb("ones", [P, P])
        self.tri = sb("tri", [P, P])
        self.tri_strict = sb("tri_strict", [P, P], BF16)
        self.ones_bf = sb("ones_bf", [P, P], BF16)
        self.cols_a = sb("cols_a", [P, P])
        self.cols_b = sb("cols_b", [P, 32])
        self.skip_col = sb("skip_col", [P, INNER // P])
        self.sq_acc = sb("sq_acc", [P, T])
        self.weight = [sb(f"weight{k}", [P, TT]) for k in range(2)]
        self.slot = [sb(f"slot{k}", [P, TT], U32) for k in range(2)]
        self.table = sb("table", [1, MAX_BLOCKS + 3], I32)
        self.logits = sb("logits", [P, TT, MG + NE])
        self.end = sb.at


def phase_modulate(nc, kept, a, dram):
    sb = Arena(nc, "p0", kept.end)
    hT_hi = sb("hT_hi", [P, KT, T], F32R)
    hT_lo = sb("hT_lo", [P, KT, T], F32R)
    x = sb("x", [P, TT, D])
    ADA = 4
    ada = sb("ada", [P, ADA, KT, 512 // 2])
    NCH = 6 * D // 256
    modr = sb("modr", [1, 6 * D])
    h_tmp = sb("h_tmp", [P, 2, T])
    rows_a = sb("rows_a", [P, P])
    rows_b = sb("rows_b", [32, P])
    skip_row = sb("skip_row", [P, HEADS])
    th_c = sb("th_c", [P, KT])
    silu_c = sb("silu_c", [P, KT])
    ss = sb("ss", [P, TT])
    var = sb("var", [P, TT])
    std = sb("std", [P, TT])
    rstd = sb("rstd", [P, TT])
    sh1 = sb("sh1", [P, KT])
    gs1 = sb("gs1", [P, KT])
    FIRST = 2 * D // 256

    with ExitStack() as ctx:
        sem = lambda n: nc.alloc_semaphore("p0_" + n)
        ps = lambda n: ctx.enter_context(nc.psum_tensor("p0_" + n, [P, HALF], F32))
        ps_cols = ps("cols")
        ps_ada = [ps("ada0"), ps("ada1")]
        ps_t = [[ps("t00"), ps("t01")], [ps("t10"), ps("t11")]]
        par_in, ident_made, consts_made, memsets = sem("par_in"), sem("ident_made"), sem("consts_made"), sem("memsets")
        ada_b_in, skip_in = sem("ada_b_in"), sem("skip_in")
        x_in = [sem(f"x_in{i}") for i in range(TT)]
        ada_in = [sem(f"ada_in{i}") for i in range(ADA)]
        ada_done, mod_row = sem("ada_done"), sem("mod_row")
        cols_turned, cols_copied, th_made, c_made = sem("cols_turned"), sem("cols_copied"), sem("th_made"), sem("c_made")
        squared, var_made, std_made, x_normed = sem("squared"), sem("var_made"), sem("std_made"), sem("x_normed")
        sh_turned, sh_made = sem("sh_turned"), sem("sh_made")
        x_turned, h_made, h_split = sem("x_turned"), sem("h_made"), sem("h_split")
        dve_seq, mod_out = sem("dve_seq"), sem("mod_out")
        blk = ctx.enter_context(nc.Block())

        @blk.sync
        def _(sp):
            sp.dma_start(rows_a[0:8, :], a["norm1_g"][0].rearrange("(j p) -> j p", p=P)).then_inc(par_in, 16)
            sp.dma_start(rows_a[8:32, :], a["conv_b"][0].rearrange("(j p) -> j p", p=P)).then_inc(par_in, 16)
            sp.dma_start(rows_a[32:128, :], a["conv_w"][0].rearrange("w (j p) -> (w j) p", p=P)).then_inc(par_in, 16)
            sp.dma_start(rows_b[0:8, :], a["pool_scale"][0].rearrange("(j p) -> j p", p=P)).then_inc(par_in, 16)
            sp.dma_start(rows_b[8:24, :], a["ssd_norm_g"][0].rearrange("(j p) -> j p", p=P)).then_inc(par_in, 16)
            sp.dma_start(rows_b[24:32, :], a["c"][0].rearrange("(j p) -> j p", p=P)).then_inc(par_in, 16)
            for n in range(NCH):
                if n >= ADA:
                    sp.wait_ge(ada_done, n - ADA + 1)
                sp.dma_start(ada[:, n % ADA], a["ada_w"][0, :, n * 256:(n + 1) * 256]
                             .rearrange("(k p) n -> p k n", p=P)).then_inc(ada_in[n % ADA], 16)
            sp.wait_ge(mod_row, NCH)
            sp.dma_start(dram["mod"], modr[0:1, 2 * D:]).then_inc(mod_out, 16)
            sp.wait_ge(mod_out, 16)

        @blk.gpsimd
        def _(pool):
            pool.memset(kept.ident[:], 0.0).then_inc(memsets, 1)
            pool.memset(kept.tri[:], 1.0).then_inc(memsets, 1)
            pool.memset(kept.tri_strict[:], 1.0).then_inc(memsets, 1)
            pool.memset(kept.ones[:], 1.0).then_inc(consts_made, 1)
            pool.memset(kept.ones_bf[:], 1.0).then_inc(consts_made, 1)
            pool.wait_ge(memsets, 3)
            pool.affine_select(out=kept.ident[:], in_=kept.ident[:], compare_op=ALU.not_equal, fill=1.0,
                               base=0, pattern=[[-1, P]], channel_multiplier=1).then_inc(ident_made, 1)
            pool.affine_select(out=kept.tri[:], in_=kept.tri[:], compare_op=ALU.is_ge, fill=0.0,
                               base=0, pattern=[[1, P]], channel_multiplier=-1).then_inc(consts_made, 1)
            pool.affine_select(out=kept.tri_strict[:], in_=kept.tri_strict[:], compare_op=ALU.is_gt, fill=0.0,
                               base=0, pattern=[[1, P]], channel_multiplier=-1).then_inc(consts_made, 1)

        @blk.scalar
        def _(act):
            act.dma_start(modr[:], a["ada_b"]).then_inc(ada_b_in, 16)
            act.dma_start(skip_row[:], a["d_skip"][0].partition_broadcast(P)).then_inc(skip_in, 16)
            for i in range(TT):
                act.dma_start(x[:, i, :], a["x"][0, i * P:(i + 1) * P, :]).then_inc(x_in[i], 16)
            act.wait_ge(cols_copied, 2)
            act.activation(th_c[:], kept.cols_b[:, 24:32], ACT.Tanh, scale=0.5).then_inc(th_made, 1)
            for i in range(TT):
                act.wait_ge(x_in[i], 16)
                if i >= 2:
                    act.wait_ge(squared, i - 1)
                act.activation(h_tmp[:, i % 2, :], x[:, i, :], ACT.Square,
                               accum_out=ss[:, i:i + 1]).then_inc(squared, 1)
            act.wait_ge(var_made, 1)
            act.activation(std[:], var[:], ACT.Sqrt).then_inc(std_made, 1)
            act.wait_ge(sh_made, 2)
            act.wait_ge(squared, TT)
            for k in range(KT):
                act.wait_ge(x_turned, k + 1)
                if k >= 2:
                    act.wait_ge(h_split, k - 1)
                for b in range(2):
                    act.activation(h_tmp[:, k % 2, b * HALF:(b + 1) * HALF], ps_t[k % 2][b][:], ACT.Identity,
                                   bias=sh1[:, k:k + 1], scale=gs1[:, k:k + 1]).then_inc(h_made, 1)

        @blk.vector
        def _(dve):
            link = Chain(dve, dve_seq)
            dve.wait_ge(cols_turned, 1)
            dve.tensor_copy(kept.cols_a[:], ps_cols[:, 0:P]).then_inc(cols_copied, 1)
            dve.tensor_copy(kept.cols_b[:], ps_cols[:, P:P + 32]).then_inc(cols_copied, 1)
            dve.wait_ge(th_made, 1)
            dve.wait_ge(cols_copied, 2)
            link(dve.scalar_tensor_tensor(silu_c[:], th_c[:], 1.0, kept.cols_b[:, 24:32], ALU.add, ALU.mult))
            dve.tensor_scalar(silu_c[:], silu_c[:], 0.5, None, ALU.mult).then_inc(c_made, 1)
            dve.wait_ge(skip_in, 16)
            dve.tensor_copy(kept.skip_col[0:64, :], skip_row[0:64, 0::2])
            dve.tensor_copy(kept.skip_col[64:128, :], skip_row[64:128, 1::2])
            dve.wait_ge(squared, TT)
            dve.tensor_scalar(var[:], ss[:], 1.0 / D, EPS, ALU.mult, ALU.add).then_inc(var_made, 1)
            dve.wait_ge(std_made, 1)
            link(dve.reciprocal(rstd[:], std[:]))
            for i in range(TT):
                dve.tensor_scalar(x[:, i, :], x[:, i, :], rstd[:, i:i + 1], None, ALU.mult).then_inc(x_normed, 1)

            def mod_chunk(n):
                dve.wait_ge(ada_done, n + 1)
                if n == 0:
                    dve.wait_ge(ada_b_in, 16)
                row = modr[0:1, n * 256:(n + 1) * 256]
                dve.tensor_tensor(row, ps_ada[n % 2][0:1, 0:256], row, ALU.add).then_inc(mod_row, 1)

            for n in range(FIRST):
                mod_chunk(n)
            dve.wait_ge(sh_turned, 1)
            dve.tensor_copy(sh1[:], ps_cols[:, 256:264]).then_inc(sh_made, 1)
            dve.scalar_tensor_tensor(gs1[:], ps_cols[:, 264:272], 1.0, kept.cols_a[:, 0:8],
                                     ALU.add, ALU.mult).then_inc(sh_made, 1)
            for k in range(KT):
                dve.wait_ge(h_made, 2 * k + 2)
                link(dve.tensor_copy(hT_hi[:, k, :], h_tmp[:, k % 2, :]))
                dve.tensor_tensor(hT_lo[:, k, :], h_tmp[:, k % 2, :], hT_hi[:, k, :].bitcast(F32),
                                  ALU.subtract).then_inc(h_split, 1)
                mod_chunk(FIRST + 2 * k)
                mod_chunk(FIRST + 2 * k + 1)

        @blk.tensor
        def _(pe):
            pe.wait_ge(par_in, 96)
            pe.wait_ge(ident_made, 1)
            pe.transpose(ps_cols[:, 0:P], rows_a[:], kept.ident[:])
            pe.transpose(ps_cols[:, P:P + 32], rows_b[:], kept.ident[0:32, 0:32]).then_inc(cols_turned, 1)
            pe.wait_ge(c_made, 1)

            def ada_chunk(n):
                pe.wait_ge(ada_in[n % ADA], 16 * (n // ADA + 1))
                if n >= 2:
                    pe.wait_ge(mod_row, n - 1)
                for k in range(KT):
                    mm = pe.matmul(ps_ada[n % 2][0:1, 0:256], silu_c[:, k:k + 1], ada[:, n % ADA, k, :],
                                   start=(k == 0), stop=(k == KT - 1))
                mm.then_inc(ada_done, 1)

            for n in range(FIRST):
                ada_chunk(n)
            pe.wait_ge(mod_row, FIRST)
            pe.wait_ge(consts_made, 4)
            for j in range(2 * KT):
                mm = pe.matmul(ps_cols[:, 256 + j:257 + j], modr[0:1, j * P:(j + 1) * P], kept.ones[0:1, 0:1],
                               start=True, stop=True)
            mm.then_inc(sh_turned, 1)
            pe.wait_ge(x_normed, TT)
            for k in range(KT):
                if k >= 2:
                    pe.wait_ge(h_made, 2 * k - 2)
                for i in range(TT):
                    mm = pe.transpose(ps_t[k % 2][i // 4][:, (i % 4) * P:(i % 4 + 1) * P],
                                      x[:, i, k * P:(k + 1) * P], kept.ident[:])
                mm.then_inc(x_turned, 1)
                ada_chunk(FIRST + 2 * k)
                ada_chunk(FIRST + 2 * k + 1)
    return hT_hi, hT_lo


def phase_steps(nc, kept, a, dram, hT_hi, hT_lo):
    sb = Arena(nc, "p1", kept.end + 2 * KT * T * 4)
    small = sb("small", [P, 5, TT, HEADS])
    small_g = sb("small_g", [P, GROUPS, 5 * TT, GH])
    acs, dt, decay, exp_acs, exp_end = (small[:, n] for n in range(5))
    w = sb("w", [P, KT, HEADS])
    w_hi = sb("w_hi", [P, KT, HEADS], F32R)
    w_lo = sb("w_lo", [P, KT, HEADS], F32R)
    bias = sb("bias", [P, HEADS])
    a_log = sb("a_log", [P, HEADS])
    a_neg = sb("a_neg", [P, HEADS])
    S = [P, TT, HEADS]
    raw, mag, ex, u, ln_u, um1, is0, a_dt, dif = (sb(n, S) for n in
                                                  ("raw", "mag", "ex", "u", "ln_u", "um1", "is0", "a_dt", "dif"))
    acs_rows = sb("acs_rows", [HEADS, T])
    with ExitStack() as ctx:
        sem = lambda n: nc.alloc_semaphore("p1_" + n)
        ps = lambda n: ctx.enter_context(nc.psum_tensor("p1_" + n, [P, HALF], F32))
        ps_dt, ps_cum, ps_end = ps("dt"), ps("cum"), ps("end")
        ps_rows = [ps("rows0"), ps("rows1")]
        par_in, w_split, dt_done, seq, act_seq = sem("par_in"), sem("w_split"), sem("dt_done"), sem("seq"), sem("act_seq")
        mag_made, ex_made, u_made, ln_made, a_made = sem("mag_made"), sem("ex_made"), sem("u_made"), sem("ln_made"), sem("a_made")
        alog_done, summed, acs_made, rows_turned = sem("alog_done"), sem("summed"), sem("acs_made"), sem("rows_turned")
        dif_made, dec_made, rows_made, rows_out = sem("dif_made"), sem("dec_made"), sem("rows_made"), sem("rows_out")
        by_group = sem("by_group")
        blk = ctx.enter_context(nc.Block())

        @blk.sync
        def _(sp):
            sp.dma_start(w[:], a["w_in"][0, :, COL_DT:COL_DT + HEADS].rearrange("(k p) n -> p k n", p=P)).then_inc(par_in, 16)
            sp.dma_start(bias[:], a["dt_bias"][0].partition_broadcast(P)).then_inc(par_in, 16)
            sp.dma_start(a_log[:], a["a_log"][0].partition_broadcast(P)).then_inc(par_in, 16)
            sp.wait_ge(rows_made, 2)
            sp.dma_start(dram["acs"], acs_rows[:]).then_inc(rows_out, 16)
            sp.wait_ge(by_group, 1)
            sp.dma_start(dram["small"], small_g[:]).then_inc(rows_out, 16)
            sp.wait_ge(rows_out, 32)

        @blk.scalar
        def _(act):
            act.wait_ge(par_in, 48)
            act.activation(a_neg[:], a_log[:], ACT.Exp).then_inc(alog_done, 1)
            act.wait_ge(mag_made, 1)
            act.activation(ex[:], mag[:], ACT.Exp, scale=-1.0).then_inc(ex_made, 1)
            act.wait_ge(u_made, 1)
            act.activation(ln_u[:], u[:], ACT.Ln).then_inc(ln_made, 1)
            act.wait_ge(dif_made, 1)
            act.activation(decay, dif[:], ACT.Exp).then_inc(dec_made, 1)
            act.activation(exp_acs, acs, ACT.Exp).then_inc(dec_made, 1)
            act.activation(exp_end, exp_end, ACT.Exp).then_inc(dec_made, 1)

        @blk.vector
        def _(dve):
            link = Chain(dve, seq)
            dve.wait_ge(par_in, 48)
            link(dve.tensor_copy(w_hi[:], w[:]))
            dve.tensor_tensor(w_lo[:], w[:], w_hi[:].bitcast(F32), ALU.subtract).then_inc(w_split, 1)
            dve.wait_ge(dt_done, 1)
            link(dve.tensor_tensor(raw[:], ps_dt[:, 0:TT * HEADS].rearrange("p (t h) -> p t h", h=HEADS),
                                   bc(bias[:].unsqueeze(1), S), ALU.add))
            link(dve.tensor_scalar(mag[:], raw[:], -1.0, None, ALU.mult))
            dve.tensor_tensor(mag[:], raw[:], mag[:], ALU.max).then_inc(mag_made, 1)
            dve.wait_ge(ex_made, 1)
            dve.tensor_scalar(u[:], ex[:], 1.0, None, ALU.add).then_inc(u_made, 1)
            dve.wait_ge(u_made, 1)
            link(dve.tensor_scalar(um1[:], u[:], -1.0, None, ALU.add))
            link(dve.tensor_scalar(is0[:], um1[:], 0.0, None, ALU.is_equal))
            link(dve.tensor_tensor(um1[:], um1[:], is0[:], ALU.add))
            link(dve.reciprocal(um1[:], um1[:]))
            dve.wait_ge(ln_made, 1)
            link(dve.tensor_tensor(ln_u[:], ln_u[:], um1[:], ALU.mult))
            link(dve.tensor_tensor(ln_u[:], ln_u[:], is0[:], ALU.add))
            link(dve.tensor_tensor(ln_u[:], ln_u[:], ex[:], ALU.mult))
            link(dve.scalar_tensor_tensor(dt, raw[:], 0.0, ln_u[:], ALU.max, ALU.add))
            dve.wait_ge(alog_done, 1)
            link(dve.tensor_scalar(a_neg[:], a_neg[:], -1.0, None, ALU.mult))
            dve.tensor_tensor(a_dt[:], dt, bc(a_neg[:].unsqueeze(1), S), ALU.mult).then_inc(a_made, 1)
            dve.wait_ge(summed, 1)
            dve.tensor_copy(acs, ps_cum[:, 0:TT * HEADS].rearrange("p (t h) -> p t h", h=HEADS)).then_inc(acs_made, 1)
            link(dve.tensor_copy(exp_end, ps_end[:, 0:TT * HEADS].rearrange("p (t h) -> p t h", h=HEADS)))
            dve.wait_ge(acs_made, 1)
            dve.tensor_tensor(dif[:], exp_end, acs, ALU.subtract).then_inc(dif_made, 1)
            for b in range(2):
                dve.wait_ge(rows_turned, b + 1)
                dve.tensor_copy(acs_rows[:, b * HALF:(b + 1) * HALF], ps_rows[b][0:HEADS, :]).then_inc(rows_made, 1)
            dve.wait_ge(dec_made, 3)
            dve.tensor_copy(small_g[:], small[:].rearrange("p a t (g h) -> p g (a t) h", h=GH)).then_inc(by_group, 1)

        @blk.tensor
        def _(pe):
            pe.wait_ge(w_split, 1)
            for i in range(TT):
                rows = slice(i * P, (i + 1) * P)
                for k in range(KT):
                    mm = product(pe, ps_dt[:, i * HEADS:(i + 1) * HEADS], hT_hi[:, k, rows], hT_lo[:, k, rows],
                                 w_hi[:, k, :], w_lo[:, k, :], k == 0, k == KT - 1)
            mm.then_inc(dt_done, 1)
            pe.wait_ge(a_made, 1)
            pe.matmul(ps_cum[:, 0:TT * HEADS], kept.tri[:], a_dt[:].rearrange("p t h -> p (t h)"), start=True, stop=True)
            pe.matmul(ps_end[:, 0:TT * HEADS], kept.ones[:], a_dt[:].rearrange("p t h -> p (t h)"),
                      start=True, stop=True).then_inc(summed, 1)
            pe.wait_ge(acs_made, 1)
            for i in range(TT):
                mm = pe.transpose(ps_rows[i // 4][0:HEADS, (i % 4) * P:(i % 4 + 1) * P], acs[:, i, :], kept.ident[:])
                if i % 4 == 3:
                    mm.then_inc(rows_turned, 1)



def phase_ssd(nc, kept, a, dram, hT_hi, hT_lo):
    sb = Arena(nc, "p2", kept.end + 2 * KT * T * 4)
    acc = sb("acc", [P, KT, T])
    RAW = 2
    raw = sb("raw", [P, RAW, KT, P])
    w_hi = sb("w_hi", [P, RAW, KT, P], F32R)
    w_lo = sb("w_lo", [P, RAW, KT, P], F32R)
    NX = INNER // GROUPS // P
    NXBC = NX + 2
    cvb = sb("cvb", [P, CONV - 1 + T])
    xcT = sb("xcT", [P, NXBC, T])
    at = sb.at
    zT = sb("zT", [P, NX, T])
    yh = sb("yh", [P, NX, T], F32R, at=at)
    at = sb.at
    yT = sb("yT", [P, NX, T])
    yl = sb("yl", [P, NX, T], F32R, at=at)
    seg = sb("seg", [P, 2, GH, P])
    XG = [P, GH, HEAD_DIM]
    x_dt, x_dec, y_tok, state = (sb(n, XG) for n in ("x_dt", "x_dec", "y_tok", "state"))
    b_tok = sb("b_tok", [P, P])
    cbm = sb("cbm", [P, P])
    gp = sb("gp", [P, 1 + CONV, NXBC])
    gs = sb("gs", [P, 5, TT, GH])
    gcol = sb("gcol", [P, 2, NX])
    NPROJ, NBR = NXBC + NX, KT
    NW = NPROJ + NBR // 2

    with ExitStack() as ctx:
        sem = lambda n: nc.alloc_semaphore("p2_" + n)
        ps = lambda n: ctx.enter_context(nc.psum_tensor("p2_" + n, [P, HALF], F32))
        pair = [[ps("pair00"), ps("pair01")], [ps("pair10"), ps("pair11")]]
        ps_x, ps_cb, ps_yd, ps_yo = ps("x"), ps("cb"), ps("yd"), ps("yo")
        w_in = [sem(f"w_in{i}") for i in range(RAW)]
        seg_in = [sem(f"seg_in{i}") for i in range(2)]
        hi_made, lo_made = sem("hi_made"), sem("lo_made")
        proj_done, br_done, proj_read, br_read = sem("proj_done"), sem("br_done"), sem("proj_read"), sem("br_read")
        pads, acc_zeroed, params = sem("pads"), sem("acc_zeroed"), sem("params")
        pre_made, th_made, xc_made, zth_made, z_made = (sem(n) for n in ("pre_made", "th_made", "xc_made", "zth_made", "z_made"))
        xt_done, xdt_made, cb_done, cbm_made, bt_made = (sem(n) for n in ("xt_done", "xdt_made", "cb_done", "cbm_made", "bt_made"))
        seg_made, exp_made, g_made, yo_done, yd_done = (sem(n) for n in ("seg_made", "exp_made", "g_made", "yo_done", "yd_done"))
        st_done, y_made, st_made, ytr_done, yT_made = (sem(n) for n in ("st_done", "y_made", "st_made", "ytr_done", "yT_made"))
        y_gated, sq_made, sq_added, yh_made, yl_made = (sem(n) for n in ("y_gated", "sq_made", "sq_added", "yh_made", "yl_made"))
        xdec_made, st_scaled, skip_made, y_skipped = sem("xdec_made"), sem("st_scaled"), sem("skip_made"), sem("y_skipped")
        seq, zeroed, acc_out, gs_in = sem("seq"), sem("zeroed"), sem("acc_out"), sem("gs_in")
        blk = ctx.enter_context(nc.Block())
        W_CREDIT = RAW
        USED_CREDIT = 2 * NBR
        BR_CREDIT = 2
        SEG_CREDIT = 2
        SQ_CREDIT = 1
        SEQ_N = 2 + NXBC * (CONV - 1) + (TT - 1)
        STEPS = (2 * (NX - 1) - 1) * KT // TT
        FIRST_STEPS = (STEPS + 1) // 2
        z_ready = [[(1 + q // 2, q % 2) for q in range(2 * (NX - 1) - 1) if (KT * (q + 1) - 1) // STEPS == c - 1]
                   for c in range(TT)]
        z_ready[0] = [(0, 0), (0, 1)]

        @blk.sync
        def _(sp):
            with sp.Fori(0, GROUPS) as g:
                def load(i, src):
                    sp.wait_ge(lo_made, g * NW + i + 1)
                    sp.dma_start(raw[:, i % RAW] if i < NPROJ else
                                 raw[:, i % RAW].rearrange("p k n -> p (k n)").rearrange("p (k n) -> p k n", k=NX),
                                 src).then_inc(w_in[i % RAW], 16)
                wide, narrow = sp.snap(g * (NX * P)), sp.snap(g * P)
                cols = [(COL_X + j * P, wide) for j in range(NX)] + [(COL_B, narrow), (COL_C, narrow)] + \
                       [(COL_Z + j * P, wide) for j in range(NX)]
                for i, (first, col) in enumerate(cols):
                    load(i, a["w_in"][0, :, first:][:, bass.ds(col, P)].rearrange("(k p) n -> p k n", p=P))
                for m in range(NBR // 2):
                    load(NPROJ + m, a["w_branch_ssd"][0, bass.ds(g * (NX * P), NX * P), 2 * m * P:(2 * m + 2) * P]
                         .rearrange("(k p) n -> p k n", p=P))
            sp.wait_ge(br_read, BR_CREDIT + GROUPS * NBR)
            sp.dma_start(dram["acc"], acc[:]).then_inc(acc_out, 16)
            sp.wait_ge(acc_out, 16)

        @blk.gpsimd
        def _(pool):
            pool.sem_inc(yd_done, SEG_CREDIT)
            pool.sem_inc(sq_added, SQ_CREDIT)
            pool.memset(cvb[:, 0:CONV - 1], 0.0).then_inc(pads, 1)
            pool.memset(kept.sq_acc[:], 0.0).then_inc(acc_zeroed, 1)
            pool.memset(acc[:], 0.0).then_inc(acc_zeroed, 1)
            x_buf = dram["x_buf"].rearrange("(b p) c -> b p c", p=P)
            pool.wait_ge(acc_zeroed, 2)
            for b in range(MAX_BLOCKS + 1):
                pool.dma_start(x_buf[b], acc[:, 0, :]).then_inc(zeroed, 16)
            with pool.Fori(0, GROUPS) as g:
                pool.dma_start(gs[:], dram["small"][:, bass.ds(g, 1)].rearrange("p g (a t) h -> p (g a) t h", t=TT)).then_inc(gs_in, 16)

                def add_skip(c):
                    ch = slice(c * P, (c + 1) * P)
                    pool.wait_ge(yT_made, g * TT + c + 1)
                    pool.wait_ge(skip_made, g * TT + c + 1)
                    pool.tensor_tensor(yT[:, :, ch], yT[:, :, ch], xcT[:, 0:NX, ch], ALU.add).then_inc(y_skipped, 1)

                pool.wait_ge(gs_in, 16 * (g + 1))
                for c in range(TT):
                    ch = slice(c * P, (c + 1) * P)
                    pool.wait_ge(xdt_made, g * TT + c + 1)
                    if c < TT - 1:
                        pool.tensor_tensor(x_dec[:], x_dt[:], bc(gs[:, 2, c, :].unsqueeze(2), XG), ALU.mult).then_inc(xdec_made, 1)
                    if c:
                        add_skip(c - 1)
                    if 0 < c < TT - 1:
                        pool.wait_ge(yo_done, g * (TT - 1) + c)
                        pool.tensor_tensor(state[:], state[:], bc(gs[:, 4, c, :].unsqueeze(2), XG), ALU.mult).then_inc(st_scaled, 1)
                    pool.tensor_tensor(xcT[:, 0:NX, ch], xcT[:, 0:NX, ch], bc(gcol[:, 1, :].unsqueeze(2), [P, NX, P]),
                                       ALU.mult).then_inc(skip_made, 1)
                add_skip(TT - 1)
                for j in range(NX):
                    pool.wait_ge(sq_made, g * NX + j + 1)
                    pool.wait_ge(sq_added, g * NX + j + SQ_CREDIT)
                    pool.tensor_tensor(kept.sq_acc[:], kept.sq_acc[:], xcT[:, j, :], ALU.add).then_inc(sq_added, 1)
            pool.wait_ge(zeroed, 16 * (MAX_BLOCKS + 1))

        @blk.scalar
        def _(act):
            with act.Fori(0, GROUPS) as g:
                def hi(i):
                    slot = i % RAW
                    act.wait_ge(w_in[slot], 16 * (g * (NW // RAW) + i // RAW + 1))
                    if i < RAW:
                        act.wait_ge(br_done, g * (2 * NBR) + 2 * NBR - 4 * (RAW - 1 - i))
                    elif i - RAW < NPROJ:
                        act.wait_ge(proj_done, g * (2 * NPROJ) + 2 * (i - RAW) + 2)
                    else:
                        act.wait_ge(br_done, g * (2 * NBR) + 4 * (i - RAW - NPROJ) + 4 + USED_CREDIT)
                    act.activation(w_hi[:, slot], raw[:, slot], ACT.Copy).then_inc(hi_made, 1)

                def load_seg(c):
                    act.wait_ge(yd_done, g * TT + c + 1)
                    act.dma_start(seg[:, c % 2], dram["acs"][bass.ds(g * GH, GH), c * P:(c + 1) * P]
                                  .partition_broadcast(P)).then_inc(seg_in[c % 2], 16)

                hi(0)
                hi(1)
                load_seg(0)
                load_seg(1)
                for i in range(NXBC):
                    if i:
                        act.wait_ge(xc_made, g * NXBC + i)
                    for b in range(2):
                        act.wait_ge(proj_done, g * (2 * NPROJ) + 2 * i + b + 1)
                        act.activation(cvb[:, CONV - 1 + b * HALF:CONV - 1 + (b + 1) * HALF], pair[i % 2][b][:],
                                       ACT.Copy).then_inc(proj_read, 1)
                    hi(i + 2)
                    act.wait_ge(pre_made, g * NXBC + i + 1)
                    act.activation(cvb[:, CONV - 1:], xcT[:, i, :], ACT.Tanh).then_inc(th_made, 1)

                def y_out(c):
                    act.wait_ge(ytr_done, g * TT + c + 1)
                    act.activation(yT[:, :, c * P:(c + 1) * P], ps_yo[:].rearrange("p (j l) -> p j l", l=P),
                                   ACT.Copy).then_inc(yT_made, 1)

                def z_half(j, b):
                    if b == 0:
                        if j == 0:
                            act.wait_ge(xc_made, g * NXBC + NXBC)
                        else:
                            act.wait_ge(z_made, g * NX + j)
                    i = NXBC + j
                    act.wait_ge(proj_done, g * (2 * NPROJ) + 2 * i + b + 1)
                    half = slice(b * HALF, (b + 1) * HALF)
                    act.activation(zT[:, j, half], pair[i % 2][b][:], ACT.Copy, scale=0.5)
                    act.activation(cvb[:, CONV - 1 + b * HALF:CONV - 1 + (b + 1) * HALF], pair[i % 2][b][:],
                                   ACT.Tanh, scale=0.5).then_inc(proj_read, 1)
                    if b == 1:
                        hi(i + 2)

                for c in range(TT):
                    if 0 < c < TT - 1:
                        load_seg(c + 1)
                    act.wait_ge(seg_made, g * TT + c + 1)
                    act.activation(seg[:, c % 2], seg[:, c % 2], ACT.Exp).then_inc(exp_made, 1)
                    act.wait_ge(cbm_made, g * TT + c + 1)
                    act.activation(b_tok[:], ps_cb[:, P:2 * P], ACT.Copy).then_inc(bt_made, 1)
                    if c:
                        y_out(c - 1)
                    for j, b in z_ready[c]:
                        z_half(j, b)
                y_out(TT - 1)
                z_half(NX - 1, 0)
                z_half(NX - 1, 1)
                for j in range(NX):
                    act.wait_ge(y_gated, g * NX + j + 1)
                    act.activation(yh[:, j, :], yT[:, j, :], ACT.Copy, scale=gcol[:, 0, j:j + 1]).then_inc(yh_made, 1)
                    act.activation(xcT[:, j, :], yT[:, j, :], ACT.Square).then_inc(sq_made, 1)
                hi(NW - 2)
                hi(NW - 1)

        @blk.vector
        def _(dve):
            dve.sem_inc(lo_made, W_CREDIT)
            dve.sem_inc(br_read, BR_CREDIT)
            dve.wait_ge(pads, 1)
            dve.wait_ge(acc_zeroed, 2)
            with dve.Fori(0, GROUPS) as g:
                link = Chain(dve, seq, g * SEQ_N, SEQ_N)

                def lo(i):
                    slot = i % RAW
                    dve.wait_ge(hi_made, g * NW + i + 1)
                    dve.tensor_tensor(w_lo[:, slot], raw[:, slot], w_hi[:, slot].bitcast(F32),
                                      ALU.subtract).then_inc(lo_made, 1)

                lo(0)
                conv_cols = kept.cols_a[:, 8:8 + (1 + CONV) * CONV_TILES].rearrange("p (w m) -> p w m", m=CONV_TILES)
                dve.tensor_copy(gp[:, :, 0:NX], conv_cols[:, :, bass.ds(g * NX, NX)])
                dve.tensor_copy(gp[:, :, NX:NX + 1], conv_cols[:, :, bass.ds(g + INNER // P, 1)])
                dve.tensor_copy(gp[:, :, NX + 1:NX + 2], conv_cols[:, :, bass.ds(g + INNER // P + GROUPS, 1)])
                dve.tensor_copy(gcol[:, 0, :], kept.cols_b[:, bass.ds(g * NX + 8, NX)])
                link(dve.tensor_copy(gcol[:, 1, :], kept.skip_col[:, bass.ds(g * NX, NX)]))
                link(dve.tensor_scalar(gp[:], gp[:], 0.5, None, ALU.mult))
                g_acs, g_dt, g_exp = gs[:, 0], gs[:, 1], gs[:, 3]
                lo(1)
                dve.wait_ge(sq_added, g * NX + SQ_CREDIT)
                for i in range(NXBC):
                    dve.wait_ge(proj_read, g * (2 * NPROJ) + 2 * i + 2)
                    link(dve.tensor_scalar(xcT[:, i, :], cvb[:, 0:T], gp[:, 1, i:i + 1], gp[:, 0, i:i + 1],
                                           ALU.mult, ALU.add))
                    for w in range(1, CONV):
                        ins = dve.scalar_tensor_tensor(xcT[:, i, :], cvb[:, w:w + T], gp[:, 1 + w, i:i + 1],
                                                       xcT[:, i, :], ALU.mult, ALU.add)
                        if w < CONV - 1:
                            link(ins)
                    ins.then_inc(pre_made, 1)
                    lo(i + 2)
                    dve.wait_ge(th_made, g * NXBC + i + 1)
                    dve.wait_ge(pre_made, g * NXBC + i + 1)
                    dve.scalar_tensor_tensor(xcT[:, i, :], cvb[:, CONV - 1:], 1.0, xcT[:, i, :],
                                             ALU.add, ALU.mult).then_inc(xc_made, 1)

                def segments(c):
                    dve.wait_ge(seg_in[c % 2], 16 * (g * (TT // 2) + c // 2 + 1))
                    for h in range(GH):
                        ins = dve.tensor_scalar(seg[:, c % 2, h, :], seg[:, c % 2, h, :], g_acs[:, c, h:h + 1], 0.0,
                                                ALU.subtract, ALU.min)
                    ins.then_inc(seg_made, 1)

                def z_gate(j):
                    dve.wait_ge(proj_read, g * (2 * NPROJ) + 2 * (NXBC + j) + 2)
                    dve.scalar_tensor_tensor(zT[:, j, :], cvb[:, CONV - 1:], 1.0, zT[:, j, :],
                                             ALU.add, ALU.mult).then_inc(z_made, 1)

                dve.wait_ge(gs_in, 16 * (g + 1))
                segments(0)
                for c in range(TT):
                    dve.wait_ge(xt_done, g * TT + c + 1)
                    xt = ps_x[:].rearrange("p (h d) -> p h d", d=HEAD_DIM)
                    dve.tensor_tensor(x_dt[:], xt, bc(g_dt[:, c, :].unsqueeze(2), XG), ALU.mult).then_inc(xdt_made, 1)
                    dve.wait_ge(cb_done, g * TT + c + 1)
                    dve.tensor_tensor(cbm[:], ps_cb[:, 0:P], kept.tri[:], ALU.mult).then_inc(cbm_made, 1)
                    dve.wait_ge(cbm_made, g * TT + c + 1)
                    dve.wait_ge(exp_made, g * TT + c + 1)
                    dve.tensor_tensor(seg[:, c % 2], seg[:, c % 2], bc(cbm[:].unsqueeze(1), [P, GH, P]),
                                      ALU.mult).then_inc(g_made, 1)
                    if c + 1 < TT:
                        segments(c + 1)
                    if c:
                        dve.wait_ge(yo_done, g * (TT - 1) + c)
                        dve.wait_ge(ytr_done, g * TT + c)
                        link(dve.tensor_tensor(y_tok[:], ps_yo[:].rearrange("p (h d) -> p h d", d=HEAD_DIM),
                                               bc(g_exp[:, c, :].unsqueeze(2), XG), ALU.mult))
                        dve.wait_ge(yd_done, g * TT + c + 1 + SEG_CREDIT)
                        dve.tensor_tensor(y_tok[:], ps_yd[:].rearrange("p (h d) -> p h d", d=HEAD_DIM), y_tok[:],
                                          ALU.add).then_inc(y_made, 1)
                    else:
                        dve.wait_ge(yd_done, g * TT + c + 1 + SEG_CREDIT)
                        dve.tensor_copy(y_tok[:], ps_yd[:].rearrange("p (h d) -> p h d", d=HEAD_DIM)).then_inc(y_made, 1)
                    if c < TT - 1:
                        dve.wait_ge(st_done, g * (TT - 1) + c + 1)
                        if c:
                            dve.wait_ge(st_scaled, g * (TT - 2) + c)
                            dve.tensor_tensor(state[:], ps_x[:].rearrange("p (h d) -> p h d", d=HEAD_DIM), state[:],
                                              ALU.add).then_inc(st_made, 1)
                        else:
                            dve.tensor_copy(state[:], ps_x[:].rearrange("p (h d) -> p h d", d=HEAD_DIM)).then_inc(st_made, 1)
                    if c == 0:
                        lo(NXBC + 2)
                    for j, b in z_ready[c]:
                        if b and j:
                            z_gate(j)
                            lo(NXBC + j + 2)
                    if c == 1:
                        z_gate(0)

                def y_gate(j):
                    dve.wait_ge(z_made, g * NX + j + 1)
                    dve.tensor_tensor(yT[:, j, :], yT[:, j, :], zT[:, j, :], ALU.mult).then_inc(y_gated, 1)

                def y_lo(j):
                    dve.wait_ge(yh_made, g * NX + j + 1)
                    dve.wait_ge(sq_made, g * NX + j + 1)
                    dve.scalar_tensor_tensor(yl[:, j, :], yT[:, j, :], gcol[:, 0, j:j + 1], yh[:, j, :].bitcast(F32),
                                             ALU.mult, ALU.subtract).then_inc(yl_made, 1)

                dve.wait_ge(y_skipped, g * TT + TT)
                y_gate(0)
                y_gate(1)
                for j in range(NX):
                    y_lo(j)
                    if j == 0:
                        z_gate(NX - 1)
                    if j + 2 < NX:
                        y_gate(j + 2)
                lo(NPROJ + 1)
                dve.wait_ge(zeroed, 16 * (MAX_BLOCKS + 1))
                for n in range(NBR):
                    for b in range(2):
                        half = slice(b * HALF, (b + 1) * HALF)
                        dve.wait_ge(br_done, g * (2 * NBR) + 2 * n + b + 1 + USED_CREDIT)
                        ins = dve.tensor_tensor(acc[:, n, half], pair[n % 2][b][:], acc[:, n, half], ALU.add)
                    ins.then_inc(br_read, 1)
                    if n % 2 and NPROJ + n // 2 + 2 < NW:
                        lo(NPROJ + n // 2 + 2)
                link.done()

        @blk.tensor
        def _(pe):
            pe.sem_inc(br_done, USED_CREDIT)
            with pe.Fori(0, GROUPS) as g:
                def begin(i):
                    pe.wait_ge(lo_made, g * NW + i + 1 + W_CREDIT)
                    pe.wait_ge(hi_made, g * NW + i + 1)

                def steps(i, first, last):
                    for n in range(first, last):
                        b, k = divmod(n, KT)
                        mm = product(pe, pair[i % 2][b][:], w_hi[:, i % RAW, k, :], w_lo[:, i % RAW, k, :],
                                     hT_hi[:, k, b * HALF:(b + 1) * HALF], hT_lo[:, k, b * HALF:(b + 1) * HALF],
                                     k == 0, k == KT - 1)
                        if k == KT - 1:
                            mm.then_inc(proj_done, 1)

                def z_steps(first, last):
                    for n in range(first, last):
                        j, step = divmod(n, 2 * KT)
                        i = NXBC + 1 + j
                        if step == 0:
                            begin(i)
                            pe.wait_ge(proj_read, g * (2 * NPROJ) + 2 * (i - 2) + 2)
                        steps(i, step, step + 1)

                for i in range(NXBC + 1):
                    begin(i)
                    if i < 2:
                        pe.wait_ge(br_read, g * NBR + i + 1)
                    else:
                        pe.wait_ge(proj_read, g * (2 * NPROJ) + 2 * (i - 2) + 2)
                    steps(i, 0, 2 * KT)

                def y_turn(c):
                    pe.wait_ge(y_made, g * TT + c + 1)
                    for j in range(NX):
                        mm = pe.transpose(ps_yo[:, j * P:(j + 1) * P],
                                          y_tok[:].rearrange("p h d -> p (h d)")[:, j * P:(j + 1) * P], kept.ident[:])
                    mm.then_inc(ytr_done, 1)

                bT, cT = xcT[:, NX, :], xcT[:, NX + 1, :]
                pe.wait_ge(xc_made, g * NXBC + NXBC)
                for c in range(TT):
                    ch = slice(c * P, (c + 1) * P)
                    if c:
                        pe.wait_ge(st_made, g * (TT - 1) + c)
                    for m in range(NX):
                        mm = pe.transpose(ps_x[:, m * P:(m + 1) * P], xcT[:, m, ch], kept.ident[:])
                    mm.then_inc(xt_done, 1)
                    pe.matmul(ps_cb[:, 0:P], bT[:, ch], cT[:, ch], start=True, stop=True)
                    pe.transpose(ps_cb[:, P:2 * P], bT[:, ch], kept.ident[:]).then_inc(cb_done, 1)
                    if c:
                        y_turn(c - 1)
                    z_steps(c * STEPS, c * STEPS + FIRST_STEPS)
                    if c:
                        pe.wait_ge(yT_made, g * TT + c)
                        pe.matmul(ps_yo[:], cT[:, ch], state[:].rearrange("p h d -> p (h d)"),
                                  start=True, stop=True).then_inc(yo_done, 1)
                    pe.wait_ge(g_made, g * TT + c + 1)
                    for h in range(GH):
                        mm = pe.matmul(ps_yd[:, h * HEAD_DIM:(h + 1) * HEAD_DIM], seg[:, c % 2, h, :], x_dt[:, h, :],
                                       start=True, stop=True)
                    mm.then_inc(yd_done, 1)
                    pe.wait_ge(bt_made, g * TT + c + 1)
                    if c < TT - 1:
                        pe.wait_ge(xdec_made, g * (TT - 1) + c + 1)
                        pe.matmul(ps_x[:], b_tok[:], x_dec[:].rearrange("p h d -> p (h d)"),
                                  start=True, stop=True).then_inc(st_done, 1)
                    z_steps(c * STEPS + FIRST_STEPS, (c + 1) * STEPS)
                z_steps(TT * STEPS, TT * STEPS + FIRST_STEPS)
                y_turn(TT - 1)
                z_steps(TT * STEPS + FIRST_STEPS, TT * STEPS + KT)

                def branch(n, b, k):
                    i = NPROJ + n // 2
                    wh = w_hi[:, i % RAW].rearrange("p k n -> p (k n)").rearrange("p (k n) -> p k n", k=NX)
                    wl = w_lo[:, i % RAW].rearrange("p k n -> p (k n)").rearrange("p (k n) -> p k n", k=NX)
                    m, half = slice((n % 2) * P, (n % 2 + 1) * P), slice(b * HALF, (b + 1) * HALF)
                    mm = product(pe, pair[n % 2][b][:], wh[:, k, m], wl[:, k, m], yh[:, k, half], yl[:, k, half],
                                 k == 0, k == NX - 1)
                    if k == NX - 1:
                        mm.then_inc(br_done, 1)

                begin(NPROJ)
                pe.wait_ge(proj_read, g * (2 * NPROJ) + 2 * NPROJ)
                for k in range(NX):
                    pe.wait_ge(yl_made, g * NX + k + 1)
                    for n in range(2):
                        for b in range(2):
                            branch(n, b, k)
                for n in range(2, NBR):
                    if n % 2 == 0:
                        begin(NPROJ + n // 2)
                    pe.wait_ge(br_read, g * NBR + n - 1 + BR_CREDIT)
                    for b in range(2):
                        for k in range(NX):
                            branch(n, b, k)


def phase_pool(nc, kept, a, dram, hT_hi, hT_lo):
    start = kept.end + 2 * KT * T * 4
    sb = Arena(nc, "p3", start)
    ypT_hi = sb("ypT_hi", [P, KT, T], F32R)
    ypT_lo = sb("ypT_lo", [P, KT, T], F32R)
    RAW = 2
    raw = sb("raw", [P, RAW, KT, P])
    w_hi = sb("w_hi", [P, RAW, KT, P], F32R)
    w_lo = sb("w_lo", [P, RAW, KT, P], F32R)
    sq_n = INNER
    at = sb.at
    xpad, win0, win1 = (sb(n, [P, PAD + T]) for n in ("xpad", "win0", "win1"))
    sb.at = at
    t_a, t_b, acc_n = (sb(n, [P, T]) for n in ("t_a", "t_b", "acc_n"))
    sb.at = at + 3 * (PAD + T) * 4
    inv_count = sb("inv_count", [P, PAD])
    edge = sb("edge", [P, PAD])
    at = u_at = sb.at
    u = sb("u", [P, KT, T])
    NDT = 4
    d_hi = sb("d_hi", [P, NDT, T], F32R, at=at)
    d_lo = sb("d_lo", [P, NDT, T], F32R, at=at + NDT * T * 4)
    rstd = kept.sq_acc

    PW = 2
    order = []
    for m in range(KT):
        order.append(("x", m))
        if m % PW == PW - 1 and m >= 2 * PW - 1:
            order.append(("w", m // PW - 1))
    order.append(("w", POOL_GROUPS - 1))
    NS = len(order)
    assert NS % RAW == 0
    pair_of, n_pairs = {}, 0
    for kind, m in order:
        for o in range(1 if kind == "x" else PW):
            pair_of[(kind, m, o)] = n_pairs
            n_pairs += 1
    assert n_pairs % 2 == 0

    with ExitStack() as ctx:
        sem = lambda n: nc.alloc_semaphore("p3_" + n)
        ps = lambda n: ctx.enter_context(nc.psum_tensor("p3_" + n, [P, HALF], F32))
        pair = [[ps("pair00"), ps("pair01")], [ps("pair10"), ps("pair11")]]
        ps_sq = [ps("sq0"), ps("sq1")]
        w_in = [sem(f"w_in{i}") for i in range(RAW)]
        acc_in = sem("acc_in")
        hi_made, lo_made, w_used = sem("hi_made"), sem("lo_made"), sem("w_used")
        pads, counts, iota_made, sq_summed, var_made, std_made = (sem(n) for n in ("pads", "counts", "iota_made", "sq_summed", "var_made", "std_made"))
        done, x_read, d_made, dh_made, dl_made, yh_made, yl_made = (sem(n) for n in
            ("done", "x_read", "d_made", "dh_made", "dl_made", "yh_made", "yl_made"))
        gb_done, gate_read, br_read, tb_used, u_made, seq, seq2 = (sem(n) for n in
            ("gb_done", "gate_read", "br_read", "tb_used", "u_made", "seq", "seq2"))
        blk = ctx.enter_context(nc.Block())
        W_CREDIT = RAW
        PASSES, NQ = KT // 2, 2
        NI = 3 * NQ
        GATE_CREDIT, BR_CREDIT, TB_CREDIT, U_CREDIT = 1, 1, 1, 1
        SEQ2 = 2 * NQ

        @blk.sync
        def _(sp):
            for n, (kind, m) in enumerate(order):
                sp.wait_ge(lo_made, n + 1)
                if kind == "x":
                    src, dst = a["w_in"][0, :, m * P:(m + 1) * P].rearrange("(k p) n -> p k n", p=P), raw[:, n % RAW]
                else:
                    src = a["pool_w"][0, m].rearrange("(k p) n -> p k n", p=P)
                    dst = raw[:, n % RAW, 0:2 * PW].rearrange("p k n -> p (k n)").rearrange("p (k n) -> p k n", k=PW)
                sp.dma_start(dst, src).then_inc(w_in[n % RAW], 16)
            for p in range(PASSES):
                for i in range(NI):
                    q, r = divmod(i, 3)
                    sp.wait_ge(lo_made, p * NI + NS + i + 1)
                    first = q * P + (COL_GATE + r * D if r < 2 else 0)
                    src = a["w_in" if r < 2 else "w_branch_pool"][0, :, p * (NQ * P) + first:p * (NQ * P) + first + P]
                    sp.dma_start(raw[:, i % RAW], src.rearrange("(k p) n -> p k n", p=P)).then_inc(w_in[i % RAW], 16)

        @blk.gpsimd
        def _(pool):
            pool.sem_inc(lo_made, W_CREDIT)
            pool.sem_inc(w_used, W_CREDIT)
            pool.sem_inc(gate_read, GATE_CREDIT)
            pool.sem_inc(br_read, BR_CREDIT)
            pool.sem_inc(tb_used, TB_CREDIT)
            pool.sem_inc(u_made, U_CREDIT)
            pool.memset(xpad[:, 0:PAD], 0.0).then_inc(pads, 1)
            pool.iota(inv_count[:], pattern=[[1, PAD]], base=1, channel_multiplier=0,
                      allow_small_or_imprecise_dtypes=True).then_inc(iota_made, 1)
            pool.wait_ge(yl_made, KT)
            with pool.Fori(0, PASSES) as p:
                for q in range(NQ):
                    pool.wait_ge(tb_used, p * NQ + q + TB_CREDIT)
                    pool.dma_start(acc_n[:], dram["acc"][:, bass.ds(p * NQ + q, 1), :]
                                   .rearrange("p k t -> p (k t)")).then_inc(acc_in, 16)

        @blk.scalar
        def _(act):
            def hi(n, base=0):
                slot = n % RAW
                act.wait_ge(w_in[slot], 16 * (base + n // RAW + 1))
                act.wait_ge(w_used, base * RAW + n + 1)
                act.activation(w_hi[:, slot], raw[:, slot], ACT.Copy).then_inc(hi_made, 1)

            hi(0)
            hi(1)
            act.wait_ge(var_made, 1)
            act.activation(rstd[:], rstd[:], ACT.Sqrt).then_inc(std_made, 1)
            for n, (kind, m) in enumerate(order):
                if kind == "x":
                    if m:
                        act.wait_ge(d_made, m)
                    k = pair_of[(kind, m, 0)]
                    for b in range(2):
                        act.wait_ge(done, 2 * k + b + 1)
                        act.activation(xpad[:, PAD + b * HALF:PAD + (b + 1) * HALF], pair[k % 2][b][:],
                                       ACT.Copy).then_inc(x_read, 1)
                else:
                    for o in range(PW):
                        k, t = pair_of[(kind, m, o)], m * PW + o
                        for b in range(2):
                            act.wait_ge(done, 2 * k + b + 1)
                            act.activation(ypT_hi[:, t, b * HALF:(b + 1) * HALF], pair[k % 2][b][:], ACT.Copy,
                                           scale=kept.cols_b[:, t:t + 1]).then_inc(yh_made, 1)
                if n + 2 < NS:
                    hi(n + 2)
                if kind == "x":
                    act.wait_ge(d_made, m + 1)
                    act.activation(d_hi[:, m % NDT, :], win1[:, 0:T], ACT.Copy).then_inc(dh_made, 1)
            with act.Fori(0, PASSES) as p:
                pass_base = p * (NI // RAW) + NS // RAW
                hi(0, pass_base)
                hi(1, pass_base)
                for i in range(NI):
                    q, r = divmod(i, 3)
                    if r < 2:
                        if r == 0:
                            act.wait_ge(u_made, p * NQ + q + U_CREDIT)
                        t = t_a if r == 0 else t_b
                        for b in range(2):
                            act.wait_ge(gb_done, p * (2 * NI) + 2 * i + b + 1)
                            ins = act.activation(t[:, b * HALF:(b + 1) * HALF], pair[i % 2][b][:], ACT.Tanh, scale=0.5)
                        ins.then_inc(gate_read, 1)
                    if i + 2 < NI:
                        hi(i + 2, pass_base)

        @blk.vector
        def _(dve):
            link = Chain(dve, seq)

            def lo(n, base=0):
                slot = n % RAW
                dve.wait_ge(hi_made, base * RAW + n + 1)
                dve.tensor_tensor(w_lo[:, slot], raw[:, slot], w_hi[:, slot].bitcast(F32),
                                  ALU.subtract).then_inc(lo_made, 1)

            lo(0)
            lo(1)
            dve.wait_ge(sq_summed, 1)
            for b in range(2):
                ins = dve.tensor_scalar(rstd[:, b * HALF:(b + 1) * HALF], ps_sq[b][:], 1.0 / INNER, EPS, ALU.mult, ALU.add)
            ins.then_inc(var_made, 1)
            dve.wait_ge(std_made, 1)
            link(dve.reciprocal(rstd[:], rstd[:]))
            dve.wait_ge(iota_made, 1)
            link(dve.reciprocal(inv_count[:], inv_count[:]))
            dve.wait_ge(pads, 1)
            for n, (kind, m) in enumerate(order):
                if kind == "x":
                    w = WINDOWS[m // PW]
                    dve.wait_ge(x_read, 2 * m + 2)
                    if m:
                        dve.wait_ge(dh_made, m)
                    src, dst, span, free = xpad, win0, 1, win1
                    while span < w:
                        link(dve.tensor_tensor(dst[:, 2 * span - 1:], src[:, 2 * span - 1:],
                                               src[:, span - 1:PAD + T - span], ALU.add))
                        src, dst, free = dst, free, dst
                        span *= 2
                    x_, s_ = xpad[:, PAD:], src[:, PAD:]
                    link(dve.tensor_tensor(edge[:, 0:w], s_[:, 0:w], inv_count[:, 0:w], ALU.mult))
                    out = win0 if src is win1 else win1
                    link(dve.scalar_tensor_tensor(out[:, 0:T], s_, 1.0 / w, x_, ALU.mult, ALU.subtract))
                    ins = dve.tensor_tensor(out[:, 0:w], edge[:, 0:w], x_[:, 0:w], ALU.subtract)
                    if out is win0:
                        link(ins)
                        ins = dve.tensor_copy(win1[:, 0:T], win0[:, 0:T])
                    ins.then_inc(d_made, 1)
                if n + 2 < NS:
                    lo(n + 2)
                if kind == "x":
                    dve.wait_ge(dh_made, m + 1)
                    dve.tensor_tensor(d_lo[:, m % NDT, :], win1[:, 0:T], d_hi[:, m % NDT, :].bitcast(F32),
                                      ALU.subtract).then_inc(dl_made, 1)
                else:
                    for o in range(PW):
                        k, t = pair_of[(kind, m, o)], m * PW + o
                        dve.wait_ge(yh_made, 2 * t + 2)
                        for b in range(2):
                            half = slice(b * HALF, (b + 1) * HALF)
                            ins = dve.scalar_tensor_tensor(ypT_lo[:, t, half], pair[k % 2][b][:], kept.cols_b[:, t:t + 1],
                                                           ypT_hi[:, t, half].bitcast(F32), ALU.mult, ALU.subtract)
                        ins.then_inc(yl_made, 1)
            with dve.Fori(0, PASSES) as p:
                link = Chain(dve, seq2, p * SEQ2, SEQ2)
                pass_base = p * (NI // RAW) + NS // RAW
                lo(0, pass_base)
                lo(1, pass_base)
                for i in range(NI):
                    q, r = divmod(i, 3)
                    if i + 2 < NI:
                        lo(i + 2, pass_base)
                    if r == 1:
                        dve.wait_ge(acc_in, 16 * (p * NQ + q + 1))
                        dve.wait_ge(gate_read, p * (2 * NQ) + 2 * q + 2 + GATE_CREDIT)
                        link(dve.scalar_tensor_tensor(t_b[:], t_b[:], 1.0, acc_n[:], ALU.add, ALU.mult))
                        dve.sem_inc(tb_used, 1)
                        link(dve.tensor_tensor(t_b[:], t_b[:], rstd[:], ALU.mult))
                    if r == 2:
                        for b in range(2):
                            half = slice(b * HALF, (b + 1) * HALF)
                            dve.wait_ge(gb_done, p * (2 * NI) + 2 * i + b + 1)
                            ins = dve.scalar_tensor_tensor(t_a[:, half], t_a[:, half], 1.0, pair[i % 2][b][:], ALU.add, ALU.mult)
                        ins.then_inc(br_read, 1)
                        dve.wait_ge(br_read, p * NQ + q + 1 + BR_CREDIT)
                        dve.tensor_tensor(u[:, bass.ds(p * NQ + q, 1), :], t_a[:].unsqueeze(1), t_b[:].unsqueeze(1),
                                          ALU.add).then_inc(u_made, 1)
                link.done()

        @blk.tensor
        def _(pe):
            for b in range(2):
                mm = pe.matmul(ps_sq[b][:], kept.ones[:], kept.sq_acc[:, b * HALF:(b + 1) * HALF], start=True, stop=True)
            mm.then_inc(sq_summed, 1)
            taken = []
            for n, (kind, m) in enumerate(order):
                pe.wait_ge(hi_made, n + 1)
                pe.wait_ge(lo_made, n + 1 + W_CREDIT)
                for o in range(1 if kind == "x" else PW):
                    k = pair_of[(kind, m, o)]
                    if k >= 2:
                        was, wm, wo = taken[k - 2]
                        if was == "x":
                            pe.wait_ge(x_read, 2 * wm + 2)
                        else:
                            pe.wait_ge(yl_made, wm * PW + wo + 1)
                    taken.append((kind, m, o))
                    for b in range(2):
                        half = slice(b * HALF, (b + 1) * HALF)
                        if kind == "x":
                            for kk in range(KT):
                                mm = product(pe, pair[k % 2][b][:], w_hi[:, n % RAW, kk, :], w_lo[:, n % RAW, kk, :],
                                             hT_hi[:, kk, half], hT_lo[:, kk, half], kk == 0, kk == KT - 1)
                        else:
                            pe.wait_ge(dl_made, m * PW + PW)
                            wh = w_hi[:, n % RAW, 0:2 * PW].rearrange("p k n -> p (k n)").rearrange("p (k n) -> p k n", k=PW)
                            wl = w_lo[:, n % RAW, 0:2 * PW].rearrange("p k n -> p (k n)").rearrange("p (k n) -> p k n", k=PW)
                            for kk in range(PW):
                                t = (m * PW + kk) % NDT
                                mm = product(pe, pair[k % 2][b][:], wh[:, kk, o * P:(o + 1) * P], wl[:, kk, o * P:(o + 1) * P],
                                             d_hi[:, t, half], d_lo[:, t, half], kk == 0, kk == PW - 1)
                        mm.then_inc(done, 1)
                pe.wait_ge(done, 2 * k + 2)
                pe.sem_inc(w_used, 1)
            pe.wait_ge(yl_made, KT)
            with pe.Fori(0, PASSES) as p:
                for i in range(NI):
                    q, r = divmod(i, 3)
                    pe.wait_ge(hi_made, p * NI + NS + i + 1)
                    pe.wait_ge(lo_made, p * NI + NS + i + 1 + W_CREDIT)
                    if i == 0:
                        pe.wait_ge(gate_read, p * (2 * NQ) + GATE_CREDIT)
                    elif i == 1:
                        pe.wait_ge(br_read, p * NQ + BR_CREDIT)
                    elif (i - 2) % 3 == 2:
                        pe.wait_ge(br_read, p * NQ + (i - 2) // 3 + 1 + BR_CREDIT)
                    else:
                        pe.wait_ge(gate_read, p * (2 * NQ) + (i - 2) // 3 * 2 + (i - 2) % 3 + 1 + GATE_CREDIT)
                    for b in range(2):
                        half = slice(b * HALF, (b + 1) * HALF)
                        rhs_hi, rhs_lo = (hT_hi, hT_lo) if r < 2 else (ypT_hi, ypT_lo)
                        for kk in range(KT):
                            mm = product(pe, pair[i % 2][b][:], w_hi[:, i % RAW, kk, :], w_lo[:, i % RAW, kk, :],
                                         rhs_hi[:, kk, half], rhs_lo[:, kk, half], kk == 0, kk == KT - 1)
                        mm.then_inc(gb_done, 1)
                    pe.wait_ge(gb_done, p * (2 * NI) + 2 * i + 2)
                    pe.sem_inc(w_used, 1)
    return u, u_at



def phase_mix(nc, kept, a, dram, u, u_at):
    fixed = kept.end
    sb = Arena(nc, "p4", fixed)
    u_hi = sb("u_hi", [P, KT, T], F32R)
    u_lo = sb("u_lo", [P, KT, T], F32R)
    w_hi = sb("w_hi", [P, KT, D], F32R)
    w_lo = sb("w_lo", [P, KT, D], F32R)
    RAW = 2
    raw = sb("raw", [P, RAW, D])
    g1, gs2, sh2 = (sb(n, [P, D]) for n in ("g1", "gs2", "sh2"))
    x = sb("x", [P, D])
    h2 = sb("h2", [P, 2, D])
    h2T = sb("h2T", [P, KT, P])
    assert sb.at <= u_at
    x1 = sb("x1", [P, TT, D], at=u_at)
    sb.at = u_at + TT * D * 4
    NR = MG + NE
    rw = sb("rw", [P, KT, NR])
    rb = sb("rb", [P, NR])
    ss, var, std, rstd = (sb(n, [P, TT]) for n in ("ss", "var", "std", "rstd"))
    with ExitStack() as ctx:
        sem = lambda n: nc.alloc_semaphore("p4_" + n)
        ps = lambda n: ctx.enter_context(nc.psum_tensor("p4_" + n, [P, HALF], F32))
        pair = [[ps("pair00"), ps("pair01")], [ps("pair10"), ps("pair11")]]
        ps_t = [ps("t0"), ps("t1")]
        ps_r = ps("r")
        w_in = [sem(f"w_in{i}") for i in range(RAW)]
        par_in, x_in, hi_made, lo_made, uh_made, ul_made, sc_made = (sem(n) for n in
            ("par_in", "x_in", "hi_made", "lo_made", "uh_made", "ul_made", "sc_made"))
        done, x1_made, squared, var_made, std_made, h2_made, turned, h2T_made, routed = (sem(n) for n in
            ("done", "x1_made", "squared", "var_made", "std_made", "h2_made", "turned", "h2T_made", "routed"))
        h2_out = [sem(f"h2_out{i}") for i in range(2)]
        seq = sem("seq")
        blk = ctx.enter_context(nc.Block())

        @blk.sync
        def _(sp):
            for k in range(KT):
                if k >= RAW:
                    sp.wait_ge(lo_made, k - RAW + 1)
                sp.dma_start(raw[:, k % RAW], a["w_out"][0, k * P:(k + 1) * P, :]).then_inc(w_in[k % RAW], 16)
            for i in range(TT):
                if i:
                    sp.wait_ge(x1_made, i)
                sp.dma_start(x[:], a["x"][0, i * P:(i + 1) * P, :]).then_inc(x_in, 16)

        @blk.gpsimd
        def _(pool):
            mod = dram["mod"]
            pool.dma_start(g1[:], mod[0, 0:D].partition_broadcast(P)).then_inc(par_in, 16)
            pool.dma_start(sh2[:], mod[0, D:2 * D].partition_broadcast(P)).then_inc(par_in, 16)
            pool.dma_start(gs2[:], mod[0, 2 * D:3 * D].partition_broadcast(P)).then_inc(par_in, 16)
            pool.dma_start(h2[:, 0], a["norm2_g"][0].partition_broadcast(P)).then_inc(par_in, 16)
            pool.dma_start(rw[:, :, 0:MG], a["router_group_w"][0].rearrange("(k p) n -> p k n", p=P)).then_inc(par_in, 16)
            pool.dma_start(rw[:, :, MG:], a["router_expert_w"][0].rearrange("(k p) n -> p k n", p=P)).then_inc(par_in, 16)
            pool.dma_start(rb[:, 0:MG], a["router_group_b"][0].partition_broadcast(P)).then_inc(par_in, 16)
            pool.dma_start(rb[:, MG:], a["router_expert_b"][0].partition_broadcast(P)).then_inc(par_in, 16)
            for k in range(KT):
                pool.wait_ge(hi_made, k + 1)
                pool.tensor_tensor(w_lo[:, k], raw[:, k % RAW], w_hi[:, k].bitcast(F32), ALU.subtract).then_inc(lo_made, 1)
            for i in range(TT):
                pool.wait_ge(h2_made, i + 1)
                pool.dma_start(dram["h2"][i * P:(i + 1) * P, :], h2[:, i % 2]).then_inc(h2_out[i % 2], 16)
            for i in range(2):
                pool.wait_ge(h2_out[i], 16 * TT // 2)

        @blk.scalar
        def _(act):
            for k in range(KT):
                act.activation(u_hi[:, k], u[:, k], ACT.Copy, scale=0.5).then_inc(uh_made, 1)
                act.wait_ge(w_in[k % RAW], 16 * (k // RAW + 1))
                act.activation(w_hi[:, k], raw[:, k % RAW], ACT.Copy).then_inc(hi_made, 1)
            for i in range(TT):
                act.wait_ge(x1_made, i + 1)
                act.activation(h2[:, i % 2], x1[:, i], ACT.Square, accum_out=ss[:, i:i + 1]).then_inc(squared, 1)
                act.wait_ge(var_made, i + 1)
                act.activation(std[:, i:i + 1], var[:, i:i + 1], ACT.Sqrt).then_inc(std_made, 1)
                if i >= 1:
                    for b in range(2):
                        act.wait_ge(turned, 2 * (i - 1) + b + 1)
                        if b == 0 and i >= 2:
                            act.wait_ge(routed, i - 1)
                        act.activation(h2T[:, 4 * b:4 * b + 4], ps_t[b][:].rearrange("p (k t) -> p k t", t=P),
                                       ACT.Copy).then_inc(h2T_made, 1)
            for b in range(2):
                act.wait_ge(turned, 2 * (TT - 1) + b + 1)
                if b == 0:
                    act.wait_ge(routed, TT - 1)
                act.activation(h2T[:, 4 * b:4 * b + 4], ps_t[b][:].rearrange("p (k t) -> p k t", t=P),
                               ACT.Copy).then_inc(h2T_made, 1)

        @blk.vector
        def _(dve):
            link = Chain(dve, seq)
            for k in range(KT):
                dve.wait_ge(uh_made, k + 1)
                dve.scalar_tensor_tensor(u_lo[:, k], u[:, k], 0.5, u_hi[:, k].bitcast(F32),
                                         ALU.mult, ALU.subtract).then_inc(ul_made, 1)
            dve.wait_ge(par_in, 16 * 8)
            link(dve.scalar_tensor_tensor(gs2[:], gs2[:], 1.0, h2[:, 0], ALU.add, ALU.mult))
            for i in range(TT):
                if i >= 2:
                    dve.wait_ge(h2_out[i % 2], 16 * (i // 2))
                    dve.wait_ge(turned, 2 * (i - 2) + 2)
                for b in range(2):
                    half = slice(b * HALF, (b + 1) * HALF)
                    dve.wait_ge(done, 2 * i + b + 1)
                    link(dve.tensor_tensor(h2[:, i % 2, half], pair[i % 2][b][:], g1[:, half], ALU.mult))
                dve.wait_ge(x_in, 16 * (i + 1))
                dve.tensor_tensor(x1[:, i], h2[:, i % 2], x[:], ALU.add).then_inc(x1_made, 1)
                dve.wait_ge(squared, i + 1)
                dve.tensor_scalar(var[:, i:i + 1], ss[:, i:i + 1], 1.0 / D, EPS, ALU.mult, ALU.add).then_inc(var_made, 1)
                dve.wait_ge(std_made, i + 1)
                link(dve.reciprocal(rstd[:, i:i + 1], std[:, i:i + 1]))
                link(dve.scalar_tensor_tensor(h2[:, i % 2], x1[:, i], rstd[:, i:i + 1], gs2[:], ALU.mult, ALU.mult))
                dve.tensor_tensor(h2[:, i % 2], h2[:, i % 2], sh2[:], ALU.add).then_inc(h2_made, 1)
            dve.wait_ge(routed, TT)
            dve.tensor_tensor(kept.logits[:], ps_r[:, 0:TT * NR].rearrange("p (t n) -> p t n", n=NR),
                              bc(rb[:].unsqueeze(1), [P, TT, NR]), ALU.add)

        @blk.tensor
        def _(pe):
            def turn(i):
                pe.wait_ge(h2_made, i + 1)
                if i:
                    pe.wait_ge(h2T_made, 2 * i)
                for k in range(KT):
                    mm = pe.transpose(ps_t[k // 4][:, (k % 4) * P:(k % 4 + 1) * P], h2[:, i % 2, k * P:(k + 1) * P],
                                      kept.ident[:])
                    if k % 4 == 3:
                        mm.then_inc(turned, 1)

            def route(i):
                pe.wait_ge(h2T_made, 2 * i + 2)
                for k in range(KT):
                    mm = pe.matmul(ps_r[:, i * NR:(i + 1) * NR], h2T[:, k, :], rw[:, k, :],
                                   start=(k == 0), stop=(k == KT - 1))
                mm.then_inc(routed, 1)

            pe.wait_ge(ul_made, KT)
            pe.wait_ge(lo_made, KT)
            pe.wait_ge(par_in, 16 * 8)
            for i in range(TT):
                if i >= 2:
                    pe.wait_ge(x1_made, i - 1)
                rows = slice(i * P, (i + 1) * P)
                for b in range(2):
                    half = slice(b * HALF, (b + 1) * HALF)
                    for k in range(KT):
                        mm = product(pe, pair[i % 2][b][:], u_hi[:, k, rows], u_lo[:, k, rows],
                                     w_hi[:, k, half], w_lo[:, k, half], k == 0, k == KT - 1)
                    mm.then_inc(done, 1)
                if i >= 1:
                    turn(i - 1)
                if i >= 2:
                    route(i - 2)
            route(TT - 2)
            turn(TT - 1)
            route(TT - 1)
    return x1


def phase_route(nc, kept, a, dram):
    sb = Arena(nc, "p5", kept.end)
    E3 = [P, TT, NE]
    G3 = [P, TT, MG]
    X3 = [P, TT, EPG]
    rev = sb("rev", [P, 1, EPG])
    gmax, gsum, gw = (sb(n, [P, TT, 1]) for n in ("gmax", "gsum", "gw"))
    glog, gexp, gone = (sb(n, G3) for n in ("glog", "gexp", "gone"))
    e_in, e_two, prod, one0, one1 = (sb(n, X3) for n in ("e_in", "e_two", "prod", "one0", "one1"))
    m0, m1, first, ratio = (sb(n, [P, TT, 1]) for n in ("m0", "m1", "first", "ratio"))
    hot = [sb(f"hot{k}", E3) for k in range(2)]
    both = sb("both", E3, BF16)
    where, slot_f = sb("where", E3), sb("slot_f", [P, TT])
    base = sb("base", [P, NE])
    count_f, count_i, blocks_f = sb("count_f", [NE, 1]), sb("count_i", [NE, 1], I32), sb("blocks_f", [NE, 1])
    blocks_bf = sb("blocks_bf", [NE, P], BF16)
    ends, block_no, past = sb("ends", [NE, 1]), sb("block_no", [NE, MAX_BLOCKS + 1]), sb("past", [NE, MAX_BLOCKS + 1])
    h2 = sb("h2", [P, TT, D])
    logits = kept.logits
    with ExitStack() as ctx:
        sem = lambda n: nc.alloc_semaphore("p5_" + n)
        ps = lambda n: ctx.enter_context(nc.psum_tensor("p5_" + n, [P, HALF], F32))
        ps_pos, ps_cnt, ps_base = ps("pos"), ps("cnt"), ps("base")
        h2_in = [sem(f"h2_in{i}") for i in range(TT)]
        iotas, seq, top_made, gexp_made, ratio_in, ratio_made = (sem(n) for n in
            ("iotas", "seq", "top_made", "gexp_made", "ratio_in", "ratio_made"))
        both_made, counted, placed, blocks_made, based, past_made, tabled, slots_made, scattered = (sem(n) for n in
            ("both_made", "counted", "placed", "blocks_made", "based", "past_made", "tabled", "slots_made", "scattered"))
        blk = ctx.enter_context(nc.Block())

        @blk.sync
        def _(sp):
            for i in range(TT):
                sp.dma_start(h2[:, i], dram["h2"][i * P:(i + 1) * P, :]).then_inc(h2_in[i], 16)

        @blk.gpsimd
        def _(pool):
            pool.iota(rev[:], pattern=[[-1, EPG]], base=EPG, channel_multiplier=0,
                      allow_small_or_imprecise_dtypes=True).then_inc(iotas, 1)
            pool.iota(block_no[:], pattern=[[1, MAX_BLOCKS + 1]], base=0, channel_multiplier=0,
                      allow_small_or_imprecise_dtypes=True).then_inc(iotas, 1)
            pool.wait_ge(slots_made, 2)
            for i in range(TT):
                pool.wait_ge(h2_in[i], 16)
                for k in range(2):
                    pool.indirect_dma_start(out=dram["x_buf"], out_offset=bass.IndirectOffsetOnAxis(ap=kept.slot[k][:, i:i + 1], axis=0),
                                            in_=h2[:, i], in_offset=None).then_inc(scattered, 16)
            pool.wait_ge(scattered, 16 * 2 * TT)

        @blk.scalar
        def _(act):
            act.wait_ge(top_made, 1)
            act.activation(gexp[:], glog[:], ACT.Exp).then_inc(gexp_made, 1)
            act.wait_ge(ratio_in, 1)
            act.activation(ratio[:], m1[:], ACT.Exp).then_inc(ratio_made, 1)

        @blk.vector
        def _(dve):
            link = Chain(dve, seq)
            TE = [P, TT, EPG]

            def first_hot(out, values, top, n):
                link(dve.tensor_reduce(top[:], values, AX.X, ALU.max))
                link(dve.tensor_tensor(out, values, bc(top[:], [P, TT, n]), ALU.is_equal))
                link(dve.tensor_tensor(out, out, bc(rev[:, :, 0:n], [P, TT, n]), ALU.mult))
                link(dve.tensor_reduce(first[:], out, AX.X, ALU.max))
                link(dve.tensor_tensor(out, out, bc(first[:], [P, TT, n]), ALU.is_equal))

            dve.wait_ge(iotas, 2)
            lg = logits[:, :, 0:MG]
            first_hot(gone[:], lg, gmax, MG)
            dve.tensor_tensor(glog[:], lg, bc(gmax[:], G3), ALU.subtract).then_inc(top_made, 1)
            for g in range(MG):
                le = logits[:, :, MG + g * EPG:MG + (g + 1) * EPG]
                out = e_in if g == 0 else prod
                link(dve.tensor_tensor(out[:], le, bc(gone[:, :, g:g + 1], TE), ALU.mult))
                if g:
                    link(dve.tensor_tensor(e_in[:], e_in[:], prod[:], ALU.add))
            first_hot(one0[:], e_in[:], m0, EPG)
            link(dve.scalar_tensor_tensor(e_two[:], one0[:], NEG, e_in[:], ALU.mult, ALU.add))
            first_hot(one1[:], e_two[:], m1, EPG)
            dve.tensor_tensor(m1[:], m1[:], m0[:], ALU.subtract).then_inc(ratio_in, 1)
            for k, one in enumerate((one0, one1)):
                for g in range(MG):
                    ins = dve.tensor_tensor(hot[k][:, :, g * EPG:(g + 1) * EPG], one[:], bc(gone[:, :, g:g + 1], TE), ALU.mult)
            link(ins)
            dve.tensor_tensor(both[:], hot[0][:], hot[1][:], ALU.add).then_inc(both_made, 1)
            dve.wait_ge(gexp_made, 1)
            link(dve.tensor_reduce(gsum[:], gexp[:], AX.X, ALU.add))
            dve.wait_ge(ratio_made, 1)
            link(dve.scalar_tensor_tensor(gw[:], ratio[:], 1.0, gsum[:], ALU.add, ALU.mult))
            link(dve.reciprocal(kept.weight[0][:], gw[:].rearrange("p t o -> p (t o)")))
            link(dve.tensor_tensor(kept.weight[1][:], ratio[:].rearrange("p t o -> p (t o)"), kept.weight[0][:], ALU.mult))
            dve.wait_ge(counted, 1)
            link(dve.tensor_scalar(count_f[:], ps_cnt[0:NE, 0:1], float(BLOCK - 1), None, ALU.add))
            link(dve.tensor_copy(count_i[:], count_f[:]))
            link(dve.tensor_scalar(count_i[:], count_i[:], BLOCK.bit_length() - 1, None, ALU.arith_shift_right))
            link(dve.tensor_copy(blocks_f[:], count_i[:]))
            dve.tensor_copy(blocks_bf[:], bc(blocks_f[:], [NE, P])).then_inc(blocks_made, 1)
            dve.wait_ge(based, 1)
            link(dve.tensor_copy(base[:], ps_base[:, 0:NE]))
            link(dve.tensor_copy(ends[:], ps_base[0:NE, NE:NE + 1]))
            dve.tensor_scalar(past[:], block_no[:], ends[:], None, ALU.is_ge).then_inc(past_made, 1)
            dve.wait_ge(placed, 1)
            link(dve.scalar_tensor_tensor(where[:], bc(base[:].unsqueeze(1), E3), float(BLOCK),
                                          ps_pos[:, 0:TT * NE].rearrange("p (t n) -> p t n", n=NE), ALU.mult, ALU.add))
            for k in range(2):
                link(dve.tensor_tensor(hot[k][:], hot[k][:], where[:], ALU.mult))
                link(dve.tensor_reduce(slot_f[:], hot[k][:], AX.X, ALU.add))
                dve.tensor_copy(kept.slot[k][:], slot_f[:]).then_inc(slots_made, 1)
                dve.wait_ge(slots_made, k + 1)
            dve.wait_ge(tabled, 1)
            dve.tensor_scalar(kept.table[0:1, 0:MAX_BLOCKS + 1], ps_cnt[0:1, 64:64 + MAX_BLOCKS + 1], float(NE - 1), None, ALU.min)
            dve.tensor_scalar(kept.table[0:1, MAX_BLOCKS + 1:MAX_BLOCKS + 2], ps_cnt[0:1, 192:193], -2.0, None, ALU.add)

        @blk.tensor
        def _(pe):
            pe.wait_ge(both_made, 1)
            for i in range(TT):
                mm = pe.matmul(ps_cnt[0:NE, 0:1], both[:, i, :], kept.ones_bf[:, 0:1], start=(i == 0), stop=(i == TT - 1))
            mm.then_inc(counted, 1)
            for i in range(TT):
                out = ps_pos[:, i * NE:(i + 1) * NE]
                for j in range(i):
                    pe.matmul(out, kept.ones_bf[:], both[:, j, :], start=(j == 0), stop=False)
                mm = pe.matmul(out, kept.tri_strict[:], both[:, i, :], start=(i == 0), stop=True)
            mm.then_inc(placed, 1)
            pe.wait_ge(blocks_made, 1)
            pe.matmul(ps_base[:, 0:NE], blocks_bf[:], kept.tri_strict[0:NE, 0:NE], start=True, stop=True)
            pe.matmul(ps_base[0:NE, NE:NE + 1], kept.tri[0:NE, 0:NE], blocks_f[:], start=True, stop=True).then_inc(based, 1)
            pe.wait_ge(past_made, 1)
            pe.matmul(ps_cnt[0:1, 64:64 + MAX_BLOCKS + 1], kept.ones[0:NE, 0:1], past[:], start=True, stop=True)
            pe.matmul(ps_cnt[0:1, 192:193], blocks_f[:], kept.ones[0:NE, 0:1], start=True, stop=True).then_inc(tabled, 1)


def phase_experts(nc, kept, a, dram):
    sb = Arena(nc, "p6", kept.end)
    FT = FF // P
    NP = KT + FT
    NS = 6
    MIN_BLOCKS = 2 * T // BLOCK
    raw = sb("raw", [P, NP, D])
    w_hi = sb("w_hi", [P, NS, D], F32R)
    w_lo = sb("w_lo", [P, NS, D], F32R)
    xb = sb("xb", [P, D])
    xT_hi = sb("xT_hi", [P, KT, P], F32R)
    xT_lo = sb("xT_lo", [P, KT, P], F32R)
    th = sb("th", [P, FF])
    s = sb("s", [P, FF])
    sT_hi = sb("sT_hi", [P, FT, P], F32R)
    sT_lo = sb("sT_lo", [P, FT, P], F32R)
    yb = sb("yb", [P, D])
    g2 = sb("g2", [P, D])
    with ExitStack() as ctx:
        sem = lambda n: nc.alloc_semaphore("p6_" + n)
        ps = lambda n: ctx.enter_context(nc.psum_tensor("p6_" + n, [P, HALF], F32))
        ps_a, ps_g, ps_s = ps("a"), ps("g"), ps("s")
        ps_x = [ps("x0"), ps("x1")]
        ps_y = [ps("y0"), ps("y1")]
        w_in = [sem(f"w_in{i}") for i in range(NP)]
        x_in, y_out, g2_in = sem("x_in"), sem("y_out"), sem("g2_in")
        hi_made, lo_made, used, x_turned, xh_made, xl_made, th_made, t_made, s_made = (sem(n) for n in
            ("hi_made", "lo_made", "used", "x_turned", "xh_made", "xl_made", "th_made", "t_made", "s_made"))
        s_turned, sh_made, sl_made, y_read, y_scaled, y_stored = (sem(n) for n in
            ("s_turned", "sh_made", "sl_made", "y_read", "y_scaled", "y_stored"))
        Y_CREDIT = 2
        blk = ctx.enter_context(nc.Block())

        def passes(eng):
            return eng.value_load(kept.table[0:1, MAX_BLOCKS + 1:MAX_BLOCKS + 2], min_val=MIN_BLOCKS - 2,
                                  max_val=MAX_BLOCKS - 2)

        def raw_slot(i):
            return (KT + i) % NP

        def split_slot(i):
            return (KT + i) % NS

        def after(j, i):
            return j * NP + (KT + i + 1)

        @blk.sync
        def _(sp):
            n = passes(sp)
            x_rows = dram["x_buf"].rearrange("(b p) d -> p b d", p=P)

            def expert(j):
                return sp.value_load(kept.table[0:1, bass.ds(j, 1)], min_val=0, max_val=NE - 1)

            def load_w13(e, i, k):
                sp.dma_start(raw[:, raw_slot(i)], a["w13"][0, bass.ds(e, 1), k * P:(k + 1) * P, :]
                             .rearrange("e p n -> p (e n)")).then_inc(w_in[raw_slot(i)], 16)

            def load_w2(e, i, k):
                sp.dma_start(raw[:, raw_slot(i)], a["w2"][0, bass.ds(e, 1), k * P:(k + 1) * P, :]
                             .rearrange("e p n -> p (e n)")).then_inc(w_in[raw_slot(i)], 16)

            def slot_free(j, i):
                sp.wait_ge(lo_made, after(j, i - NP))

            sp.dma_start(xb[:], x_rows[:, 0, :]).then_inc(x_in, 16)
            e = expert(0)
            for k in range(KT):
                load_w13(e, k - KT, k)
            e = expert(1)
            for k in range(FT):
                load_w13(e, k, k)
            sp.wait_ge(x_turned, 2)
            sp.dma_start(xb[:], x_rows[:, 1, :]).then_inc(x_in, 16)
            with sp.Fori(0, n) as j:
                e = expert(j + 1)
                for i in range(FT, KT):
                    slot_free(j, i)
                    load_w13(e, i, i)
                e = expert(j)
                for i in range(KT, NP):
                    slot_free(j, i)
                    load_w2(e, i, i - KT)
                sp.wait_ge(x_turned, 2 * j + 4)
                sp.dma_start(xb[:].unsqueeze(1), x_rows[:, bass.ds(j + 2, 1), :]).then_inc(x_in, 16)
                e = expert(j + 2)
                for i in range(FT):
                    slot_free(j + 1, i)
                    load_w13(e, i, i)
            e = expert(n + 1)
            for i in range(FT, KT):
                slot_free(n, i)
                load_w13(e, i, i)
            e = expert(n)
            for i in range(KT, NP):
                slot_free(n, i)
                load_w2(e, i, i - KT)
            e = expert(n + 1)
            for i in range(FT):
                slot_free(n + 1, i)
                load_w2(e, i, i)

        @blk.gpsimd
        def _(pool):
            pool.dma_start(g2[:], dram["mod"][0, 3 * D:4 * D].partition_broadcast(P)).then_inc(g2_in, 16)
            pool.sem_inc(y_stored, 1)
            n = passes(pool)
            y_rows = dram["x_buf"].rearrange("(b p) d -> p b d", p=P)
            pool.wait_ge(g2_in, 16)

            with pool.Fori(0, n + 2) as j:
                pool.wait_ge(y_read, 2 * j + 2 + Y_CREDIT)
                pool.tensor_tensor(yb[:], yb[:], g2[:], ALU.mult).then_inc(y_scaled, 1)
                pool.wait_ge(y_scaled, j + 1)
                pool.dma_start(y_rows[:, bass.ds(j, 1), :], yb[:].unsqueeze(1)).then_inc(y_out, 16)
                pool.wait_ge(y_out, j * 16 + 16)
                pool.sem_inc(y_stored, 1)

        @blk.scalar
        def _(act):
            n = passes(act)

            def hi(j, i):
                slot = raw_slot(i)
                act.wait_ge(w_in[slot], (j + (KT + i) // NP) * 16 + 16)
                if not (isinstance(j, int) and after(j, i) <= NS):
                    act.wait_ge(used, after(j, i - NS))
                act.activation(w_hi[:, split_slot(i)], raw[:, slot], ACT.Copy).then_inc(hi_made, 1)

            def x_hi(j):
                for b in range(2):
                    act.wait_ge(x_turned, 2 * j + (b + 1))
                    act.activation(xT_hi[:, 4 * b:4 * b + 4], ps_x[b][:].rearrange("p (k t) -> p k t", t=P),
                                   ACT.Copy).then_inc(xh_made, 1)

            def gate(j, p, last):
                act.wait_ge(used, after(p, last))
                act.activation(th[:], ps_a[:], ACT.Tanh, scale=0.5).then_inc(th_made, 1)

            def s_hi(j):
                act.wait_ge(s_turned, j + 1)
                act.activation(sT_hi[:], ps_s[:].rearrange("p (k t) -> p k t", t=P), ACT.Copy).then_inc(sh_made, 1)

            def y_copy(j, p, last):
                act.wait_ge(used, after(p, last))
                act.wait_ge(y_stored, j + 1)
                for b in range(2):
                    act.activation(yb[:, b * HALF:(b + 1) * HALF], ps_y[b][:], ACT.Copy).then_inc(y_read, 1)

            act.sem_inc(y_read, Y_CREDIT)
            for i in range(-KT, NS - KT):
                hi(0, i)
            x_hi(0)
            for i in range(NS - KT, NS - FT):
                hi(0, i)
            gate(0, 0, -1)
            x_hi(1)
            for i in range(NS - FT, NS):
                hi(0, i)
            with act.Fori(0, n) as j:
                s_hi(j)
                for i in range(NS, KT + NS):
                    hi(j, i)
                gate(j + 1, j, KT - 1)
                x_hi(j + 2)
                for i in range(KT + NS, NP + NS):
                    hi(j, i)
                y_copy(j, j, NP - 1)
            s_hi(n)
            for i in range(NS, KT + NS):
                hi(n, i)
            gate(n + 1, n, KT - 1)
            for i in range(KT + NS, NP + FT):
                hi(n, i)
            y_copy(n, n, NP - 1)
            s_hi(n + 1)
            y_copy(n + 1, n + 1, FT - 1)

        @blk.vector
        def _(dve):
            n = passes(dve)

            def lo(j, i):
                dve.wait_ge(hi_made, after(j, i))
                dve.tensor_tensor(w_lo[:, split_slot(i)], raw[:, raw_slot(i)], w_hi[:, split_slot(i)].bitcast(F32),
                                  ALU.subtract).then_inc(lo_made, 1)

            def x_lo(j):
                for b in range(2):
                    dve.wait_ge(xh_made, 2 * j + (b + 1))
                    ks = slice(4 * b, 4 * b + 4)
                    dve.tensor_tensor(xT_lo[:, ks], ps_x[b][:].rearrange("p (k t) -> p k t", t=P),
                                      xT_hi[:, ks].bitcast(F32), ALU.subtract).then_inc(xl_made, 1)

            def gate(j):
                dve.wait_ge(th_made, j + 1)
                dve.scalar_tensor_tensor(th[:], th[:], 1.0, ps_a[:], ALU.add, ALU.mult).then_inc(t_made, 1)
                dve.wait_ge(t_made, j + 1)
                dve.scalar_tensor_tensor(s[:], th[:], 0.5, ps_g[:], ALU.mult, ALU.mult).then_inc(s_made, 1)

            def s_lo(j):
                dve.wait_ge(sh_made, j + 1)
                dve.tensor_tensor(sT_lo[:], ps_s[:].rearrange("p (k t) -> p k t", t=P), sT_hi[:].bitcast(F32),
                                  ALU.subtract).then_inc(sl_made, 1)

            for i in range(-KT, NS - KT):
                lo(0, i)
            x_lo(0)
            for i in range(NS - KT, NS - FT):
                lo(0, i)
            gate(0)
            x_lo(1)
            for i in range(NS - FT, NS):
                lo(0, i)
            with dve.Fori(0, n) as j:
                s_lo(j)
                for i in range(NS, KT + NS):
                    lo(j, i)
                gate(j + 1)
                x_lo(j + 2)
                for i in range(KT + NS, NP + NS):
                    lo(j, i)
            s_lo(n)
            for i in range(NS, KT + NS):
                lo(n, i)
            gate(n + 1)
            for i in range(KT + NS, NP + FT):
                lo(n, i)
            s_lo(n + 1)

        @blk.tensor
        def _(pe):
            n = passes(pe)

            def turn_x(j):
                pe.wait_ge(x_in, j * 16 + 16)
                for k in range(KT):
                    mm = pe.transpose(ps_x[k // 4][:, (k % 4) * P:(k % 4 + 1) * P], xb[:, k * P:(k + 1) * P], kept.ident[:])
                    if k % 4 == 3:
                        mm.then_inc(x_turned, 1)

            def turn_s(j):
                pe.wait_ge(s_made, j + 1)
                for k in range(FT):
                    mm = pe.transpose(ps_s[:, k * P:(k + 1) * P], s[:, k * P:(k + 1) * P], kept.ident[:])
                mm.then_inc(s_turned, 1)

            def up(j, p, first):
                for k in range(KT):
                    if k % 4 == 0:
                        pe.wait_ge(xl_made, j * 2 + (k // 4 + 1))
                    pe.wait_ge(lo_made, after(p, first + k))
                    for b, out in enumerate((ps_a, ps_g)):
                        half = slice(b * HALF, (b + 1) * HALF)
                        slot = split_slot(first + k)
                        mm = product(pe, out[:], xT_hi[:, k], xT_lo[:, k], w_hi[:, slot, half], w_lo[:, slot, half],
                                     k == 0, k == KT - 1)
                    mm.then_inc(used, 1)

            def down(j, first, p):
                pe.wait_ge(sl_made, j + 1)
                pe.wait_ge(y_read, 2 * j + Y_CREDIT)
                for k in range(FT):
                    pe.wait_ge(lo_made, after(p, first + k))
                    slot = split_slot(first + k)
                    for b in range(2):
                        half = slice(b * HALF, (b + 1) * HALF)
                        mm = product(pe, ps_y[b][:], sT_hi[:, k], sT_lo[:, k], w_hi[:, slot, half], w_lo[:, slot, half],
                                     k == 0, k == FT - 1)
                    mm.then_inc(used, 1)

            turn_x(0)
            up(0, 0, -KT)
            turn_x(1)
            with pe.Fori(0, n) as j:
                turn_s(j)
                up(j + 1, j, 0)
                turn_x(j + 2)
                down(j, KT, j)
            turn_s(n)
            up(n + 1, n, 0)
            down(n, KT, n)
            turn_s(n + 1)
            down(n + 1, 0, n + 1)

def phase_combine(nc, kept, a, dram, x1, out):
    sb = Arena(nc, "p7", kept.end)
    R = 3
    y0, y1 = sb("y0", [P, R, D]), sb("y1", [P, R, D])
    sq = sb("sq", [P, 2, D])
    gf = sb("gf", [P, D])
    res = sb("res", [P, 2, D])
    ss, var, std, rstd = (sb(n, [P, TT]) for n in ("ss", "var", "std", "rstd"))
    with ExitStack() as ctx:
        sem = lambda n: nc.alloc_semaphore("p7_" + n)
        y_in = [[sem(f"y_in{k}{i}") for i in range(R)] for k in range(2)]
        res_out = [sem(f"res_out{i}") for i in range(2)]
        gf_in, seq, used0, used1, x2_made, squared, var_made, std_made, res_made = (sem(n) for n in
            ("gf_in", "seq", "used0", "used1", "x2_made", "squared", "var_made", "std_made", "res_made"))
        blk = ctx.enter_context(nc.Block())

        @blk.sync
        def _(sp):
            sp.dma_start(gf[:], a["final_norm_g"].partition_broadcast(P)).then_inc(gf_in, 16)
            for i in range(TT):
                sp.wait_ge(res_made, i + 1)
                sp.dma_start(out[0, i * P:(i + 1) * P, :], res[:, i % 2]).then_inc(res_out[i % 2], 16)
            for i in range(2):
                sp.wait_ge(res_out[i], 16 * TT // 2)

        @blk.gpsimd
        def _(pool):
            for i in range(TT):
                if i >= R:
                    pool.wait_ge(x2_made, i - R + 1)
                for k, y in enumerate((y0, y1)):
                    pool.indirect_dma_start(out=y[:, i % R], out_offset=None, in_=dram["x_buf"],
                                            in_offset=bass.IndirectOffsetOnAxis(ap=kept.slot[k][:, i:i + 1], axis=0)
                                            ).then_inc(y_in[k][i % R], 16)

        @blk.scalar
        def _(act):
            for i in range(TT):
                act.wait_ge(x2_made, i + 1)
                if i >= 2:
                    act.wait_ge(squared, i - 1)
                act.activation(sq[:, i % 2], x1[:, i], ACT.Square, accum_out=ss[:, i:i + 1]).then_inc(squared, 1)
                act.wait_ge(var_made, i + 1)
                act.activation(std[:, i:i + 1], var[:, i:i + 1], ACT.Sqrt).then_inc(std_made, 1)

        @blk.vector
        def _(dve):
            link = Chain(dve, seq)

            def norm(i):
                dve.wait_ge(squared, i + 1)
                dve.tensor_scalar(var[:, i:i + 1], ss[:, i:i + 1], 1.0 / D, EPS, ALU.mult, ALU.add).then_inc(var_made, 1)
                dve.wait_ge(std_made, i + 1)
                link(dve.reciprocal(rstd[:, i:i + 1], std[:, i:i + 1]))
                if i >= 2:
                    dve.wait_ge(res_out[i % 2], 16 * (i // 2))
                dve.scalar_tensor_tensor(res[:, i % 2], x1[:, i], rstd[:, i:i + 1], gf[:], ALU.mult, ALU.mult).then_inc(res_made, 1)

            dve.wait_ge(gf_in, 16)
            for i in range(TT):
                dve.wait_ge(y_in[0][i % R], 16 * (i // R + 1))
                link(dve.scalar_tensor_tensor(x1[:, i], y0[:, i % R], kept.weight[0][:, i:i + 1], x1[:, i], ALU.mult, ALU.add))
                dve.wait_ge(y_in[1][i % R], 16 * (i // R + 1))
                dve.scalar_tensor_tensor(x1[:, i], y1[:, i % R], kept.weight[1][:, i:i + 1], x1[:, i],
                                         ALU.mult, ALU.add).then_inc(x2_made, 1)
                if i:
                    norm(i - 1)
            norm(TT - 1)


def build(nc, a, out, stop=9):
    dram = {
        "mod": nc.dram_tensor("mod_rows", (1, 4 * D), F32).ap(),
        "acs": nc.dram_tensor("acs_rows", (HEADS, T), F32).ap(),
        "small": nc.dram_tensor("small_by_group", (P, GROUPS, 5 * TT, GH), F32).ap(),
        "acc": nc.dram_tensor("acc_ssd", (P, KT, T), F32).ap(),
        "h2": nc.dram_tensor("h2_rows", (T, D), F32).ap(),
        "x_buf": nc.dram_tensor("x_buf", ((MAX_BLOCKS + 1) * BLOCK, D), F32).ap(),
    }
    kept = Kept(nc)
    with nc.cleanup_on_exit():
        hT_hi, hT_lo = phase_modulate(nc, kept, a, dram)
        phase_steps(nc, kept, a, dram, hT_hi, hT_lo)
        phase_ssd(nc, kept, a, dram, hT_hi, hT_lo)
    u, u_at = phase_pool(nc, kept, a, dram, hT_hi, hT_lo)
    x1 = phase_mix(nc, kept, a, dram, u, u_at)
    phase_route(nc, kept, a, dram)
    phase_experts(nc, kept, a, dram)
    phase_combine(nc, kept, a, dram, x1, out)


NAMES = ["x", "c", "ada_w", "ada_b", "norm1_g", "w_in", "pool_w", "pool_scale", "conv_w", "conv_b", "dt_bias", "a_log",
         "d_skip", "ssd_norm_g", "w_branch_pool", "w_branch_ssd", "w_out", "norm2_g", "router_group_w",
         "router_group_b", "router_expert_w", "router_expert_b", "w13", "w2", "final_norm_g"]


def kernel(**inputs):
    import concourse.bacc as bacc
    from concourse.bass_utils import run_bass_kernel_spmd

    nc = bacc.Bacc("TRN2", target_bir_lowering=False, num_devices=1)
    arrays, aps = {}, {}
    for name in NAMES:
        value = np.ascontiguousarray(inputs[name])
        arrays[f"in_{name}"] = value
        aps[name] = nc.dram_tensor(f"in_{name}", value.shape, mybir.dt.from_np(value.dtype), kind="ExternalInput").ap()
    out = nc.dram_tensor("out_0", (1, T, D), F32, kind="ExternalOutput").ap()
    build(nc, aps, out)
    return run_bass_kernel_spmd(nc, [arrays], core_ids=[0]).results[0]["out_0"]
```

```python
from contextlib import ExitStack

import numpy as np

import concourse.bass as bass
from concourse import mybir

F32 = mybir.dt.float32
F32R = mybir.dt.float32r
BF16 = mybir.dt.bfloat16
U32 = mybir.dt.uint32
I32 = mybir.dt.int32
ALU = mybir.AluOpType
ACT = mybir.ActivationFunctionType
AX = mybir.AxisListType

P = 128
D = 1024
T = 1024
KT = D // P
TT = T // P
HALF = 512
HEADS = 32
HEAD_DIM = 64
GROUPS = 4
GH = HEADS // GROUPS
INNER = HEADS * HEAD_DIM
STATE = 128
CONV = 4
CONV_TILES = (INNER + 2 * GROUPS * STATE) // P
COL_Z = D
COL_X = COL_Z + INNER
COL_B = COL_X + INNER
COL_C = COL_B + GROUPS * STATE
COL_DT = COL_C + GROUPS * STATE
COL_GATE = COL_DT + HEADS
POOL_GROUPS = 4
WINDOWS = (2, 4, 8, 16)
PAD = max(WINDOWS)
MG = 4
EPG = 8
NE = MG * EPG
FF = 512
BLOCK = P
MAX_BLOCKS = 2 * T // BLOCK + NE - 1
EPS = 1e-6
NEG = -3.0e38

BASE = 16512


class Arena:

    def __init__(self, nc, prefix, start):
        self.nc, self.prefix, self.at = nc, prefix, start

    def __call__(self, name, shape, dtype=F32, at=None):
        offset = self.at if at is None else at
        t = self.nc.alloc_sbuf_tensor_at(f"{self.prefix}_{name}", shape, dtype, offset=offset)
        size = int(np.prod(shape[1:])) * (2 if dtype == BF16 else 4)
        if at is None:
            self.at = offset + (size + 31) // 32 * 32
        return t


class Chain:

    def __init__(self, eng, sem, base=0, per_pass=None):
        self.eng, self.sem, self.base, self.n, self.per_pass = eng, sem, base, 0, per_pass

    def __call__(self, ins):
        ins.then_inc(self.sem, 1)
        self.n += 1
        self.eng.wait_ge(self.sem, self.base + self.n)

    def done(self):
        assert self.per_pass is None or self.n == self.per_pass, (self.n, self.per_pass)


def bc(ap, shape):
    return ap.to_broadcast(shape)


def product(pe, out, hi, lo, rhs_hi, rhs_lo, start, stop):
    pe.matmul(out, hi, rhs_hi, start=start, stop=False)
    pe.matmul(out, hi, rhs_lo, start=False, stop=False)
    return pe.matmul(out, lo, rhs_hi, start=False, stop=stop)


class Kept:

    def __init__(self, nc):
        sb = self.sb = Arena(nc, "kept", BASE)
        self.ident = sb("ident", [P, P])
        self.ones = sb("ones", [P, P])
        self.tri = sb("tri", [P, P])
        self.tri_strict = sb("tri_strict", [P, P], BF16)
        self.ones_bf = sb("ones_bf", [P, P], BF16)
        self.cols_a = sb("cols_a", [P, P])
        self.cols_b = sb("cols_b", [P, 32])
        self.skip_col = sb("skip_col", [P, INNER // P])
        self.sq_acc = sb("sq_acc", [P, T])
        self.weight = [sb(f"weight{k}", [P, TT]) for k in range(2)]
        self.table = sb("table", [1, MAX_BLOCKS + 3], I32)
        self.logits = sb("logits", [P, TT, MG + NE])
        self.end = sb.at


def phase_start(nc, kept, a, dram):
    sb = Arena(nc, "p0", kept.end)
    hT_hi = sb("hT_hi", [P, KT, T], F32R)
    hT_lo = sb("hT_lo", [P, KT, T], F32R)
    x = sb("x", [P, TT, D])
    ADA = 4
    ada = sb("ada", [P, ADA, KT, 512 // 2])
    NCH = 6 * D // 256
    modr = sb("modr", [1, 6 * D])
    h_tmp = sb("h_tmp", [P, 2, T])
    rows_a = sb("rows_a", [P, P])
    rows_b = sb("rows_b", [32, P])
    skip_row = sb("skip_row", [P, HEADS])
    th_c = sb("th_c", [P, KT])
    silu_c = sb("silu_c", [P, KT])
    ss = sb("ss", [P, TT])
    var = sb("var", [P, TT])
    std = sb("std", [P, TT])
    rstd = sb("rstd", [P, TT])
    sh1 = sb("sh1", [P, KT])
    gs1 = sb("gs1", [P, KT])
    FIRST = 2 * D // 256
    small = sb("small", [P, 5, TT, HEADS])
    small_g = sb("small_g", [P, GROUPS, 5 * TT, GH])
    acs, dt, decay, exp_acs, exp_end = (small[:, n] for n in range(5))
    w = sb("w", [P, KT, HEADS])
    w_hi = sb("w_hi", [P, KT, HEADS], F32R)
    w_lo = sb("w_lo", [P, KT, HEADS], F32R)
    bias = sb("bias", [P, HEADS])
    a_log = sb("a_log", [P, HEADS])
    a_neg = sb("a_neg", [P, HEADS])
    S = [P, TT, HEADS]
    raw, mag, ex, u, ln_u, um1, is0, a_dt, dif = (sb(n, S) for n in
                                                  ("raw", "mag", "ex", "u", "ln_u", "um1", "is0", "a_dt", "dif"))
    acs_rows = sb("acs_rows", [HEADS, T])
    raw_rows = sb("raw_rows", [HEADS, T])

    POOLS, DVES = (8, 9, 10), (3, 6, 14, 18, 21)
    ORDER = (0, 1, 2, 3, 4, 5, 7, 6, 8, 9, 10, 11, 12, 13, 15, 14, 16, 17, 19, 18, 20, 22, 21, 23)
    assert sorted(ORDER) == list(range(NCH)) and set(ORDER[:FIRST]) == set(range(FIRST))
    part_p = sb("part_p", [P, len(POOLS), 256])
    PARTS = 3
    part_d = sb("part_d", [P, PARTS, 256])
    AFTER_DT, AFTER_TURN, AFTER_SUMS = 3, 4, 1

    with ExitStack() as ctx:
        sem = lambda n: nc.alloc_semaphore("p0_" + n)
        ps = lambda n: ctx.enter_context(nc.psum_tensor("p0_" + n, [P, HALF], F32))
        ps_cols = ps("cols")
        ps_ada = [ps("ada0"), ps("ada1")]
        ps_t = [[ps("t00"), ps("t01")], [ps("t10"), ps("t11")]]
        ps_raw = [ps_cols, ps("raw1")]
        ps_dt, ps_cum, ps_end, ps_rows = ps_t[0][0], ps_t[0][1], ps_t[1][0], [ps_t[1][1], ps_raw[1]]
        par_in, ident_made, consts_made, memsets = sem("par_in"), sem("ident_made"), sem("consts_made"), sem("memsets")
        ada_b_in, skip_in = sem("ada_b_in"), sem("skip_in")
        x_in = [sem(f"x_in{i}") for i in range(TT)]
        ada_in = [sem(f"ada_in{i}") for i in range(ADA)]
        ada_done, mod_row = sem("ada_done"), sem("mod_row")
        cols_turned, cols_copied, th_made, c_made = sem("cols_turned"), sem("cols_copied"), sem("th_made"), sem("c_made")
        squared, var_made, std_made, x_normed = sem("squared"), sem("var_made"), sem("std_made"), sem("x_normed")
        sh_turned, sh_made = sem("sh_turned"), sem("sh_made")
        x_turned, h_made, h_split = sem("x_turned"), sem("h_made"), sem("h_split")
        part_p_made, part_d_made, part_seq = sem("part_p_made"), sem("part_d_made"), sem("part_seq")
        wdt_in, w_split, raw_done, raw_read, dt_done = sem("wdt_in"), sem("w_split"), sem("raw_done"), sem("raw_read"), sem("dt_done")
        mag_made, ex_made, u_made, ln_made, a_made = sem("mag_made"), sem("ex_made"), sem("u_made"), sem("ln_made"), sem("a_made")
        alog_done, summed, acs_made, rows_turned = sem("alog_done"), sem("summed"), sem("acs_made"), sem("rows_turned")
        dif_made, dec_made, rows_made, rows_out = sem("dif_made"), sem("dec_made"), sem("rows_made"), sem("rows_out")
        by_group = sem("by_group")
        dve_seq, mod_out = sem("dve_seq"), sem("mod_out")
        blk = ctx.enter_context(nc.Block())

        @blk.sync
        def _(sp):
            sp.dma_start(rows_a[0:8, :], a["norm1_g"][0].rearrange("(j p) -> j p", p=P)).then_inc(par_in, 16)
            sp.dma_start(rows_a[8:32, :], a["conv_b"][0].rearrange("(j p) -> j p", p=P)).then_inc(par_in, 16)
            sp.dma_start(rows_a[32:128, :], a["conv_w"][0].rearrange("w (j p) -> (w j) p", p=P)).then_inc(par_in, 16)
            sp.dma_start(rows_b[0:8, :], a["pool_scale"][0].rearrange("(j p) -> j p", p=P)).then_inc(par_in, 16)
            sp.dma_start(rows_b[8:24, :], a["ssd_norm_g"][0].rearrange("(j p) -> j p", p=P)).then_inc(par_in, 16)
            sp.dma_start(rows_b[24:32, :], a["c"][0].rearrange("(j p) -> j p", p=P)).then_inc(par_in, 16)
            for n in range(NCH):
                if n == ADA:
                    for i in range(TT):
                        sp.dma_start(x[:, i, :], a["x"][0, i * P:(i + 1) * P, :]).then_inc(x_in[i], 16)
                    sp.dma_start(w[:], a["w_in"][0, :, COL_DT:COL_DT + HEADS].rearrange("(k p) n -> p k n", p=P)).then_inc(wdt_in, 16)
                    sp.dma_start(bias[:], a["dt_bias"][0].partition_broadcast(P)).then_inc(wdt_in, 16)
                    sp.dma_start(a_log[:], a["a_log"][0].partition_broadcast(P)).then_inc(wdt_in, 16)
                if n - ADA in POOLS:
                    sp.wait_ge(part_p_made, POOLS.index(n - ADA) + 1)
                elif n - ADA in DVES:
                    sp.wait_ge(part_d_made, DVES.index(n - ADA) + 1)
                elif n >= ADA:
                    sp.wait_ge(ada_done, ORDER.index(n - ADA) + 1)
                sp.dma_start(ada[:, n % ADA], a["ada_w"][0, :, n * 256:(n + 1) * 256]
                             .rearrange("(k p) n -> p k n", p=P)).then_inc(ada_in[n % ADA], 16)
            sp.wait_ge(rows_made, 2)
            sp.dma_start(dram["acs"], acs_rows[:]).then_inc(rows_out, 16)
            sp.wait_ge(by_group, 1)
            sp.dma_start(dram["small"], small_g[:]).then_inc(rows_out, 16)
            sp.wait_ge(mod_row, NCH)
            sp.dma_start(dram["mod"], modr[0:1, 2 * D:]).then_inc(mod_out, 16)
            sp.wait_ge(rows_out, 32)
            sp.wait_ge(mod_out, 16)

        @blk.gpsimd
        def _(pool):
            pool.memset(kept.ident[:], 0.0).then_inc(memsets, 1)
            pool.memset(kept.tri[:], 1.0).then_inc(memsets, 1)
            pool.memset(kept.tri_strict[:], 1.0).then_inc(memsets, 1)
            pool.memset(kept.ones[:], 1.0).then_inc(consts_made, 1)
            pool.memset(kept.ones_bf[:], 1.0).then_inc(consts_made, 1)
            pool.wait_ge(memsets, 3)
            pool.affine_select(out=kept.ident[:], in_=kept.ident[:], compare_op=ALU.not_equal, fill=1.0,
                               base=0, pattern=[[-1, P]], channel_multiplier=1).then_inc(ident_made, 1)
            pool.affine_select(out=kept.tri[:], in_=kept.tri[:], compare_op=ALU.is_ge, fill=0.0,
                               base=0, pattern=[[1, P]], channel_multiplier=-1).then_inc(consts_made, 1)
            pool.affine_select(out=kept.tri_strict[:], in_=kept.tri_strict[:], compare_op=ALU.is_gt, fill=0.0,
                               base=0, pattern=[[1, P]], channel_multiplier=-1).then_inc(consts_made, 1)
            link = Chain(pool, part_seq)
            pool.wait_ge(c_made, 1)
            for p, n in enumerate(POOLS):
                pool.wait_ge(ada_in[n % ADA], 16 * (n // ADA + 1))
                chunk, tiles = ada[:, n % ADA], KT
                link(pool.tensor_tensor(chunk, chunk, bc(silu_c[:].unsqueeze(2), [P, KT, 256]), ALU.mult))
                while tiles > 2:
                    tiles //= 2
                    link(pool.tensor_tensor(chunk[:, 0:tiles], chunk[:, 0:tiles], chunk[:, tiles:2 * tiles], ALU.add))
                pool.tensor_tensor(part_p[:, p, :], chunk[:, 0], chunk[:, 1], ALU.add).then_inc(part_p_made, 1)

        @blk.scalar
        def _(act):
            act.dma_start(modr[:], a["ada_b"]).then_inc(ada_b_in, 16)
            act.dma_start(skip_row[:], a["d_skip"][0].partition_broadcast(P)).then_inc(skip_in, 16)
            act.wait_ge(cols_copied, 2)
            act.activation(th_c[:], kept.cols_b[:, 24:32], ACT.Tanh, scale=0.5).then_inc(th_made, 1)
            for i in range(TT):
                act.wait_ge(x_in[i], 16)
                if i >= 2:
                    act.wait_ge(squared, i - 1)
                act.activation(h_tmp[:, i % 2, :], x[:, i, :], ACT.Square,
                               accum_out=ss[:, i:i + 1]).then_inc(squared, 1)
            act.wait_ge(var_made, 1)
            act.activation(std[:], var[:], ACT.Sqrt).then_inc(std_made, 1)
            act.wait_ge(sh_made, 2)
            act.wait_ge(squared, TT)
            for k in range(KT):
                act.wait_ge(x_turned, k + 1)
                if k >= 2:
                    act.wait_ge(h_split, k - 1)
                for b in range(2):
                    act.activation(h_tmp[:, k % 2, b * HALF:(b + 1) * HALF], ps_t[k % 2][b][:], ACT.Identity,
                                   bias=sh1[:, k:k + 1], scale=gs1[:, k:k + 1]).then_inc(h_made, 1)
            for b in range(2):
                act.wait_ge(raw_done, b + 1)
                act.activation(raw_rows[:, b * HALF:(b + 1) * HALF], ps_raw[b][0:HEADS, :], ACT.Copy).then_inc(raw_read, 1)
            act.wait_ge(wdt_in, 48)
            act.activation(a_neg[:], a_log[:], ACT.Exp).then_inc(alog_done, 1)
            act.wait_ge(mag_made, 1)
            act.activation(ex[:], mag[:], ACT.Exp, scale=-1.0).then_inc(ex_made, 1)
            act.wait_ge(u_made, 1)
            act.activation(ln_u[:], u[:], ACT.Ln).then_inc(ln_made, 1)
            act.wait_ge(dif_made, 1)
            act.activation(decay, dif[:], ACT.Exp).then_inc(dec_made, 1)
            act.activation(exp_acs, acs, ACT.Exp).then_inc(dec_made, 1)
            act.activation(exp_end, exp_end, ACT.Exp).then_inc(dec_made, 1)

        @blk.vector
        def _(dve):
            link = Chain(dve, dve_seq)
            dve.wait_ge(cols_turned, 1)
            dve.tensor_copy(kept.cols_a[:], ps_cols[:, 0:P]).then_inc(cols_copied, 1)
            dve.tensor_copy(kept.cols_b[:], ps_cols[:, P:P + 32]).then_inc(cols_copied, 1)
            dve.wait_ge(th_made, 1)
            dve.wait_ge(cols_copied, 2)
            link(dve.scalar_tensor_tensor(silu_c[:], th_c[:], 1.0, kept.cols_b[:, 24:32], ALU.add, ALU.mult))
            dve.tensor_scalar(silu_c[:], silu_c[:], 0.5, None, ALU.mult).then_inc(c_made, 1)
            dve.wait_ge(skip_in, 16)
            dve.tensor_copy(kept.skip_col[0:64, :], skip_row[0:64, 0::2])
            dve.tensor_copy(kept.skip_col[64:128, :], skip_row[64:128, 1::2])

            def mod_chunk(n):
                dve.wait_ge(ada_done, n + 1)
                if n == 0:
                    dve.wait_ge(ada_b_in, 16)
                row = modr[0:1, ORDER[n] * 256:(ORDER[n] + 1) * 256]
                dve.tensor_tensor(row, ps_ada[n % 2][0:1, 0:256], row, ALU.add).then_inc(mod_row, 1)

            def part_chunk(n):
                p = DVES.index(n)
                dve.wait_ge(ada_in[n % ADA], 16 * (n // ADA + 1))
                out = part_d[:, p % PARTS, :]
                link(dve.tensor_scalar(out, ada[:, n % ADA, 0, :], silu_c[:, 0:1], None, ALU.mult))
                for k in range(1, KT):
                    ins = dve.scalar_tensor_tensor(out, ada[:, n % ADA, k, :], silu_c[:, k:k + 1], out, ALU.mult, ALU.add)
                    if k < KT - 1:
                        link(ins)
                ins.then_inc(part_d_made, 1)

            dve.wait_ge(c_made, 1)
            for n in range(ADA):
                if n == 2:
                    part_chunk(3)
                mod_chunk(n)
            dve.wait_ge(squared, TT)
            dve.tensor_scalar(var[:], ss[:], 1.0 / D, EPS, ALU.mult, ALU.add).then_inc(var_made, 1)
            dve.wait_ge(std_made, 1)
            link(dve.reciprocal(rstd[:], std[:]))
            for i in range(TT):
                dve.tensor_scalar(x[:, i, :], x[:, i, :], rstd[:, i:i + 1], None, ALU.mult).then_inc(x_normed, 1)
                if i % 2 == 1 and ADA + i // 2 < FIRST:
                    mod_chunk(ADA + i // 2)
                if i == 3:
                    part_chunk(6)
            dve.wait_ge(wdt_in, 48)
            link(dve.tensor_copy(w_hi[:], w[:]))
            dve.tensor_tensor(w_lo[:], w[:], w_hi[:].bitcast(F32), ALU.subtract).then_inc(w_split, 1)
            dve.wait_ge(sh_turned, 1)
            dve.tensor_copy(sh1[:], ps_cols[:, 256:264]).then_inc(sh_made, 1)
            dve.scalar_tensor_tensor(gs1[:], ps_cols[:, 264:272], 1.0, kept.cols_a[:, 0:8],
                                     ALU.add, ALU.mult).then_inc(sh_made, 1)
            for k in range(KT):
                dve.wait_ge(h_made, 2 * k + 2)
                link(dve.tensor_copy(hT_hi[:, k, :], h_tmp[:, k % 2, :]))
                dve.tensor_tensor(hT_lo[:, k, :], h_tmp[:, k % 2, :], hT_hi[:, k, :].bitcast(F32),
                                  ALU.subtract).then_inc(h_split, 1)
            for n in range(FIRST, FIRST + AFTER_DT):
                mod_chunk(n)
            dve.wait_ge(dt_done, 1)
            link(dve.tensor_tensor(raw[:], ps_dt[:, 0:TT * HEADS].rearrange("p (t h) -> p t h", h=HEADS),
                                   bc(bias[:].unsqueeze(1), S), ALU.add))
            link(dve.tensor_scalar(mag[:], raw[:], -1.0, None, ALU.mult))
            dve.tensor_tensor(mag[:], raw[:], mag[:], ALU.max).then_inc(mag_made, 1)
            n = FIRST + AFTER_DT
            mod_chunk(n)
            part_chunk(14)
            dve.wait_ge(ex_made, 1)
            dve.tensor_scalar(u[:], ex[:], 1.0, None, ALU.add).then_inc(u_made, 1)
            dve.wait_ge(u_made, 1)
            link(dve.tensor_scalar(um1[:], u[:], -1.0, None, ALU.add))
            link(dve.tensor_scalar(is0[:], um1[:], 0.0, None, ALU.is_equal))
            link(dve.tensor_tensor(um1[:], um1[:], is0[:], ALU.add))
            link(dve.reciprocal(um1[:], um1[:]))
            mod_chunk(n + 1)
            dve.wait_ge(ln_made, 1)
            link(dve.tensor_tensor(ln_u[:], ln_u[:], um1[:], ALU.mult))
            link(dve.tensor_tensor(ln_u[:], ln_u[:], is0[:], ALU.add))
            link(dve.tensor_tensor(ln_u[:], ln_u[:], ex[:], ALU.mult))
            link(dve.scalar_tensor_tensor(dt, raw[:], 0.0, ln_u[:], ALU.max, ALU.add))
            mod_chunk(n + 2)
            dve.wait_ge(alog_done, 1)
            link(dve.tensor_scalar(a_neg[:], a_neg[:], -1.0, None, ALU.mult))
            dve.tensor_tensor(a_dt[:], dt, bc(a_neg[:].unsqueeze(1), S), ALU.mult).then_inc(a_made, 1)
            mod_chunk(n + 3)
            dve.wait_ge(summed, 1)
            dve.tensor_copy(acs, ps_cum[:, 0:TT * HEADS].rearrange("p (t h) -> p t h", h=HEADS)).then_inc(acs_made, 1)
            link(dve.tensor_copy(exp_end, ps_end[:, 0:TT * HEADS].rearrange("p (t h) -> p t h", h=HEADS)))
            dve.wait_ge(acs_made, 1)
            dve.tensor_tensor(dif[:], exp_end, acs, ALU.subtract).then_inc(dif_made, 1)
            mod_chunk(n + 4)
            for b in range(2):
                dve.wait_ge(rows_turned, b + 1)
                dve.tensor_copy(acs_rows[:, b * HALF:(b + 1) * HALF], ps_rows[b][0:HEADS, :]).then_inc(rows_made, 1)
            dve.wait_ge(dec_made, 3)
            dve.tensor_copy(small_g[:], small[:].rearrange("p a t (g h) -> p g (a t) h", h=GH)).then_inc(by_group, 1)
            for m in range(n + 5, NCH):
                if m == n + 5:
                    part_chunk(18)
                if m == n + 9:
                    part_chunk(21)
                mod_chunk(m)

        @blk.tensor
        def _(pe):
            pe.wait_ge(par_in, 96)
            pe.wait_ge(ident_made, 1)
            pe.transpose(ps_cols[:, 0:P], rows_a[:], kept.ident[:])
            pe.transpose(ps_cols[:, P:P + 32], rows_b[:], kept.ident[0:32, 0:32]).then_inc(cols_turned, 1)
            pe.wait_ge(c_made, 1)

            def ada_chunk(n):
                m = ORDER[n]
                if n >= 2:
                    pe.wait_ge(mod_row, n - 1)
                if m in POOLS or m in DVES:
                    if m in POOLS:
                        pe.wait_ge(part_p_made, POOLS.index(m) + 1)
                        part = part_p[:, POOLS.index(m), :]
                    else:
                        pe.wait_ge(part_d_made, DVES.index(m) + 1)
                        part = part_d[:, DVES.index(m) % PARTS, :]
                    mm = pe.matmul(ps_ada[n % 2][0:1, 0:256], kept.ones[:, 0:1], part, start=True, stop=True)
                else:
                    pe.wait_ge(ada_in[m % ADA], 16 * (m // ADA + 1))
                    for k in range(KT):
                        mm = pe.matmul(ps_ada[n % 2][0:1, 0:256], silu_c[:, k:k + 1], ada[:, m % ADA, k, :],
                                       start=(k == 0), stop=(k == KT - 1))
                mm.then_inc(ada_done, 1)

            pe.wait_ge(consts_made, 4)
            for n in range(FIRST):
                ada_chunk(n)
            pe.wait_ge(mod_row, FIRST)
            for j in range(2 * KT):
                mm = pe.matmul(ps_cols[:, 256 + j:257 + j], modr[0:1, j * P:(j + 1) * P], kept.ones[0:1, 0:1],
                               start=True, stop=True)
            mm.then_inc(sh_turned, 1)
            pe.wait_ge(x_normed, TT)
            pe.wait_ge(w_split, 1)
            pe.wait_ge(sh_made, 2)

            def raw_step(k):
                pe.wait_ge(h_split, k + 1)
                for b in range(2):
                    half = slice(b * HALF, (b + 1) * HALF)
                    mm = product(pe, ps_raw[b][0:HEADS, :], w_hi[:, k, :], w_lo[:, k, :], hT_hi[:, k, half],
                                 hT_lo[:, k, half], k == 0, k == KT - 1)
                    if k == KT - 1:
                        mm.then_inc(raw_done, 1)

            for k in range(KT):
                if k >= 2:
                    pe.wait_ge(h_made, 2 * k - 2)
                for i in range(TT):
                    mm = pe.transpose(ps_t[k % 2][i // 4][:, (i % 4) * P:(i % 4 + 1) * P],
                                      x[:, i, k * P:(k + 1) * P], kept.ident[:])
                mm.then_inc(x_turned, 1)
                if k >= 2:
                    raw_step(k - 2)
            raw_step(KT - 2)
            raw_step(KT - 1)
            n = FIRST
            for n in range(n, n + AFTER_DT):
                ada_chunk(n)
            pe.wait_ge(raw_read, 2)
            for i in range(TT):
                mm = pe.transpose(ps_dt[:, i * HEADS:(i + 1) * HEADS], raw_rows[:, i * P:(i + 1) * P],
                                  kept.ident[0:HEADS, 0:HEADS])
            mm.then_inc(dt_done, 1)
            for n in range(n + 1, n + 1 + AFTER_TURN):
                ada_chunk(n)
            pe.wait_ge(a_made, 1)
            pe.matmul(ps_cum[:, 0:TT * HEADS], kept.tri[:], a_dt[:].rearrange("p t h -> p (t h)"), start=True, stop=True)
            pe.matmul(ps_end[:, 0:TT * HEADS], kept.ones[:], a_dt[:].rearrange("p t h -> p (t h)"),
                      start=True, stop=True).then_inc(summed, 1)
            for n in range(n + 1, n + 1 + AFTER_SUMS):
                ada_chunk(n)
            pe.wait_ge(acs_made, 1)
            for i in range(TT):
                mm = pe.transpose(ps_rows[i // 4][0:HEADS, (i % 4) * P:(i % 4 + 1) * P], acs[:, i, :], kept.ident[:])
                if i % 4 == 3:
                    mm.then_inc(rows_turned, 1)
            for n in range(n + 1, NCH):
                ada_chunk(n)
    return hT_hi, hT_lo


def phase_ssd(nc, kept, a, dram, hT_hi, hT_lo):
    sb = Arena(nc, "p2", kept.end + 2 * KT * T * 4)
    acc = sb("acc", [P, KT, T])
    RAW = 2
    raw = sb("raw", [P, RAW, KT, P])
    w_hi = sb("w_hi", [P, RAW, KT, P], F32R)
    w_lo = sb("w_lo", [P, RAW, KT, P], F32R)
    NX = INNER // GROUPS // P
    NXBC = NX + 2
    cvb = sb("cvb", [P, CONV - 1 + T])
    xcT = sb("xcT", [P, NXBC, T])
    at = sb.at
    zT = sb("zT", [P, NX, T])
    yh = sb("yh", [P, NX, T], F32R, at=at)
    at = sb.at
    yT = sb("yT", [P, NX, T])
    yl = sb("yl", [P, NX, T], F32R, at=at)
    seg = sb("seg", [P, 2, GH, P])
    XG = [P, GH, HEAD_DIM]
    x_dt, x_dec, y_tok, state = (sb(n, XG) for n in ("x_dt", "x_dec", "y_tok", "state"))
    b_tok = sb("b_tok", [P, P])
    cbm = sb("cbm", [P, P])
    gp = sb("gp", [P, 1 + CONV, NXBC])
    gs = sb("gs", [P, 5, TT, GH])
    gcol = sb("gcol", [P, 2, NX])
    NPROJ, NBR = NXBC + NX, KT
    NW = NPROJ + NBR // 2

    with ExitStack() as ctx:
        sem = lambda n: nc.alloc_semaphore("p2_" + n)
        ps = lambda n: ctx.enter_context(nc.psum_tensor("p2_" + n, [P, HALF], F32))
        pair = [[ps("pair00"), ps("pair01")], [ps("pair10"), ps("pair11")]]
        ps_x, ps_cb, ps_yd, ps_yo = ps("x"), ps("cb"), ps("yd"), ps("yo")
        w_in = [sem(f"w_in{i}") for i in range(RAW)]
        seg_in = [sem(f"seg_in{i}") for i in range(2)]
        hi_made, lo_made, lo0_made = sem("hi_made"), sem("lo_made"), sem("lo0_made")
        proj_done, br_done, proj_read, br_read = sem("proj_done"), sem("br_done"), sem("proj_read"), sem("br_read")
        pads, acc_zeroed = sem("pads"), sem("acc_zeroed")
        pre_made, th_made, xc_made, z_made = (sem(n) for n in ("pre_made", "th_made", "xc_made", "z_made"))
        xt_done, xdt_made, cb_done, cbm_made, bt_made = (sem(n) for n in ("xt_done", "xdt_made", "cb_done", "cbm_made", "bt_made"))
        seg_made, exp_made, g_made, yo_done, yd_done = (sem(n) for n in ("seg_made", "exp_made", "g_made", "yo_done", "yd_done"))
        st_done, y_made, st_made, ytr_done, yT_made = (sem(n) for n in ("st_done", "y_made", "st_made", "ytr_done", "yT_made"))
        y_gated, sq_made, sq_added, yh_made, yl_made = (sem(n) for n in ("y_gated", "sq_made", "sq_added", "yh_made", "yl_made"))
        xdec_made, st_scaled, skip_made, y_skipped = sem("xdec_made"), sem("st_scaled"), sem("skip_made"), sem("y_skipped")
        seq, acc_out, gs_in = sem("seq"), sem("acc_out"), sem("gs_in")
        blk = ctx.enter_context(nc.Block())
        W_CREDIT = RAW
        USED_CREDIT = 2 * NBR
        BR_CREDIT = 2
        SEG_CREDIT = 2
        SQ_CREDIT = 1
        SEQ_N = 2 + NXBC * (CONV - 1) + (TT - 1)
        STEPS = (2 * (NX - 1) - 1) * KT // TT
        FIRST_STEPS = (STEPS + 1) // 2
        z_ready = [[(1 + q // 2, q % 2) for q in range(2 * (NX - 1) - 1) if (KT * (q + 1) - 1) // STEPS == c - 1]
                   for c in range(TT)]
        z_ready[0] = [(0, 0), (0, 1)]

        @blk.sync
        def _(sp):
            with sp.Fori(0, GROUPS) as g:
                def load(i, src):
                    if i == RAW:
                        sp.wait_ge(lo0_made, g + 1)
                    else:
                        sp.wait_ge(lo_made, g * (NW - 1) + (i if i > RAW else i + 1))
                    sp.dma_start(raw[:, i % RAW] if i < NPROJ else
                                 raw[:, i % RAW].rearrange("p k n -> p (k n)").rearrange("p (k n) -> p k n", k=NX),
                                 src).then_inc(w_in[i % RAW], 16)
                wide, narrow = sp.snap(g * (NX * P)), sp.snap(g * P)
                cols = [(COL_X + j * P, wide) for j in range(NX)] + [(COL_B, narrow), (COL_C, narrow)] + \
                       [(COL_Z + j * P, wide) for j in range(NX)]
                for i, (first, col) in enumerate(cols):
                    load(i, a["w_in"][0, :, first:][:, bass.ds(col, P)].rearrange("(k p) n -> p k n", p=P))
                for m in range(NBR // 2):
                    load(NPROJ + m, a["w_branch_ssd"][0, bass.ds(g * (NX * P), NX * P), 2 * m * P:(2 * m + 2) * P]
                         .rearrange("(k p) n -> p k n", p=P))
            for n in range(NBR):
                sp.wait_ge(br_read, BR_CREDIT + (GROUPS - 1) * NBR + n + 1)
                sp.dma_start(dram["acc"][:, n, :], acc[:, n, :]).then_inc(acc_out, 16)
            sp.wait_ge(acc_out, 16 * NBR)

        @blk.gpsimd
        def _(pool):
            pool.sem_inc(yd_done, SEG_CREDIT)
            pool.sem_inc(sq_added, SQ_CREDIT)
            pool.memset(cvb[:, 0:CONV - 1], 0.0).then_inc(pads, 1)
            pool.memset(kept.sq_acc[:], 0.0).then_inc(acc_zeroed, 1)
            pool.memset(acc[:, 0:KT // 2], 0.0).then_inc(acc_zeroed, 1)
            pool.wait_ge(acc_zeroed, 3)
            with pool.Fori(0, GROUPS) as g:
                pool.dma_start(gs[:], dram["small"][:, bass.ds(g, 1)].rearrange("p g (a t) h -> p (g a) t h", t=TT)).then_inc(gs_in, 16)
                pool.wait_ge(hi_made, g * NW + 1)
                pool.tensor_tensor(w_lo[:, 0], raw[:, 0], w_hi[:, 0].bitcast(F32), ALU.subtract).then_inc(lo0_made, 1)

                def add_skip(c):
                    ch = slice(c * P, (c + 1) * P)
                    pool.wait_ge(yT_made, g * TT + c + 1)
                    pool.wait_ge(skip_made, g * TT + c + 1)
                    pool.tensor_tensor(yT[:, :, ch], yT[:, :, ch], xcT[:, 0:NX, ch], ALU.add).then_inc(y_skipped, 1)

                pool.wait_ge(gs_in, 16 * (g + 1))
                for c in range(TT):
                    ch = slice(c * P, (c + 1) * P)
                    pool.wait_ge(xdt_made, g * TT + c + 1)
                    if c < TT - 1:
                        pool.tensor_tensor(x_dec[:], x_dt[:], bc(gs[:, 2, c, :].unsqueeze(2), XG), ALU.mult).then_inc(xdec_made, 1)
                    if c:
                        add_skip(c - 1)
                    if 0 < c < TT - 1:
                        pool.wait_ge(yo_done, g * (TT - 1) + c)
                        pool.tensor_tensor(state[:], state[:], bc(gs[:, 4, c, :].unsqueeze(2), XG), ALU.mult).then_inc(st_scaled, 1)
                    pool.tensor_tensor(xcT[:, 0:NX, ch], xcT[:, 0:NX, ch], bc(gcol[:, 1, :].unsqueeze(2), [P, NX, P]),
                                       ALU.mult).then_inc(skip_made, 1)
                add_skip(TT - 1)
                for j in range(NX):
                    pool.wait_ge(sq_made, g * NX + j + 1)
                    pool.wait_ge(sq_added, g * NX + j + SQ_CREDIT)
                    pool.tensor_tensor(kept.sq_acc[:], kept.sq_acc[:], xcT[:, j, :], ALU.add).then_inc(sq_added, 1)

        @blk.scalar
        def _(act):
            with act.Fori(0, GROUPS) as g:
                def hi(i):
                    slot = i % RAW
                    act.wait_ge(w_in[slot], 16 * (g * (NW // RAW) + i // RAW + 1))
                    if i < RAW:
                        act.wait_ge(br_done, g * (2 * NBR) + 2 * NBR - 4 * (RAW - 1 - i))
                    elif i - RAW < NPROJ:
                        act.wait_ge(proj_done, g * (2 * NPROJ) + 2 * (i - RAW) + 2)
                    else:
                        act.wait_ge(br_done, g * (2 * NBR) + 4 * (i - RAW - NPROJ) + 4 + USED_CREDIT)
                    act.activation(w_hi[:, slot], raw[:, slot], ACT.Copy).then_inc(hi_made, 1)

                def load_seg(c):
                    act.wait_ge(yd_done, g * TT + c + 1)
                    act.dma_start(seg[:, c % 2], dram["acs"][bass.ds(g * GH, GH), c * P:(c + 1) * P]
                                  .partition_broadcast(P)).then_inc(seg_in[c % 2], 16)

                hi(0)
                hi(1)
                load_seg(0)
                load_seg(1)
                for i in range(NXBC):
                    if i:
                        act.wait_ge(xc_made, g * NXBC + i)
                    for b in range(2):
                        act.wait_ge(proj_done, g * (2 * NPROJ) + 2 * i + b + 1)
                        act.activation(cvb[:, CONV - 1 + b * HALF:CONV - 1 + (b + 1) * HALF], pair[i % 2][b][:],
                                       ACT.Copy).then_inc(proj_read, 1)
                    hi(i + 2)
                    act.wait_ge(pre_made, g * NXBC + i + 1)
                    act.activation(cvb[:, CONV - 1:], xcT[:, i, :], ACT.Tanh).then_inc(th_made, 1)

                def y_out(c):
                    act.wait_ge(ytr_done, g * TT + c + 1)
                    act.activation(yT[:, :, c * P:(c + 1) * P], ps_yo[:].rearrange("p (j l) -> p j l", l=P),
                                   ACT.Copy).then_inc(yT_made, 1)

                def z_half(j, b):
                    if b == 0:
                        if j == 0:
                            act.wait_ge(xc_made, g * NXBC + NXBC)
                        else:
                            act.wait_ge(z_made, g * NX + j)
                    i = NXBC + j
                    act.wait_ge(proj_done, g * (2 * NPROJ) + 2 * i + b + 1)
                    half = slice(b * HALF, (b + 1) * HALF)
                    act.activation(zT[:, j, half], pair[i % 2][b][:], ACT.Copy, scale=0.5)
                    act.activation(cvb[:, CONV - 1 + b * HALF:CONV - 1 + (b + 1) * HALF], pair[i % 2][b][:],
                                   ACT.Tanh, scale=0.5).then_inc(proj_read, 1)
                    if b == 1:
                        hi(i + 2)

                for c in range(TT):
                    if 0 < c < TT - 1:
                        load_seg(c + 1)
                    act.wait_ge(seg_made, g * TT + c + 1)
                    act.activation(seg[:, c % 2], seg[:, c % 2], ACT.Exp).then_inc(exp_made, 1)
                    act.wait_ge(cbm_made, g * TT + c + 1)
                    act.activation(b_tok[:], ps_cb[:, P:2 * P], ACT.Copy).then_inc(bt_made, 1)
                    if c:
                        y_out(c - 1)
                    for j, b in z_ready[c]:
                        z_half(j, b)
                y_out(TT - 1)
                z_half(NX - 1, 0)
                for j in range(NX):
                    if j == 1:
                        z_half(NX - 1, 1)
                    act.wait_ge(y_gated, g * NX + j + 1)
                    act.activation(yh[:, j, :], yT[:, j, :], ACT.Copy, scale=gcol[:, 0, j:j + 1]).then_inc(yh_made, 1)
                    act.activation(xcT[:, j, :], yT[:, j, :], ACT.Square).then_inc(sq_made, 1)
                hi(NW - 2)
                hi(NW - 1)

        @blk.vector
        def _(dve):
            dve.sem_inc(lo_made, W_CREDIT)
            dve.sem_inc(br_read, BR_CREDIT)
            dve.memset(acc[:, KT // 2:], 0.0).then_inc(acc_zeroed, 1)
            dve.wait_ge(pads, 1)
            with dve.Fori(0, GROUPS) as g:
                link = Chain(dve, seq, g * SEQ_N, SEQ_N)

                def lo(i):
                    slot = i % RAW
                    dve.wait_ge(hi_made, g * NW + i + 1)
                    dve.tensor_tensor(w_lo[:, slot], raw[:, slot], w_hi[:, slot].bitcast(F32),
                                      ALU.subtract).then_inc(lo_made, 1)

                conv_cols = kept.cols_a[:, 8:8 + (1 + CONV) * CONV_TILES].rearrange("p (w m) -> p w m", m=CONV_TILES)
                dve.tensor_copy(gp[:, :, 0:NX], conv_cols[:, :, bass.ds(g * NX, NX)])
                dve.tensor_copy(gp[:, :, NX:NX + 1], conv_cols[:, :, bass.ds(g + INNER // P, 1)])
                dve.tensor_copy(gp[:, :, NX + 1:NX + 2], conv_cols[:, :, bass.ds(g + INNER // P + GROUPS, 1)])
                dve.tensor_copy(gcol[:, 0, :], kept.cols_b[:, bass.ds(g * NX + 8, NX)])
                link(dve.tensor_copy(gcol[:, 1, :], kept.skip_col[:, bass.ds(g * NX, NX)]))
                link(dve.tensor_scalar(gp[:], gp[:], 0.5, None, ALU.mult))
                g_acs, g_dt, g_exp = gs[:, 0], gs[:, 1], gs[:, 3]
                lo(1)
                dve.wait_ge(sq_added, g * NX + SQ_CREDIT)
                for i in range(NXBC):
                    dve.wait_ge(proj_read, g * (2 * NPROJ) + 2 * i + 2)
                    link(dve.tensor_scalar(xcT[:, i, :], cvb[:, 0:T], gp[:, 1, i:i + 1], gp[:, 0, i:i + 1],
                                           ALU.mult, ALU.add))
                    for w in range(1, CONV):
                        ins = dve.scalar_tensor_tensor(xcT[:, i, :], cvb[:, w:w + T], gp[:, 1 + w, i:i + 1],
                                                       xcT[:, i, :], ALU.mult, ALU.add)
                        if w < CONV - 1:
                            link(ins)
                    ins.then_inc(pre_made, 1)
                    lo(i + 2)
                    dve.wait_ge(th_made, g * NXBC + i + 1)
                    dve.wait_ge(pre_made, g * NXBC + i + 1)
                    dve.scalar_tensor_tensor(xcT[:, i, :], cvb[:, CONV - 1:], 1.0, xcT[:, i, :],
                                             ALU.add, ALU.mult).then_inc(xc_made, 1)

                def segments(c):
                    dve.wait_ge(seg_in[c % 2], 16 * (g * (TT // 2) + c // 2 + 1))
                    for h in range(GH):
                        ins = dve.tensor_scalar(seg[:, c % 2, h, :], seg[:, c % 2, h, :], g_acs[:, c, h:h + 1], 0.0,
                                                ALU.subtract, ALU.min)
                    ins.then_inc(seg_made, 1)

                def z_gate(j):
                    dve.wait_ge(proj_read, g * (2 * NPROJ) + 2 * (NXBC + j) + 2)
                    dve.scalar_tensor_tensor(zT[:, j, :], cvb[:, CONV - 1:], 1.0, zT[:, j, :],
                                             ALU.add, ALU.mult).then_inc(z_made, 1)

                dve.wait_ge(gs_in, 16 * (g + 1))
                segments(0)
                for c in range(TT):
                    dve.wait_ge(xt_done, g * TT + c + 1)
                    xt = ps_x[:].rearrange("p (h d) -> p h d", d=HEAD_DIM)
                    dve.tensor_tensor(x_dt[:], xt, bc(g_dt[:, c, :].unsqueeze(2), XG), ALU.mult).then_inc(xdt_made, 1)
                    dve.wait_ge(cb_done, g * TT + c + 1)
                    dve.tensor_tensor(cbm[:], ps_cb[:, 0:P], kept.tri[:], ALU.mult).then_inc(cbm_made, 1)
                    dve.wait_ge(cbm_made, g * TT + c + 1)
                    dve.wait_ge(exp_made, g * TT + c + 1)
                    dve.tensor_tensor(seg[:, c % 2], seg[:, c % 2], bc(cbm[:].unsqueeze(1), [P, GH, P]),
                                      ALU.mult).then_inc(g_made, 1)
                    if c + 1 < TT:
                        segments(c + 1)
                    if c:
                        dve.wait_ge(yo_done, g * (TT - 1) + c)
                        dve.wait_ge(ytr_done, g * TT + c)
                        link(dve.tensor_tensor(y_tok[:], ps_yo[:].rearrange("p (h d) -> p h d", d=HEAD_DIM),
                                               bc(g_exp[:, c, :].unsqueeze(2), XG), ALU.mult))
                        dve.wait_ge(yd_done, g * TT + c + 1 + SEG_CREDIT)
                        dve.tensor_tensor(y_tok[:], ps_yd[:].rearrange("p (h d) -> p h d", d=HEAD_DIM), y_tok[:],
                                          ALU.add).then_inc(y_made, 1)
                    else:
                        dve.wait_ge(yd_done, g * TT + c + 1 + SEG_CREDIT)
                        dve.tensor_copy(y_tok[:], ps_yd[:].rearrange("p (h d) -> p h d", d=HEAD_DIM)).then_inc(y_made, 1)
                    if c < TT - 1:
                        dve.wait_ge(st_done, g * (TT - 1) + c + 1)
                        if c:
                            dve.wait_ge(st_scaled, g * (TT - 2) + c)
                            dve.tensor_tensor(state[:], ps_x[:].rearrange("p (h d) -> p h d", d=HEAD_DIM), state[:],
                                              ALU.add).then_inc(st_made, 1)
                        else:
                            dve.tensor_copy(state[:], ps_x[:].rearrange("p (h d) -> p h d", d=HEAD_DIM)).then_inc(st_made, 1)
                    if c == 0:
                        lo(NXBC + 2)
                    for j, b in z_ready[c]:
                        if b and j:
                            z_gate(j)
                            lo(NXBC + j + 2)
                    if c == 1:
                        z_gate(0)

                def y_gate(j):
                    dve.wait_ge(z_made, g * NX + j + 1)
                    dve.tensor_tensor(yT[:, j, :], yT[:, j, :], zT[:, j, :], ALU.mult).then_inc(y_gated, 1)

                def y_lo(j):
                    dve.wait_ge(yh_made, g * NX + j + 1)
                    dve.wait_ge(sq_made, g * NX + j + 1)
                    dve.scalar_tensor_tensor(yl[:, j, :], yT[:, j, :], gcol[:, 0, j:j + 1], yh[:, j, :].bitcast(F32),
                                             ALU.mult, ALU.subtract).then_inc(yl_made, 1)

                dve.wait_ge(y_skipped, g * TT + TT)
                y_gate(0)
                y_gate(1)
                for j in range(NX):
                    y_lo(j)
                    if j == 0:
                        z_gate(NX - 1)
                    if j + 2 < NX:
                        y_gate(j + 2)
                lo(NPROJ + 1)
                dve.wait_ge(acc_zeroed, 3)
                for n in range(NBR):
                    for b in range(2):
                        half = slice(b * HALF, (b + 1) * HALF)
                        dve.wait_ge(br_done, g * (2 * NBR) + 2 * n + b + 1 + USED_CREDIT)
                        ins = dve.tensor_tensor(acc[:, n, half], pair[n % 2][b][:], acc[:, n, half], ALU.add)
                    ins.then_inc(br_read, 1)
                    if n % 2 and NPROJ + n // 2 + 2 < NW:
                        lo(NPROJ + n // 2 + 2)
                link.done()

        @blk.tensor
        def _(pe):
            pe.sem_inc(br_done, USED_CREDIT)
            with pe.Fori(0, GROUPS) as g:
                def begin(i):
                    if i == 0:
                        pe.wait_ge(lo0_made, g + 1)
                    else:
                        pe.wait_ge(lo_made, g * (NW - 1) + i + W_CREDIT)
                    pe.wait_ge(hi_made, g * NW + i + 1)

                def steps(i, first, last):
                    for n in range(first, last):
                        b, k = divmod(n, KT)
                        mm = product(pe, pair[i % 2][b][:], w_hi[:, i % RAW, k, :], w_lo[:, i % RAW, k, :],
                                     hT_hi[:, k, b * HALF:(b + 1) * HALF], hT_lo[:, k, b * HALF:(b + 1) * HALF],
                                     k == 0, k == KT - 1)
                        if k == KT - 1:
                            mm.then_inc(proj_done, 1)

                def z_steps(first, last):
                    for n in range(first, last):
                        j, step = divmod(n, 2 * KT)
                        i = NXBC + 1 + j
                        if step == 0:
                            begin(i)
                            pe.wait_ge(proj_read, g * (2 * NPROJ) + 2 * (i - 2) + 2)
                        steps(i, step, step + 1)

                for i in range(NXBC + 1):
                    begin(i)
                    if i < 2:
                        pe.wait_ge(br_read, g * NBR + i + 1)
                    else:
                        pe.wait_ge(proj_read, g * (2 * NPROJ) + 2 * (i - 2) + 2)
                    steps(i, 0, 2 * KT)

                def y_turn(c):
                    pe.wait_ge(y_made, g * TT + c + 1)
                    for j in range(NX):
                        mm = pe.transpose(ps_yo[:, j * P:(j + 1) * P],
                                          y_tok[:].rearrange("p h d -> p (h d)")[:, j * P:(j + 1) * P], kept.ident[:])
                    mm.then_inc(ytr_done, 1)

                bT, cT = xcT[:, NX, :], xcT[:, NX + 1, :]
                pe.wait_ge(xc_made, g * NXBC + NXBC)
                for c in range(TT):
                    ch = slice(c * P, (c + 1) * P)
                    if c:
                        pe.wait_ge(st_made, g * (TT - 1) + c)
                    for m in range(NX):
                        mm = pe.transpose(ps_x[:, m * P:(m + 1) * P], xcT[:, m, ch], kept.ident[:])
                    mm.then_inc(xt_done, 1)
                    pe.matmul(ps_cb[:, 0:P], bT[:, ch], cT[:, ch], start=True, stop=True)
                    pe.transpose(ps_cb[:, P:2 * P], bT[:, ch], kept.ident[:]).then_inc(cb_done, 1)
                    if c:
                        y_turn(c - 1)
                    z_steps(c * STEPS, c * STEPS + FIRST_STEPS)
                    if c:
                        pe.wait_ge(yT_made, g * TT + c)
                        pe.matmul(ps_yo[:], cT[:, ch], state[:].rearrange("p h d -> p (h d)"),
                                  start=True, stop=True).then_inc(yo_done, 1)
                    pe.wait_ge(g_made, g * TT + c + 1)
                    for h in range(GH):
                        mm = pe.matmul(ps_yd[:, h * HEAD_DIM:(h + 1) * HEAD_DIM], seg[:, c % 2, h, :], x_dt[:, h, :],
                                       start=True, stop=True)
                    mm.then_inc(yd_done, 1)
                    pe.wait_ge(bt_made, g * TT + c + 1)
                    if c < TT - 1:
                        pe.wait_ge(xdec_made, g * (TT - 1) + c + 1)
                        pe.matmul(ps_x[:], b_tok[:], x_dec[:].rearrange("p h d -> p (h d)"),
                                  start=True, stop=True).then_inc(st_done, 1)
                    z_steps(c * STEPS + FIRST_STEPS, (c + 1) * STEPS)
                z_steps(TT * STEPS, TT * STEPS + FIRST_STEPS)
                y_turn(TT - 1)
                z_steps(TT * STEPS + FIRST_STEPS, TT * STEPS + KT)

                def branch(n, b, k):
                    i = NPROJ + n // 2
                    wh = w_hi[:, i % RAW].rearrange("p k n -> p (k n)").rearrange("p (k n) -> p k n", k=NX)
                    wl = w_lo[:, i % RAW].rearrange("p k n -> p (k n)").rearrange("p (k n) -> p k n", k=NX)
                    m, half = slice((n % 2) * P, (n % 2 + 1) * P), slice(b * HALF, (b + 1) * HALF)
                    mm = product(pe, pair[n % 2][b][:], wh[:, k, m], wl[:, k, m], yh[:, k, half], yl[:, k, half],
                                 k == 0, k == NX - 1)
                    if k == NX - 1:
                        mm.then_inc(br_done, 1)

                begin(NPROJ)
                pe.wait_ge(proj_read, g * (2 * NPROJ) + 2 * NPROJ)
                for k in range(NX):
                    pe.wait_ge(yl_made, g * NX + k + 1)
                    for n in range(2):
                        for b in range(2):
                            branch(n, b, k)
                for n in range(2, NBR):
                    if n % 2 == 0:
                        begin(NPROJ + n // 2)
                    pe.wait_ge(br_read, g * NBR + n - 1 + BR_CREDIT)
                    for b in range(2):
                        for k in range(NX):
                            branch(n, b, k)


def phase_pool(nc, kept, a, dram, hT_hi, hT_lo):
    start = kept.end + 2 * KT * T * 4
    sb = Arena(nc, "p3", start)
    ypT_hi = sb("ypT_hi", [P, KT, T], F32R)
    ypT_lo = sb("ypT_lo", [P, KT, T], F32R)
    RAW = 2
    raw = sb("raw", [P, RAW, KT, P])
    w_hi = sb("w_hi", [P, RAW, KT, P], F32R)
    w_lo = sb("w_lo", [P, RAW, KT, P], F32R)
    at = sb.at
    xpad, win0, win1 = (sb(n, [P, PAD + T]) for n in ("xpad", "win0", "win1"))
    sb.at = at
    t_a, t_b, acc_n = (sb(n, [P, T]) for n in ("t_a", "t_b", "acc_n"))
    sb.at = at + 3 * (PAD + T) * 4
    inv_count = sb("inv_count", [P, PAD])
    edge = sb("edge", [P, PAD])
    at = u_at = sb.at
    u = sb("u", [P, KT, T])
    NDT = 4
    d_hi = sb("d_hi", [P, NDT, T], F32R, at=at)
    d_lo = sb("d_lo", [P, NDT, T], F32R, at=at + NDT * T * 4)
    rstd = kept.sq_acc

    def result(m):
        return win0 if (WINDOWS[POOL_GROUPS - 1 - m // PW].bit_length() - 1) % 2 == 0 else win1

    PW = 2

    def tile(m):
        return (POOL_GROUPS - 1 - m // PW) * PW + m % PW

    order = []
    for m in range(KT):
        order.append(("x", m))
        if m % PW == PW - 1 and m >= 2 * PW - 1:
            order.append(("w", m // PW - 1))
    order.append(("w", POOL_GROUPS - 1))
    NS = len(order)
    assert NS % RAW == 0
    pair_of, n_pairs = {}, 0
    for kind, m in order:
        for o in range(1 if kind == "x" else PW):
            pair_of[(kind, m, o)] = n_pairs
            n_pairs += 1
    last_pair = [pair_of[(kind, m, 0 if kind == "x" else PW - 1)] for kind, m in order]

    with ExitStack() as ctx:
        sem = lambda n: nc.alloc_semaphore("p3_" + n)
        ps = lambda n: ctx.enter_context(nc.psum_tensor("p3_" + n, [P, HALF], F32))
        pair = [[ps("pair00"), ps("pair01")], [ps("pair10"), ps("pair11")]]
        pair.append([ps("pair20"), ps("pair21")])
        NPAIR = len(pair)
        gate_pair = [pair[(n_pairs + n) % NPAIR] for n in range(2)]
        ps_sq = [ps("sq0"), ps("sq1")]
        w_in = [sem(f"w_in{i}") for i in range(RAW)]
        acc_in = sem("acc_in")
        hi_made, lo_made = sem("hi_made"), sem("lo_made")
        pads, iota_made, sq_summed, var_made, std_made = (sem(n) for n in ("pads", "iota_made", "sq_summed", "var_made", "std_made"))
        done, x_read, d_made, dh_made, dl_made, yh_made, yl_made = (sem(n) for n in
            ("done", "x_read", "d_made", "dh_made", "dl_made", "yh_made", "yl_made"))
        gb_done, gate_read, br_read, tb_used, u_made, seq, seq2 = (sem(n) for n in
            ("gb_done", "gate_read", "br_read", "tb_used", "u_made", "seq", "seq2"))
        blk = ctx.enter_context(nc.Block())
        W_CREDIT = RAW
        PASSES, NQ = KT // 2, 2
        NI = 3 * NQ
        GATE_CREDIT, BR_CREDIT, TB_CREDIT, U_CREDIT = 1, 1, 1, 1
        SEQ2 = 2 * NQ

        @blk.sync
        def _(sp):
            for n, (kind, m) in enumerate(order):
                sp.wait_ge(lo_made, n + 1)
                if kind == "x":
                    src, dst = a["w_in"][0, :, tile(m) * P:(tile(m) + 1) * P].rearrange("(k p) n -> p k n", p=P), raw[:, n % RAW]
                else:
                    src = a["pool_w"][0, POOL_GROUPS - 1 - m].rearrange("(k p) n -> p k n", p=P)
                    dst = raw[:, n % RAW, 0:2 * PW].rearrange("p k n -> p (k n)").rearrange("p (k n) -> p k n", k=PW)
                sp.dma_start(dst, src).then_inc(w_in[n % RAW], 16)
            for p in range(PASSES):
                for i in range(NI):
                    q, r = divmod(i, 3)
                    sp.wait_ge(lo_made, p * NI + NS + i + 1)
                    first = q * P + (COL_GATE + r * D if r < 2 else 0)
                    src = a["w_in" if r < 2 else "w_branch_pool"][0, :, p * (NQ * P) + first:p * (NQ * P) + first + P]
                    sp.dma_start(raw[:, i % RAW], src.rearrange("(k p) n -> p k n", p=P)).then_inc(w_in[i % RAW], 16)

        @blk.gpsimd
        def _(pool):
            pool.sem_inc(lo_made, W_CREDIT)
            pool.sem_inc(gate_read, GATE_CREDIT)
            pool.sem_inc(br_read, BR_CREDIT)
            pool.sem_inc(tb_used, TB_CREDIT)
            pool.sem_inc(u_made, U_CREDIT)
            pool.memset(xpad[:, 0:PAD], 0.0).then_inc(pads, 1)
            pool.iota(inv_count[:], pattern=[[1, PAD]], base=1, channel_multiplier=0,
                      allow_small_or_imprecise_dtypes=True).then_inc(iota_made, 1)
            pool.wait_ge(yl_made, KT)
            with pool.Fori(0, PASSES) as p:
                for q in range(NQ):
                    pool.wait_ge(tb_used, p * NQ + q + TB_CREDIT)
                    pool.dma_start(acc_n[:], dram["acc"][:, bass.ds(p * NQ + q, 1), :]
                                   .rearrange("p k t -> p (k t)")).then_inc(acc_in, 16)

        @blk.scalar
        def _(act):
            def split_hi(slot, count):
                act.wait_ge(w_in[slot], 16 * count)
                act.activation(w_hi[:, slot], raw[:, slot], ACT.Copy).then_inc(hi_made, 1)

            def hi(n):
                if n >= RAW:
                    act.wait_ge(done, 2 * last_pair[n - RAW] + 2)
                split_hi(n % RAW, n // RAW + 1)

            hi(0)
            hi(1)
            act.wait_ge(var_made, 1)
            act.activation(rstd[:], rstd[:], ACT.Sqrt).then_inc(std_made, 1)
            for n, (kind, m) in enumerate(order):
                if kind == "x":
                    if m:
                        act.wait_ge(d_made, m)
                    k = pair_of[(kind, m, 0)]
                    for b in range(2):
                        act.wait_ge(done, 2 * k + b + 1)
                        act.activation(xpad[:, PAD + b * HALF:PAD + (b + 1) * HALF], pair[k % NPAIR][b][:],
                                       ACT.Copy).then_inc(x_read, 1)
                else:
                    for o in range(PW):
                        k, t = pair_of[(kind, m, o)], tile(m * PW + o)
                        for b in range(2):
                            act.wait_ge(done, 2 * k + b + 1)
                            act.activation(ypT_hi[:, t, b * HALF:(b + 1) * HALF], pair[k % NPAIR][b][:], ACT.Copy,
                                           scale=kept.cols_b[:, t:t + 1]).then_inc(yh_made, 1)
                hi(n + 2)
                if kind == "x":
                    act.wait_ge(d_made, m + 1)
                    act.activation(d_hi[:, m % NDT, :], result(m)[:, 0:T], ACT.Copy).then_inc(dh_made, 1)

            def gates(p, last):
                for i in range(NI):
                    q, r = divmod(i, 3)
                    if r < 2:
                        if r == 0:
                            act.wait_ge(u_made, p * NQ + q + U_CREDIT)
                        t = t_a if r == 0 else t_b
                        for b in range(2):
                            act.wait_ge(gb_done, p * (2 * NI) + 2 * i + b + 1)
                            ins = act.activation(t[:, b * HALF:(b + 1) * HALF], gate_pair[i % 2][b][:], ACT.Tanh, scale=0.5)
                        ins.then_inc(gate_read, 1)
                    if not last or i + RAW < NI:
                        act.wait_ge(gb_done, p * (2 * NI) + 2 * i + 2)
                        split_hi(i % RAW, p * (NI // RAW) + (NS + i) // RAW + 2)

            with act.Fori(0, PASSES - 1) as p:
                gates(p, False)
            gates(PASSES - 1, True)

        @blk.vector
        def _(dve):
            link = Chain(dve, seq)

            def lo(slot, count):
                dve.wait_ge(hi_made, count)
                dve.tensor_tensor(w_lo[:, slot], raw[:, slot], w_hi[:, slot].bitcast(F32),
                                  ALU.subtract).then_inc(lo_made, 1)

            lo(0, 1)
            lo(1, 2)
            dve.wait_ge(sq_summed, 1)
            for b in range(2):
                ins = dve.tensor_scalar(rstd[:, b * HALF:(b + 1) * HALF], ps_sq[b][:], 1.0 / INNER, EPS, ALU.mult, ALU.add)
            ins.then_inc(var_made, 1)
            dve.wait_ge(std_made, 1)
            link(dve.reciprocal(rstd[:], rstd[:]))
            dve.wait_ge(iota_made, 1)
            link(dve.reciprocal(inv_count[:], inv_count[:]))
            dve.wait_ge(pads, 1)
            for n, (kind, m) in enumerate(order):
                if kind == "x":
                    w = WINDOWS[POOL_GROUPS - 1 - m // PW]
                    dve.wait_ge(x_read, 2 * m + 2)
                    if m:
                        dve.wait_ge(dh_made, m)
                        dve.wait_ge(dl_made, m)
                    src, dst, span, free = xpad, win0, 1, win1
                    while span < w:
                        link(dve.tensor_tensor(dst[:, 2 * span - 1:], src[:, 2 * span - 1:],
                                               src[:, span - 1:PAD + T - span], ALU.add))
                        if span == 1:
                            lo(n % RAW, n + 3)
                        src, dst, free = dst, free, dst
                        span *= 2
                    x_, s_ = xpad[:, PAD:], src[:, PAD:]
                    link(dve.tensor_tensor(edge[:, 0:w], s_[:, 0:w], inv_count[:, 0:w], ALU.mult))
                    out = dst
                    assert out is result(m)
                    link(dve.scalar_tensor_tensor(out[:, 0:T], s_, 1.0 / w, x_, ALU.mult, ALU.subtract))
                    dve.tensor_tensor(out[:, 0:w], edge[:, 0:w], x_[:, 0:w], ALU.subtract).then_inc(d_made, 1)
                if kind == "x":
                    dve.wait_ge(dh_made, m + 1)
                    dve.wait_ge(d_made, m + 1)
                    dve.tensor_tensor(d_lo[:, m % NDT, :], result(m)[:, 0:T], d_hi[:, m % NDT, :].bitcast(F32),
                                      ALU.subtract).then_inc(dl_made, 1)
                else:
                    for o in range(PW):
                        k, t = pair_of[(kind, m, o)], tile(m * PW + o)
                        dve.wait_ge(yh_made, 2 * (m * PW + o) + 2)
                        for b in range(2):
                            half = slice(b * HALF, (b + 1) * HALF)
                            ins = dve.scalar_tensor_tensor(ypT_lo[:, t, half], pair[k % NPAIR][b][:], kept.cols_b[:, t:t + 1],
                                                           ypT_hi[:, t, half].bitcast(F32), ALU.mult, ALU.subtract)
                        ins.then_inc(yl_made, 1)
                    lo(n % RAW, n + 3)

            def gates(p, last):
                link = Chain(dve, seq2, p * SEQ2, SEQ2)
                for i in range(NI):
                    q, r = divmod(i, 3)
                    if r == 2:
                        for b in range(2):
                            half = slice(b * HALF, (b + 1) * HALF)
                            dve.wait_ge(gb_done, p * (2 * NI) + 2 * i + b + 1)
                            ins = dve.scalar_tensor_tensor(t_a[:, half], t_a[:, half], 1.0, gate_pair[i % 2][b][:], ALU.add, ALU.mult)
                        ins.then_inc(br_read, 1)
                    if not last or i + RAW < NI:
                        lo(i % RAW, p * NI + NS + i + 3)
                    if r == 1:
                        dve.wait_ge(acc_in, 16 * (p * NQ + q + 1))
                        dve.wait_ge(gate_read, p * (2 * NQ) + 2 * q + 2 + GATE_CREDIT)
                        link(dve.scalar_tensor_tensor(t_b[:], t_b[:], 1.0, acc_n[:], ALU.add, ALU.mult))
                        dve.sem_inc(tb_used, 1)
                        link(dve.tensor_tensor(t_b[:], t_b[:], rstd[:], ALU.mult))
                    if r == 2:
                        dve.wait_ge(br_read, p * NQ + q + 1 + BR_CREDIT)
                        column = p * NQ + q
                        dve.tensor_tensor(u[:, bass.ds(column, 1), :], t_a[:].unsqueeze(1), t_b[:].unsqueeze(1),
                                          ALU.add).then_inc(u_made, 1)
                link.done()

            with dve.Fori(0, PASSES - 1) as p:
                gates(p, False)
            gates(PASSES - 1, True)

        @blk.tensor
        def _(pe):
            for b in range(2):
                mm = pe.matmul(ps_sq[b][:], kept.ones[:], kept.sq_acc[:, b * HALF:(b + 1) * HALF], start=True, stop=True)
            mm.then_inc(sq_summed, 1)
            taken = []
            for n, (kind, m) in enumerate(order):
                pe.wait_ge(hi_made, n + 1)
                pe.wait_ge(lo_made, n + 1 + W_CREDIT)
                for o in range(1 if kind == "x" else PW):
                    k = pair_of[(kind, m, o)]
                    if k >= NPAIR:
                        was, wm, wo = taken[k - NPAIR]
                        if was == "x":
                            pe.wait_ge(x_read, 2 * wm + 2)
                        else:
                            pe.wait_ge(yl_made, wm * PW + wo + 1)
                    taken.append((kind, m, o))
                    for b in range(2):
                        half = slice(b * HALF, (b + 1) * HALF)
                        if kind == "x":
                            for kk in range(KT):
                                mm = product(pe, pair[k % NPAIR][b][:], w_hi[:, n % RAW, kk, :], w_lo[:, n % RAW, kk, :],
                                             hT_hi[:, kk, half], hT_lo[:, kk, half], kk == 0, kk == KT - 1)
                        else:
                            pe.wait_ge(dl_made, m * PW + PW)
                            wh = w_hi[:, n % RAW, 0:2 * PW].rearrange("p k n -> p (k n)").rearrange("p (k n) -> p k n", k=PW)
                            wl = w_lo[:, n % RAW, 0:2 * PW].rearrange("p k n -> p (k n)").rearrange("p (k n) -> p k n", k=PW)
                            for kk in range(PW):
                                t = (m * PW + kk) % NDT
                                mm = product(pe, pair[k % NPAIR][b][:], wh[:, kk, o * P:(o + 1) * P], wl[:, kk, o * P:(o + 1) * P],
                                             d_hi[:, t, half], d_lo[:, t, half], kk == 0, kk == PW - 1)
                        mm.then_inc(done, 1)
            pe.wait_ge(yl_made, KT - 1)
            with pe.Fori(0, PASSES) as p:
                for i in range(NI):
                    q, r = divmod(i, 3)
                    pe.wait_ge(hi_made, p * NI + NS + i + 1)
                    pe.wait_ge(lo_made, p * NI + NS + i + 1 + W_CREDIT)
                    if i == 0:
                        pe.wait_ge(gate_read, p * (2 * NQ) + GATE_CREDIT)
                    elif i == 1:
                        pe.wait_ge(br_read, p * NQ + BR_CREDIT)
                    elif (i - 2) % 3 == 2:
                        pe.wait_ge(br_read, p * NQ + (i - 2) // 3 + 1 + BR_CREDIT)
                    else:
                        pe.wait_ge(gate_read, p * (2 * NQ) + (i - 2) // 3 * 2 + (i - 2) % 3 + 1 + GATE_CREDIT)
                    if r == 2:
                        pe.wait_ge(yl_made, KT)
                    for b in range(2):
                        half = slice(b * HALF, (b + 1) * HALF)
                        rhs_hi, rhs_lo = (hT_hi, hT_lo) if r < 2 else (ypT_hi, ypT_lo)
                        for kk in range(KT):
                            mm = product(pe, gate_pair[i % 2][b][:], w_hi[:, i % RAW, kk, :], w_lo[:, i % RAW, kk, :],
                                         rhs_hi[:, kk, half], rhs_lo[:, kk, half], kk == 0, kk == KT - 1)
                        mm.then_inc(gb_done, 1)
    return u, u_at



def phase_mix(nc, kept, a, dram, u, u_at):
    fixed = kept.end
    sb = Arena(nc, "p4", fixed)
    u_hi = sb("u_hi", [P, KT, T], F32R)
    u_lo = sb("u_lo", [P, KT, T], F32R)
    w_hi = sb("w_hi", [P, KT, D], F32R)
    w_lo = sb("w_lo", [P, KT, D], F32R)
    raw = sb("raw", [P, 2, D])
    g1, gs2, sh2 = (sb(n, [P, D]) for n in ("g1", "gs2", "sh2"))
    x = sb("x", [P, D])
    h2 = sb("h2", [P, 2, D])
    h2T = sb("h2T", [P, KT, P])
    raw = [raw[:, 0], raw[:, 1], h2[:, 0], h2[:, 1]]
    RAW = len(raw)
    g_n = h2T[:].rearrange("p k t -> p (k t)")
    assert sb.at <= u_at
    x1 = sb("x1", [P, TT, D], at=u_at)
    sb.at = u_at + TT * D * 4
    NR = MG + NE
    rw = sb("rw", [P, KT, NR])
    rb = sb("rb", [P, NR])
    ss, var, std, rstd = (sb(n, [P, TT]) for n in ("ss", "var", "std", "rstd"))
    with ExitStack() as ctx:
        sem = lambda n: nc.alloc_semaphore("p4_" + n)
        ps = lambda n: ctx.enter_context(nc.psum_tensor("p4_" + n, [P, HALF], F32))
        pair = [[ps("pair00"), ps("pair01")], [ps("pair10"), ps("pair11")]]
        ps_t = [ps("t0"), ps("t1")]
        ps_r = ps("r")
        w_in = [sem(f"w_in{i}") for i in range(RAW)]
        par_in, x_in, hi_made, lo_made, uh_made, ul_made = (sem(n) for n in
            ("par_in", "x_in", "hi_made", "lo_made", "uh_made", "ul_made"))
        done, x1_made, squared, var_made, std_made, h2_made, turned, h2T_made, routed = (sem(n) for n in
            ("done", "x1_made", "squared", "var_made", "std_made", "h2_made", "turned", "h2T_made", "routed"))
        h2_out = [sem(f"h2_out{i}") for i in range(2)]
        seq = sem("seq")
        blk = ctx.enter_context(nc.Block())

        @blk.sync
        def _(sp):
            for k in range(KT):
                if k >= RAW:
                    sp.wait_ge(lo_made, k - RAW + 1)
                sp.dma_start(raw[k % RAW], a["w_out"][0, k * P:(k + 1) * P, :]).then_inc(w_in[k % RAW], 16)
            for i in range(TT):
                if i:
                    sp.wait_ge(x1_made, i)
                sp.dma_start(x[:], a["x"][0, i * P:(i + 1) * P, :]).then_inc(x_in, 16)

        @blk.gpsimd
        def _(pool):
            mod = dram["mod"]
            pool.wait_ge(hi_made, KT - 3)
            pool.dma_start(g1[:], mod[0, 0:D].partition_broadcast(P)).then_inc(par_in, 16)
            pool.dma_start(sh2[:], mod[0, D:2 * D].partition_broadcast(P)).then_inc(par_in, 16)
            pool.dma_start(gs2[:], mod[0, 2 * D:3 * D].partition_broadcast(P)).then_inc(par_in, 16)
            pool.dma_start(g_n, a["norm2_g"][0].partition_broadcast(P)).then_inc(par_in, 16)
            pool.dma_start(rw[:, :, 0:MG], a["router_group_w"][0].rearrange("(k p) n -> p k n", p=P)).then_inc(par_in, 16)
            pool.dma_start(rw[:, :, MG:], a["router_expert_w"][0].rearrange("(k p) n -> p k n", p=P)).then_inc(par_in, 16)
            pool.dma_start(rb[:, 0:MG], a["router_group_b"][0].partition_broadcast(P)).then_inc(par_in, 16)
            pool.dma_start(rb[:, MG:], a["router_expert_b"][0].partition_broadcast(P)).then_inc(par_in, 16)
            for i in range(TT):
                pool.wait_ge(h2_made, i + 1)
                pool.dma_start(dram["h2"][i * P:(i + 1) * P, :], h2[:, i % 2]).then_inc(h2_out[i % 2], 16)
            for i in range(2):
                pool.wait_ge(h2_out[i], 16 * TT // 2)

        @blk.scalar
        def _(act):
            for k in range(KT):
                act.activation(u_hi[:, k], u[:, k], ACT.Copy, scale=0.5).then_inc(uh_made, 1)
                act.wait_ge(w_in[k % RAW], 16 * (k // RAW + 1))
                act.activation(w_hi[:, k], raw[k % RAW], ACT.Copy).then_inc(hi_made, 1)
            for i in range(TT):
                act.wait_ge(x1_made, i + 1)
                act.activation(h2[:, i % 2], x1[:, i], ACT.Square, accum_out=ss[:, i:i + 1]).then_inc(squared, 1)
                act.wait_ge(var_made, i + 1)
                act.activation(std[:, i:i + 1], var[:, i:i + 1], ACT.Sqrt).then_inc(std_made, 1)
                if i >= 1:
                    for b in range(2):
                        act.wait_ge(turned, 2 * (i - 1) + b + 1)
                        if b == 0 and i >= 2:
                            act.wait_ge(routed, i - 1)
                        act.activation(h2T[:, 4 * b:4 * b + 4], ps_t[b][:].rearrange("p (k t) -> p k t", t=P),
                                       ACT.Copy).then_inc(h2T_made, 1)
            for b in range(2):
                act.wait_ge(turned, 2 * (TT - 1) + b + 1)
                if b == 0:
                    act.wait_ge(routed, TT - 1)
                act.activation(h2T[:, 4 * b:4 * b + 4], ps_t[b][:].rearrange("p (k t) -> p k t", t=P),
                               ACT.Copy).then_inc(h2T_made, 1)

        @blk.vector
        def _(dve):
            link = Chain(dve, seq)
            for k in range(KT):
                dve.wait_ge(uh_made, k + 1)
                dve.scalar_tensor_tensor(u_lo[:, k], u[:, k], 0.5, u_hi[:, k].bitcast(F32),
                                         ALU.mult, ALU.subtract).then_inc(ul_made, 1)
                dve.wait_ge(hi_made, k + 1)
                dve.tensor_tensor(w_lo[:, k], raw[k % RAW], w_hi[:, k].bitcast(F32), ALU.subtract).then_inc(lo_made, 1)
            dve.wait_ge(par_in, 16 * 8)
            link(dve.scalar_tensor_tensor(gs2[:], gs2[:], 1.0, g_n, ALU.add, ALU.mult))
            for i in range(TT):
                if i >= 2:
                    dve.wait_ge(h2_out[i % 2], 16 * (i // 2))
                    dve.wait_ge(turned, 2 * (i - 2) + 2)
                for b in range(2):
                    half = slice(b * HALF, (b + 1) * HALF)
                    dve.wait_ge(done, 2 * i + b + 1)
                    link(dve.tensor_tensor(h2[:, i % 2, half], pair[i % 2][b][:], g1[:, half], ALU.mult))
                dve.wait_ge(x_in, 16 * (i + 1))
                dve.tensor_tensor(x1[:, i], h2[:, i % 2], x[:], ALU.add).then_inc(x1_made, 1)
                dve.wait_ge(squared, i + 1)
                dve.tensor_scalar(var[:, i:i + 1], ss[:, i:i + 1], 1.0 / D, EPS, ALU.mult, ALU.add).then_inc(var_made, 1)
                dve.wait_ge(std_made, i + 1)
                link(dve.reciprocal(rstd[:, i:i + 1], std[:, i:i + 1]))
                link(dve.scalar_tensor_tensor(h2[:, i % 2], x1[:, i], rstd[:, i:i + 1], gs2[:], ALU.mult, ALU.mult))
                dve.tensor_tensor(h2[:, i % 2], h2[:, i % 2], sh2[:], ALU.add).then_inc(h2_made, 1)
            dve.wait_ge(routed, TT)
            dve.tensor_tensor(kept.logits[:], ps_r[:, 0:TT * NR].rearrange("p (t n) -> p t n", n=NR),
                              bc(rb[:].unsqueeze(1), [P, TT, NR]), ALU.add)

        @blk.tensor
        def _(pe):
            def turn(i):
                pe.wait_ge(h2_made, i + 1)
                if i:
                    pe.wait_ge(h2T_made, 2 * i)
                for k in range(KT):
                    mm = pe.transpose(ps_t[k // 4][:, (k % 4) * P:(k % 4 + 1) * P], h2[:, i % 2, k * P:(k + 1) * P],
                                      kept.ident[:])
                    if k % 4 == 3:
                        mm.then_inc(turned, 1)

            def route(i):
                pe.wait_ge(h2T_made, 2 * i + 2)
                if i == 0:
                    pe.wait_ge(par_in, 16 * 8)
                for k in range(KT):
                    mm = pe.matmul(ps_r[:, i * NR:(i + 1) * NR], h2T[:, k, :], rw[:, k, :],
                                   start=(k == 0), stop=(k == KT - 1))
                mm.then_inc(routed, 1)

            def out_step(i, b, k):
                rows, half = slice(i * P, (i + 1) * P), slice(b * HALF, (b + 1) * HALF)
                mm = product(pe, pair[i % 2][b][:], u_hi[:, k, rows], u_lo[:, k, rows],
                             w_hi[:, k, half], w_lo[:, k, half], k == 0, k == KT - 1)
                if k == KT - 1:
                    mm.then_inc(done, 1)

            for k in range(KT):
                pe.wait_ge(ul_made, k + 1)
                pe.wait_ge(lo_made, k + 1)
                for i in range(2):
                    for b in range(2):
                        out_step(i, b, k)
            for i in range(2, TT):
                pe.wait_ge(x1_made, i - 1)
                for b in range(2):
                    for k in range(KT):
                        out_step(i, b, k)
                turn(i - 2)
                if i >= 3:
                    route(i - 3)
            turn(TT - 2)
            route(TT - 3)
            route(TT - 2)
            turn(TT - 1)
            route(TT - 1)
    return x1


def routing(nc, kept, start, ps_pos, ps_cnt, ps_base, ps_tok):
    sb = Arena(nc, "p5", start)
    E3 = [P, TT, NE]
    G3 = [P, TT, MG]
    X3 = [P, TT, EPG]
    rev = sb("rev", [P, 1, EPG])
    gmax, gsum, gw = (sb(n, [P, TT, 1]) for n in ("gmax", "gsum", "gw"))
    glog, gexp, gone = (sb(n, G3) for n in ("glog", "gexp", "gone"))
    e_in, e_two, prod, one0, one1 = (sb(n, X3) for n in ("e_in", "e_two", "prod", "one0", "one1"))
    m0, m1, first, ratio = (sb(n, [P, TT, 1]) for n in ("m0", "m1", "first", "ratio"))
    hot = [sb(f"hot{k}", E3) for k in range(2)]
    both = sb("both", E3, BF16)
    where, slot_f = sb("where", E3), sb("slot_f", [P, TT])
    base = sb("base", [P, NE])
    count_f, count_i, blocks_f = sb("count_f", [NE, 1]), sb("count_i", [NE, 1], I32), sb("blocks_f", [NE, 1])
    blocks_bf = sb("blocks_bf", [NE, P], BF16)
    ends, block_no, past = sb("ends", [NE, 1]), sb("block_no", [P, MAX_BLOCKS + 1]), sb("past", [NE, MAX_BLOCKS + 1])
    row_no, choice_no = sb("row_no", [P, P]), sb("choice_no", [P, 2, TT])
    block_i, block_of, row_of = sb("block_i", [P, TT], I32), sb("block_of", [P, TT]), sb("row_of", [P, TT])
    NB = MAX_BLOCKS + 1
    at_row, at_block = sb("at_row", [P, 2 * TT, P]), sb("at_block", [P, 2 * TT, NB])
    choices, tokens = sb("choices", [P, NB], U32), sb("tokens", [P, NB], U32)
    choice_f, token_f = sb("choice_f", [P, NB]), sb("token_f", [P, NB])
    past_f, part_no = sb("past_f", [P, 2, NB]), sb("part_no", [P, 1])
    EMPTY = 2 * T
    logits = kept.logits
    sem = lambda n: nc.alloc_semaphore("p5_" + n)
    iotas, seq, top_made, gexp_made, ratio_in, ratio_made = (sem(n) for n in
        ("iotas", "seq", "top_made", "gexp_made", "ratio_in", "ratio_made"))
    both_made, counted, placed, blocks_made, based, past_made, tabled, spots_made, inverted = (sem(n) for n in
        ("both_made", "counted", "placed", "blocks_made", "based", "past_made", "tabled", "spots_made", "inverted"))
    tokens_made = sem("tokens_made")
    table_made = sem("table_made")

    def route_gpsimd(pool):
        pool.iota(rev[:], pattern=[[-1, EPG]], base=EPG, channel_multiplier=0,
                  allow_small_or_imprecise_dtypes=True).then_inc(iotas, 1)
        pool.iota(block_no[:], pattern=[[1, MAX_BLOCKS + 1]], base=0, channel_multiplier=0,
                  allow_small_or_imprecise_dtypes=True).then_inc(iotas, 1)
        pool.iota(row_no[:], pattern=[[1, P]], base=0, channel_multiplier=0,
                  allow_small_or_imprecise_dtypes=True).then_inc(iotas, 1)
        pool.iota(part_no[:], pattern=[[0, 1]], base=0, channel_multiplier=1,
                  allow_small_or_imprecise_dtypes=True).then_inc(iotas, 1)
        pool.iota(choice_no[:], pattern=[[T, 2], [P, TT]], base=-EMPTY, channel_multiplier=1,
                  allow_small_or_imprecise_dtypes=True).then_inc(iotas, 1)

    def route_scalar(act):
        act.wait_ge(top_made, 1)
        act.activation(gexp[:], glog[:], ACT.Exp).then_inc(gexp_made, 1)
        act.wait_ge(ratio_in, 1)
        act.activation(ratio[:], m1[:], ACT.Exp).then_inc(ratio_made, 1)

    def route_vector(dve):
        link = Chain(dve, seq)
        TE = [P, TT, EPG]

        def first_hot(out, values, top, n):
            link(dve.tensor_reduce(top[:], values, AX.X, ALU.max))
            link(dve.tensor_tensor(out, values, bc(top[:], [P, TT, n]), ALU.is_equal))
            link(dve.tensor_tensor(out, out, bc(rev[:, :, 0:n], [P, TT, n]), ALU.mult))
            link(dve.tensor_reduce(first[:], out, AX.X, ALU.max))
            link(dve.tensor_tensor(out, out, bc(first[:], [P, TT, n]), ALU.is_equal))

        dve.wait_ge(iotas, 5)
        lg = logits[:, :, 0:MG]
        first_hot(gone[:], lg, gmax, MG)
        dve.tensor_tensor(glog[:], lg, bc(gmax[:], G3), ALU.subtract).then_inc(top_made, 1)
        for g in range(MG):
            le = logits[:, :, MG + g * EPG:MG + (g + 1) * EPG]
            out = e_in if g == 0 else prod
            link(dve.tensor_tensor(out[:], le, bc(gone[:, :, g:g + 1], TE), ALU.mult))
            if g:
                link(dve.tensor_tensor(e_in[:], e_in[:], prod[:], ALU.add))
        first_hot(one0[:], e_in[:], m0, EPG)
        link(dve.scalar_tensor_tensor(e_two[:], one0[:], NEG, e_in[:], ALU.mult, ALU.add))
        first_hot(one1[:], e_two[:], m1, EPG)
        dve.tensor_tensor(m1[:], m1[:], m0[:], ALU.subtract).then_inc(ratio_in, 1)
        for k, one in enumerate((one0, one1)):
            for g in range(MG):
                ins = dve.tensor_tensor(hot[k][:, :, g * EPG:(g + 1) * EPG], one[:], bc(gone[:, :, g:g + 1], TE), ALU.mult)
        link(ins)
        dve.tensor_tensor(both[:], hot[0][:], hot[1][:], ALU.add).then_inc(both_made, 1)
        dve.wait_ge(gexp_made, 1)
        link(dve.tensor_reduce(gsum[:], gexp[:], AX.X, ALU.add))
        dve.wait_ge(ratio_made, 1)
        link(dve.scalar_tensor_tensor(gw[:], ratio[:], 1.0, gsum[:], ALU.add, ALU.mult))
        link(dve.reciprocal(kept.weight[0][:], gw[:].rearrange("p t o -> p (t o)")))
        link(dve.tensor_tensor(kept.weight[1][:], ratio[:].rearrange("p t o -> p (t o)"), kept.weight[0][:], ALU.mult))
        dve.wait_ge(counted, 1)
        link(dve.tensor_scalar(count_f[:], ps_cnt[0:NE, 0:1], float(BLOCK - 1), None, ALU.add))
        link(dve.tensor_copy(count_i[:], count_f[:]))
        link(dve.tensor_scalar(count_i[:], count_i[:], BLOCK.bit_length() - 1, None, ALU.arith_shift_right))
        link(dve.tensor_copy(blocks_f[:], count_i[:]))
        dve.tensor_copy(blocks_bf[:], bc(blocks_f[:], [NE, P])).then_inc(blocks_made, 1)
        dve.wait_ge(based, 1)
        link(dve.tensor_copy(base[:], ps_base[:, 0:NE]))
        link(dve.tensor_copy(ends[:], ps_base[0:NE, NE:NE + 1]))
        dve.tensor_scalar(past[:], block_no[0:NE], ends[:], None, ALU.is_ge).then_inc(past_made, 1)
        dve.wait_ge(placed, 1)
        link(dve.scalar_tensor_tensor(where[:], bc(base[:].unsqueeze(1), E3), float(BLOCK),
                                      ps_pos[:, 0:TT * NE].rearrange("p (t n) -> p t n", n=NE), ALU.mult, ALU.add))
        dve.wait_ge(tabled, 1)
        dve.tensor_scalar(kept.table[0:1, 0:MAX_BLOCKS + 1], ps_cnt[0:1, 64:64 + MAX_BLOCKS + 1], float(NE - 1), None,
                          ALU.min).then_inc(table_made, 1)
        dve.tensor_scalar(kept.table[0:1, MAX_BLOCKS + 1:MAX_BLOCKS + 2], ps_cnt[0:1, 192:193], -2.0, None,
                          ALU.add).then_inc(table_made, 1)
        dve.tensor_scalar(kept.table[0:1, MAX_BLOCKS + 2:MAX_BLOCKS + 3], ps_cnt[0:1, 192:193], -4.0, None,
                          ALU.add).then_inc(table_made, 1)
        for n in range(2):
            link(dve.tensor_tensor(hot[n][:], hot[n][:], where[:], ALU.mult))
            link(dve.tensor_reduce(slot_f[:], hot[n][:], AX.X, ALU.add))
            link(dve.tensor_copy(block_i[:], slot_f[:]))
            link(dve.tensor_scalar(block_i[:], block_i[:], BLOCK.bit_length() - 1, None, ALU.arith_shift_right))
            link(dve.tensor_copy(block_of[:], block_i[:]))
            link(dve.scalar_tensor_tensor(row_of[:], block_of[:], -float(BLOCK), slot_f[:], ALU.mult, ALU.add))
            for i in range(TT):
                dve.tensor_scalar(at_row[:, n * TT + i], row_no[:], row_of[:, i:i + 1], None, ALU.is_equal)
                ins = dve.tensor_scalar(at_block[:, n * TT + i], block_no[:], block_of[:, i:i + 1], choice_no[:, n, i:i + 1],
                                        ALU.is_equal, ALU.mult)
            ins.then_inc(spots_made, 1)
            dve.wait_ge(spots_made, n + 1)
        dve.wait_ge(inverted, 1)
        link(dve.tensor_scalar(choice_f[:], ps_tok[:, 0:NB], float(EMPTY), None, ALU.add))
        link(dve.tensor_scalar(token_f[:], choice_f[:], float(T), -float(T), ALU.is_ge, ALU.mult))
        link(dve.tensor_scalar(past_f[:, 0], choice_f[:], float(EMPTY), -float(T), ALU.is_ge, ALU.mult))
        link(dve.tensor_scalar(past_f[:, 1], choice_f[:], float(EMPTY), part_no[:, 0:1], ALU.is_ge, ALU.mult))
        link(dve.tensor_tensor(token_f[:], token_f[:], choice_f[:], ALU.add))
        link(dve.tensor_tensor(token_f[:], token_f[:], past_f[:, 0], ALU.add))
        link(dve.tensor_tensor(choice_f[:], choice_f[:], past_f[:, 1], ALU.add))
        dve.tensor_copy(choices[:], choice_f[:]).then_inc(tokens_made, 1)
        dve.tensor_copy(tokens[:], token_f[:]).then_inc(tokens_made, 1)

    def route_tensor(pe):
        pe.wait_ge(both_made, 1)
        for i in range(TT):
            mm = pe.matmul(ps_cnt[0:NE, 0:1], both[:, i, :], kept.ones_bf[:, 0:1], start=(i == 0), stop=(i == TT - 1))
        mm.then_inc(counted, 1)
        for i in range(TT):
            out = ps_pos[:, i * NE:(i + 1) * NE]
            for j in range(i):
                pe.matmul(out, kept.ones_bf[:], both[:, j, :], start=(j == 0), stop=False)
            mm = pe.matmul(out, kept.tri_strict[:], both[:, i, :], start=(i == 0), stop=True)
        mm.then_inc(placed, 1)
        pe.wait_ge(blocks_made, 1)
        pe.matmul(ps_base[:, 0:NE], blocks_bf[:], kept.tri_strict[0:NE, 0:NE], start=True, stop=True)
        pe.matmul(ps_base[0:NE, NE:NE + 1], kept.tri[0:NE, 0:NE], blocks_f[:], start=True, stop=True).then_inc(based, 1)
        pe.wait_ge(past_made, 1)
        pe.matmul(ps_cnt[0:1, 64:64 + MAX_BLOCKS + 1], kept.ones[0:NE, 0:1], past[:], start=True, stop=True)
        pe.matmul(ps_cnt[0:1, 192:193], blocks_f[:], kept.ones[0:NE, 0:1], start=True, stop=True).then_inc(tabled, 1)
        for n in range(2 * TT):
            if n % TT == 0:
                pe.wait_ge(spots_made, n // TT + 1)
            mm = pe.matmul(ps_tok[:, 0:NB], at_row[:, n, :], at_block[:, n, :], start=(n == 0), stop=(n == 2 * TT - 1))
        mm.then_inc(inverted, 1)

    return route_gpsimd, route_scalar, route_vector, route_tensor, table_made, choices, tokens, tokens_made


def phase_experts(nc, kept, a, dram):
    sb = Arena(nc, "p6", kept.end)
    FT = FF // P
    NP = KT + FT
    NS = 6
    MIN_BLOCKS = 2 * T // BLOCK
    raw = sb("raw", [P, NP, D])
    w_hi = sb("w_hi", [P, NS, D], F32R)
    w_lo = sb("w_lo", [P, NS, D], F32R)
    xb = sb("xb", [P, D])
    xT_hi = sb("xT_hi", [P, KT, P], F32R)
    xT_lo = sb("xT_lo", [P, KT, P], F32R)
    th = sb("th", [P, FF])
    s = sb("s", [P, FF])
    sT_hi = sb("sT_hi", [P, FT, P], F32R)
    sT_lo = sb("sT_lo", [P, FT, P], F32R)
    yb = sb("yb", [P, D])
    g2 = sb("g2", [P, D])
    x_row, y_row = sb("x_row", [P, 1], U32), sb("y_row", [P, 1], U32)
    with ExitStack() as ctx:
        sem = lambda n: nc.alloc_semaphore("p6_" + n)
        ps = lambda n: ctx.enter_context(nc.psum_tensor("p6_" + n, [P, HALF], F32))
        ps_a, ps_g, ps_s = ps("a"), ps("g"), ps("s")
        ps_x = [ps("x0"), ps("x1")]
        ps_y = [ps("y0"), ps("y1")]
        w_in = [sem(f"w_in{i}") for i in range(NP)]
        x_in, y_out, g2_in = sem("x_in"), sem("y_out"), sem("g2_in")
        x_row_made, x_row_seen, y_row_seen = (sem(n) for n in ("x_row_made", "x_row_seen", "y_row_seen"))
        hi_made, lo_made, used, x_turned, xh_made, xl_made, th_made, t_made, s_made = (sem(n) for n in
            ("hi_made", "lo_made", "used", "x_turned", "xh_made", "xl_made", "th_made", "t_made", "s_made"))
        s_turned, sh_made, sl_made, y_read, y_scaled, y_stored = (sem(n) for n in
            ("s_turned", "sh_made", "sl_made", "y_read", "y_scaled", "y_stored"))
        Y_CREDIT = 2
        route_gpsimd, route_scalar, route_vector, route_tensor, table_made, choices, tokens, tokens_made = \
            routing(nc, kept, sb.at, ps_y[0], ps_y[1], ps_s, ps_g)
        blk = ctx.enter_context(nc.Block())

        def passes(eng):
            eng.wait_ge(table_made, 3)
            return eng.value_load(kept.table[0:1, MAX_BLOCKS + 1:MAX_BLOCKS + 2], min_val=MIN_BLOCKS - 2,
                                  max_val=MAX_BLOCKS - 2)

        def raw_slot(i):
            return (KT + i) % NP

        def split_slot(i):
            return (KT + i) % NS

        def after(j, i):
            return j * NP + (KT + i + 1)

        @blk.sync
        def _(sp):
            n = passes(sp)

            def expert(j):
                return sp.value_load(kept.table[0:1, bass.ds(j, 1)], min_val=0, max_val=NE - 1)

            def load_w13(e, i, k):
                sp.dma_start(raw[:, raw_slot(i)], a["w13"][0, bass.ds(e, 1), k * P:(k + 1) * P, :]
                             .rearrange("e p n -> p (e n)")).then_inc(w_in[raw_slot(i)], 16)

            def load_w2(e, i, k):
                sp.dma_start(raw[:, raw_slot(i)], a["w2"][0, bass.ds(e, 1), k * P:(k + 1) * P, :]
                             .rearrange("e p n -> p (e n)")).then_inc(w_in[raw_slot(i)], 16)

            def slot_free(j, i):
                sp.wait_ge(lo_made, after(j, i - NP))

            def pieces(load, e, last, j, first, count, k0):
                with sp.If_ne(e.val, last.val):
                    for i in range(first, first + count):
                        slot_free(j, i)
                        load(e, i, k0 + i - first)
                with sp.Else():
                    for i in range(first, first + count):
                        slot_free(j, i)
                        sp.sem_inc(w_in[raw_slot(i)], 16)

            e = expert(0)
            for k in range(KT):
                if k == NS:
                    sp.wait_ge(x_row_seen, 1)
                load_w13(e, k - KT, k)
            e = expert(1)
            for k in range(FT):
                load_w13(e, k, k)
            e0 = expert(0)
            for i in range(FT, KT):
                slot_free(0, i)
                load_w13(e, i, i)
            for i in range(KT, NP):
                slot_free(0, i)
                load_w2(e0, i, i - KT)
            pieces(load_w13, expert(2), e, 1, 0, FT, 0)
            with sp.Fori(1, n) as j:
                e, e1, e2, last = expert(j), expert(j + 1), expert(j + 2), expert(j - 1)
                pieces(load_w13, e1, e, j, FT, KT - FT, FT)
                pieces(load_w2, e, last, j, KT, FT, 0)
                pieces(load_w13, e2, e1, j + 1, 0, FT, 0)
            e, e1, last = expert(n), expert(n + 1), expert(n - 1)
            pieces(load_w13, e1, e, n, FT, KT - FT, FT)
            pieces(load_w2, e, last, n, KT, FT, 0)
            for i in range(FT):
                slot_free(n + 1, i)
                load_w2(e1, i, i)

        @blk.gpsimd
        def _(pool):
            pool.dma_start(g2[:], dram["mod"][0, 3 * D:4 * D].partition_broadcast(P)).then_inc(g2_in, 16)
            pool.sem_inc(y_stored, 1)
            route_gpsimd(pool)
            pool.wait_ge(table_made, 3)
            pool.wait_ge(tokens_made, 2)
            m = pool.value_load(kept.table[0:1, MAX_BLOCKS + 2:MAX_BLOCKS + 3], min_val=MIN_BLOCKS - 4,
                                max_val=MAX_BLOCKS - 4)

            def gather_x(j):
                pool.tensor_copy(x_row[:], tokens[:, bass.ds(j, 1)]).then_inc(x_row_made, 1)
                pool.wait_ge(x_row_made, j + 1)
                pool.sem_inc(x_row_seen, 1)
                pool.indirect_dma_start(out=xb[:], out_offset=None, in_=dram["h2"],
                                        in_offset=bass.IndirectOffsetOnAxis(ap=x_row[:, 0:1], axis=0)).then_inc(x_in, 16)

            def start_y(j):
                pool.wait_ge(y_read, 2 * j + 2 + Y_CREDIT)
                pool.tensor_tensor(yb[:], yb[:], g2[:], ALU.mult).then_inc(y_scaled, 1)
                pool.tensor_copy(y_row[:], choices[:, bass.ds(j, 1)]).then_inc(y_scaled, 1)
                pool.wait_ge(y_scaled, 2 * j + 2)
                pool.sem_inc(y_row_seen, 1)
                pool.indirect_dma_start(out=dram["y"], in_=yb[:], in_offset=None,
                                        out_offset=bass.IndirectOffsetOnAxis(ap=y_row[:, 0:1], axis=0)).then_inc(y_out, 16)

            def finish_y(j):
                pool.wait_ge(y_out, j * 16 + 16)
                pool.sem_inc(y_stored, 1)

            pool.wait_ge(g2_in, 16)

            gather_x(0)
            for j in range(1, 4):
                pool.wait_ge(x_turned, 2 * j)
                gather_x(j)
            start_y(0)
            with pool.Fori(0, m) as j:
                pool.wait_ge(x_turned, 2 * j + 8)
                gather_x(j + 4)
                finish_y(j)
                start_y(j + 1)
            for j in range(3):
                finish_y(m + j)
                start_y(m + (j + 1))
            finish_y(m + 3)

        @blk.scalar
        def _(act):
            route_scalar(act)
            n = passes(act)

            def hi(j, i):
                slot = raw_slot(i)
                act.wait_ge(w_in[slot], (j + (KT + i) // NP) * 16 + 16)
                if not (isinstance(j, int) and after(j, i) <= NS):
                    act.wait_ge(used, after(j, i - NS))
                act.activation(w_hi[:, split_slot(i)], raw[:, slot], ACT.Copy).then_inc(hi_made, 1)

            def x_hi(j):
                for b in range(2):
                    act.wait_ge(x_turned, 2 * j + (b + 1))
                    act.activation(xT_hi[:, 4 * b:4 * b + 4], ps_x[b][:].rearrange("p (k t) -> p k t", t=P),
                                   ACT.Copy).then_inc(xh_made, 1)

            def gate(j, p, last):
                act.wait_ge(used, after(p, last))
                act.activation(th[:], ps_a[:], ACT.Tanh, scale=0.5).then_inc(th_made, 1)

            def s_hi(j):
                act.wait_ge(s_turned, j + 1)
                act.activation(sT_hi[:], ps_s[:].rearrange("p (k t) -> p k t", t=P), ACT.Copy).then_inc(sh_made, 1)

            def y_copy(j, p, last):
                act.wait_ge(used, after(p, last))
                act.wait_ge(y_stored, j + 1)
                for b in range(2):
                    act.activation(yb[:, b * HALF:(b + 1) * HALF], ps_y[b][:], ACT.Copy).then_inc(y_read, 1)

            act.sem_inc(y_read, Y_CREDIT)
            for i in range(-KT, NS - KT):
                hi(0, i)
            x_hi(0)
            for i in range(NS - KT, NS - FT):
                hi(0, i)
            gate(0, 0, -1)
            x_hi(1)
            for i in range(NS - FT, NS):
                hi(0, i)
            with act.Fori(0, n) as j:
                s_hi(j)
                for i in range(NS, KT + NS):
                    hi(j, i)
                gate(j + 1, j, KT - 1)
                x_hi(j + 2)
                for i in range(KT + NS, NP + NS):
                    hi(j, i)
                y_copy(j, j, NP - 1)
            s_hi(n)
            for i in range(NS, KT + NS):
                hi(n, i)
            gate(n + 1, n, KT - 1)
            for i in range(KT + NS, NP + FT):
                hi(n, i)
            y_copy(n, n, NP - 1)
            s_hi(n + 1)
            y_copy(n + 1, n + 1, FT - 1)

        @blk.vector
        def _(dve):
            route_vector(dve)
            n = passes(dve)

            def lo(j, i):
                dve.wait_ge(hi_made, after(j, i))
                dve.tensor_tensor(w_lo[:, split_slot(i)], raw[:, raw_slot(i)], w_hi[:, split_slot(i)].bitcast(F32),
                                  ALU.subtract).then_inc(lo_made, 1)

            def x_lo(j):
                for b in range(2):
                    dve.wait_ge(xh_made, 2 * j + (b + 1))
                    ks = slice(4 * b, 4 * b + 4)
                    dve.tensor_tensor(xT_lo[:, ks], ps_x[b][:].rearrange("p (k t) -> p k t", t=P),
                                      xT_hi[:, ks].bitcast(F32), ALU.subtract).then_inc(xl_made, 1)

            def gate(j):
                dve.wait_ge(th_made, j + 1)
                dve.scalar_tensor_tensor(th[:], th[:], 1.0, ps_a[:], ALU.add, ALU.mult).then_inc(t_made, 1)
                dve.wait_ge(t_made, j + 1)
                dve.scalar_tensor_tensor(s[:], th[:], 0.5, ps_g[:], ALU.mult, ALU.mult).then_inc(s_made, 1)

            def s_lo(j):
                dve.wait_ge(sh_made, j + 1)
                dve.tensor_tensor(sT_lo[:], ps_s[:].rearrange("p (k t) -> p k t", t=P), sT_hi[:].bitcast(F32),
                                  ALU.subtract).then_inc(sl_made, 1)

            for i in range(-KT, NS - KT):
                lo(0, i)
            x_lo(0)
            for i in range(NS - KT, NS - FT):
                lo(0, i)
            gate(0)
            x_lo(1)
            for i in range(NS - FT, NS):
                lo(0, i)
            with dve.Fori(0, n) as j:
                s_lo(j)
                for i in range(NS, KT + NS):
                    lo(j, i)
                gate(j + 1)
                x_lo(j + 2)
                for i in range(KT + NS, NP + NS):
                    lo(j, i)
            s_lo(n)
            for i in range(NS, KT + NS):
                lo(n, i)
            gate(n + 1)
            for i in range(KT + NS, NP + FT):
                lo(n, i)
            s_lo(n + 1)

        @blk.tensor
        def _(pe):
            route_tensor(pe)
            n = passes(pe)

            def turn_x(j):
                pe.wait_ge(x_in, j * 16 + 16)
                for k in range(KT):
                    mm = pe.transpose(ps_x[k // 4][:, (k % 4) * P:(k % 4 + 1) * P], xb[:, k * P:(k + 1) * P], kept.ident[:])
                    if k % 4 == 3:
                        mm.then_inc(x_turned, 1)

            def turn_s(j):
                pe.wait_ge(s_made, j + 1)
                for k in range(FT):
                    mm = pe.transpose(ps_s[:, k * P:(k + 1) * P], s[:, k * P:(k + 1) * P], kept.ident[:])
                mm.then_inc(s_turned, 1)

            def up(j, p, first):
                for k in range(KT):
                    if k % 4 == 0:
                        pe.wait_ge(xl_made, j * 2 + (k // 4 + 1))
                    pe.wait_ge(lo_made, after(p, first + k))
                    for b, out in enumerate((ps_a, ps_g)):
                        half = slice(b * HALF, (b + 1) * HALF)
                        slot = split_slot(first + k)
                        mm = product(pe, out[:], xT_hi[:, k], xT_lo[:, k], w_hi[:, slot, half], w_lo[:, slot, half],
                                     k == 0, k == KT - 1)
                    mm.then_inc(used, 1)

            def down(j, first, p):
                pe.wait_ge(sl_made, j + 1)
                pe.wait_ge(y_read, 2 * j + Y_CREDIT)
                for k in range(FT):
                    pe.wait_ge(lo_made, after(p, first + k))
                    slot = split_slot(first + k)
                    for b in range(2):
                        half = slice(b * HALF, (b + 1) * HALF)
                        mm = product(pe, ps_y[b][:], sT_hi[:, k], sT_lo[:, k], w_hi[:, slot, half], w_lo[:, slot, half],
                                     k == 0, k == FT - 1)
                    mm.then_inc(used, 1)

            turn_x(0)
            up(0, 0, -KT)
            turn_x(1)
            with pe.Fori(0, n) as j:
                turn_s(j)
                up(j + 1, j, 0)
                turn_x(j + 2)
                down(j, KT, j)
            turn_s(n)
            up(n + 1, n, 0)
            down(n, KT, n)
            turn_s(n + 1)
            down(n + 1, 0, n + 1)

def phase_combine(nc, kept, a, dram, x1, out):
    sb = Arena(nc, "p7", kept.end)
    R = 3
    y0, y1 = sb("y0", [P, R, D]), sb("y1", [P, R, D])
    sq = sb("sq", [P, 2, D])
    gf = sb("gf", [P, D])
    res = sb("res", [P, 2, D])
    ss, var, std, rstd = (sb(n, [P, TT]) for n in ("ss", "var", "std", "rstd"))
    with ExitStack() as ctx:
        sem = lambda n: nc.alloc_semaphore("p7_" + n)
        y_in = [[sem(f"y_in{k}{i}") for i in range(R)] for k in range(2)]
        res_out = [sem(f"res_out{i}") for i in range(2)]
        gf_in, seq, used0, used1, x2_made, squared, var_made, std_made, res_made = (sem(n) for n in
            ("gf_in", "seq", "used0", "used1", "x2_made", "squared", "var_made", "std_made", "res_made"))
        blk = ctx.enter_context(nc.Block())

        @blk.sync
        def _(sp):
            for i in range(TT):
                if i >= R:
                    sp.wait_ge(x2_made, i - R + 1)
                for k, y in enumerate((y0, y1)):
                    sp.dma_start(y[:, i % R], dram["y"][k * T + i * P:k * T + (i + 1) * P, :]).then_inc(y_in[k][i % R], 16)

        @blk.gpsimd
        def _(pool):
            pool.dma_start(gf[:], a["final_norm_g"].partition_broadcast(P)).then_inc(gf_in, 16)
            for i in range(TT):
                pool.wait_ge(res_made, i + 1)
                pool.dma_start(out[0, i * P:(i + 1) * P, :], res[:, i % 2]).then_inc(res_out[i % 2], 16)
            for i in range(2):
                pool.wait_ge(res_out[i], 16 * TT // 2)

        @blk.scalar
        def _(act):
            for i in range(TT):
                act.wait_ge(x2_made, i + 1)
                if i >= 2:
                    act.wait_ge(squared, i - 1)
                act.activation(sq[:, i % 2], x1[:, i], ACT.Square, accum_out=ss[:, i:i + 1]).then_inc(squared, 1)
                act.wait_ge(var_made, i + 1)
                act.activation(std[:, i:i + 1], var[:, i:i + 1], ACT.Sqrt).then_inc(std_made, 1)

        @blk.vector
        def _(dve):
            link = Chain(dve, seq)

            def norm(i):
                dve.wait_ge(squared, i + 1)
                dve.tensor_scalar(var[:, i:i + 1], ss[:, i:i + 1], 1.0 / D, EPS, ALU.mult, ALU.add).then_inc(var_made, 1)
                dve.wait_ge(std_made, i + 1)
                link(dve.reciprocal(rstd[:, i:i + 1], std[:, i:i + 1]))
                if i >= 2:
                    dve.wait_ge(res_out[i % 2], 16 * (i // 2))
                dve.scalar_tensor_tensor(res[:, i % 2], x1[:, i], rstd[:, i:i + 1], gf[:], ALU.mult, ALU.mult).then_inc(res_made, 1)

            dve.wait_ge(gf_in, 16)
            for i in range(TT):
                dve.wait_ge(y_in[0][i % R], 16 * (i // R + 1))
                link(dve.scalar_tensor_tensor(x1[:, i], y0[:, i % R], kept.weight[0][:, i:i + 1], x1[:, i], ALU.mult, ALU.add))
                dve.wait_ge(y_in[1][i % R], 16 * (i // R + 1))
                dve.scalar_tensor_tensor(x1[:, i], y1[:, i % R], kept.weight[1][:, i:i + 1], x1[:, i],
                                         ALU.mult, ALU.add).then_inc(x2_made, 1)
                if i:
                    norm(i - 1)
            norm(TT - 1)


def build(nc, a, out):
    dram = {
        "mod": nc.dram_tensor("mod_rows", (1, 4 * D), F32).ap(),
        "acs": nc.dram_tensor("acs_rows", (HEADS, T), F32).ap(),
        "small": nc.dram_tensor("small_by_group", (P, GROUPS, 5 * TT, GH), F32).ap(),
        "acc": nc.dram_tensor("acc_ssd", (P, KT, T), F32).ap(),
        "h2": nc.dram_tensor("h2_rows", (T, D), F32).ap(),
        "y": nc.dram_tensor("y_rows", (2 * T + P, D), F32).ap(),
    }
    kept = Kept(nc)
    with nc.cleanup_on_exit():
        hT_hi, hT_lo = phase_start(nc, kept, a, dram)
        phase_ssd(nc, kept, a, dram, hT_hi, hT_lo)
    u, u_at = phase_pool(nc, kept, a, dram, hT_hi, hT_lo)
    x1 = phase_mix(nc, kept, a, dram, u, u_at)
    phase_experts(nc, kept, a, dram)
    phase_combine(nc, kept, a, dram, x1, out)


NAMES = ["x", "c", "ada_w", "ada_b", "norm1_g", "w_in", "pool_w", "pool_scale", "conv_w", "conv_b", "dt_bias", "a_log",
         "d_skip", "ssd_norm_g", "w_branch_pool", "w_branch_ssd", "w_out", "norm2_g", "router_group_w",
         "router_group_b", "router_expert_w", "router_expert_b", "w13", "w2", "final_norm_g"]


def kernel(**inputs):
    import concourse.bacc as bacc
    from concourse.bass_utils import run_bass_kernel_spmd

    nc = bacc.Bacc("TRN2", target_bir_lowering=False, num_devices=1)
    arrays, aps = {}, {}
    for name in NAMES:
        value = np.ascontiguousarray(inputs[name])
        arrays[f"in_{name}"] = value
        aps[name] = nc.dram_tensor(f"in_{name}", value.shape, mybir.dt.from_np(value.dtype), kind="ExternalInput").ap()
    out = nc.dram_tensor("out_0", (1, T, D), F32, kind="ExternalOutput").ap()
    build(nc, aps, out)
    return run_bass_kernel_spmd(nc, [arrays], core_ids=[0]).results[0]["out_0"]
```
